# Optimizing a Trainium2 kernel written in Bass

```python
import jax, jax.numpy as jnp
from jax import lax
import numpy as np

D_MODEL = 2048
BATCH = 1
SEQ = 512
DEPTH = 2
DEC_BATCH = 1
DEC_SEQ = 64
PAST_LEN = 512

CHUNK = 64
Q_BLOCK = 128
N_A_LAYERS = DEPTH // 2
N_B_LAYERS = DEPTH - N_A_LAYERS

FOX_HEADS = 16
FOX_HEAD_DIM = D_MODEL // FOX_HEADS
FOX_WIDTH = FOX_HEADS * FOX_HEAD_DIM
FOX_IN = 4 * FOX_WIDTH + FOX_HEADS
FOX_FORGET_BIAS = 3.0

MLA_HEADS = 16
Q_LORA_RANK = 512
KV_LORA_RANK = 512
QK_NOPE_DIM = 128
QK_ROPE_DIM = 64
V_HEAD_DIM = 128
MLA_WIDTH = MLA_HEADS * V_HEAD_DIM
MLA_IN = Q_LORA_RANK + MLA_WIDTH
MLA_SCALE = (QK_NOPE_DIM + QK_ROPE_DIM) ** -0.5
FOX_SCALE = FOX_HEAD_DIM ** -0.5

ROPE_THETA = 10000.0
NORM_EPS = 1e-6
NEG_INF = -1e30

kernel_name = 'yoco_fox_mla_streaming_encoder'

def _rms_norm(x, g):
    xf = x.astype(jnp.float32)
    y = xf * lax.rsqrt(jnp.mean(xf * xf, axis=-1, keepdims=True) + NORM_EPS)
    return (y * g.astype(jnp.float32)).astype(x.dtype)

def _rope(x, pos):
    half = x.shape[-1] // 2
    inv = ROPE_THETA ** (-jnp.arange(half, dtype=jnp.float32) / half)
    ang = pos.astype(jnp.float32)[:, None] * inv[None, :]
    ang = ang.reshape((ang.shape[0],) + (1,) * (x.ndim - 3) + (half,))
    cos, sin = jnp.cos(ang), jnp.sin(ang)
    xf = x.astype(jnp.float32)
    x1, x2 = xf[..., :half], xf[..., half:]
    return jnp.concatenate([x1 * cos - x2 * sin, x2 * cos + x1 * sin], axis=-1).astype(x.dtype)

def _to_blocks(a, nb):
    return jnp.moveaxis(a.reshape((a.shape[0], nb, a.shape[1] // nb) + a.shape[2:]), 1, 0)

def _from_blocks(a):
    a = jnp.moveaxis(a, 0, 1)
    return a.reshape((a.shape[0], a.shape[1] * a.shape[2]) + a.shape[3:])

def _sweep_queries(block_fn, q_arrays, qpos, kv_arrays):
    T = qpos.shape[0]
    if T <= Q_BLOCK:
        return block_fn(*q_arrays, qpos, *kv_arrays)
    nb = T // Q_BLOCK
    blocked = tuple(_to_blocks(a, nb) for a in q_arrays)
    out = lax.map(lambda blk: block_fn(*blk[:-1], blk[-1], *kv_arrays),
                  blocked + (qpos.reshape(nb, Q_BLOCK),))
    return _from_blocks(out)

def _fox_block(q, fq, qpos, k, v, fk, kpos):
    logits = jnp.einsum('bqhd,bkhd->bhqk', q, k, preferred_element_type=jnp.float32) * FOX_SCALE
    decay = jnp.swapaxes(fq, 1, 2)[..., :, None] - jnp.swapaxes(fk, 1, 2)[..., None, :]
    mask = kpos[None, :] <= qpos[:, None]
    p = jax.nn.softmax(jnp.where(mask, logits + decay, NEG_INF), axis=-1)
    return jnp.einsum('bhqk,bkhd->bqhd', p.astype(v.dtype), v)

def _mla_block(qn, qr, qpos, kn, kr, v, kpos):
    logits = (jnp.einsum('bqhd,bkhd->bhqk', qn, kn, preferred_element_type=jnp.float32)
              + jnp.einsum('bqhr,bkr->bhqk', qr, kr, preferred_element_type=jnp.float32)) * MLA_SCALE
    mask = (kpos // CHUNK)[None, :] <= (qpos // CHUNK)[:, None]
    p = jax.nn.softmax(jnp.where(mask, logits, NEG_INF), axis=-1)
    return jnp.einsum('bhqk,bkhd->bqhd', p.astype(v.dtype), v)

def _fox_layer(x, past, g_norm, w_in, b_f, g_q, g_k, w_out):
    B, T, _ = x.shape
    h = _rms_norm(x, g_norm)
    proj = h @ w_in
    q, k, v, gate, f_logit = jnp.split(proj, [FOX_WIDTH, 2 * FOX_WIDTH, 3 * FOX_WIDTH, 4 * FOX_WIDTH], axis=-1)
    q = _rms_norm(q.reshape(B, T, FOX_HEADS, FOX_HEAD_DIM), g_q)
    k = _rms_norm(k.reshape(B, T, FOX_HEADS, FOX_HEAD_DIM), g_k)
    v = v.reshape(B, T, FOX_HEADS, FOX_HEAD_DIM)
    logf = jax.nn.log_sigmoid(f_logit.astype(jnp.float32) + b_f.astype(jnp.float32))
    if past is None:
        k_all, v_all, logf_all = k, v, logf
    else:
        pk, pv, plf = past
        k_all = jnp.concatenate([pk.astype(k.dtype), k], axis=1)
        v_all = jnp.concatenate([pv.astype(v.dtype), v], axis=1)
        logf_all = jnp.concatenate([plf.astype(jnp.float32), logf], axis=1)
    F = jnp.cumsum(logf_all, axis=1)
    P = k_all.shape[1] - T
    kpos = jnp.arange(P + T)
    qpos = P + jnp.arange(T)
    o = _sweep_queries(_fox_block, (q, F[:, P:]), qpos, (k_all, v_all, F, kpos))
    o = o.reshape(B, T, FOX_WIDTH) * jax.nn.silu(gate)
    return x + o @ w_out, (k, v, logf.astype(x.dtype))

def _shared_latent(x, pos, g_kv_in, w_dkv, g_ckv, g_krope):
    h = _rms_norm(x, g_kv_in)
    ck = h @ w_dkv
    c = _rms_norm(ck[..., :KV_LORA_RANK], g_ckv)
    kr = _rope(_rms_norm(ck[..., KV_LORA_RANK:], g_krope), pos)
    return c, kr

def _expand_latent(c, w_ukv, g_knope):
    kv = jnp.einsum('bsc,chd->bshd', c, w_ukv)
    kn = _rms_norm(kv[..., :QK_NOPE_DIM], g_knope)
    return kn, kv[..., QK_NOPE_DIM:]

def _mla_layer(x, qpos, kn, kr, v, kpos, g_norm, w_in, g_qa, w_uq, g_qn, g_qr, w_out):
    B, T, _ = x.shape
    h = _rms_norm(x, g_norm)
    proj = h @ w_in
    q_lat, gate = proj[..., :Q_LORA_RANK], proj[..., Q_LORA_RANK:]
    q = jnp.einsum('btc,chd->bthd', _rms_norm(q_lat, g_qa), w_uq)
    qn = _rms_norm(q[..., :QK_NOPE_DIM], g_qn)
    qr = _rope(_rms_norm(q[..., QK_NOPE_DIM:], g_qr), qpos)
    o = _sweep_queries(_mla_block, (qn, qr), qpos, (kn, kr, v, kpos))
    o = o.reshape(B, T, MLA_WIDTH) * jax.nn.silu(gate)
    return x + o @ w_out

def _trunk(x, past_fox, past_mla, fox_norm_g, fox_w_in, fox_b_f, fox_q_norm_g, fox_k_norm_g, fox_w_out,
           kv_norm_g, mla_w_dkv, mla_ckv_norm_g, mla_krope_norm_g, mla_w_ukv, mla_knope_norm_g,
           mla_norm_g, mla_w_in, mla_qa_norm_g, mla_w_uq, mla_qnope_norm_g, mla_qrope_norm_g, mla_w_out):
    T = x.shape[1]
    past_len = 0 if past_mla is None else past_mla[0].shape[1]
    pos = past_len + jnp.arange(T)
    fox_rows = []
    for layer in range(DEPTH):
        if layer < N_A_LAYERS:
            past = None if past_fox is None else (past_fox[0][layer], past_fox[1][layer], past_fox[2][layer])
            x, rows = _fox_layer(x, past, fox_norm_g[layer], fox_w_in[layer], fox_b_f[layer],
                                 fox_q_norm_g[layer], fox_k_norm_g[layer], fox_w_out[layer])
            fox_rows.append(rows)
        else:
            j = layer - N_A_LAYERS
            if j == 0:
                c_new, kr_new = _shared_latent(x, pos, kv_norm_g, mla_w_dkv, mla_ckv_norm_g, mla_krope_norm_g)
                if past_mla is None:
                    c_all, kr_all = c_new, kr_new
                else:
                    c_all = jnp.concatenate([past_mla[0].astype(c_new.dtype), c_new], axis=1)
                    kr_all = jnp.concatenate([past_mla[1].astype(kr_new.dtype), kr_new], axis=1)
                kn, v = _expand_latent(c_all, mla_w_ukv, mla_knope_norm_g)
                kpos = jnp.arange(c_all.shape[1])
            x = _mla_layer(x, pos, kn, kr_all, v, kpos, mla_norm_g[j], mla_w_in[j], mla_qa_norm_g[j],
                           mla_w_uq[j], mla_qnope_norm_g[j], mla_qrope_norm_g[j], mla_w_out[j])
    fox_k = jnp.stack([r[0] for r in fox_rows])
    fox_v = jnp.stack([r[1] for r in fox_rows])
    fox_logf = jnp.stack([r[2] for r in fox_rows])
    return x, fox_k, fox_v, fox_logf, c_new, kr_new

def setup_inputs(seed: int = 0) -> dict:
    key = jax.random.key(seed)
    ks = jax.random.split(key, 26)

    def nrm(k, shape, scale=1.0):
        return scale * jax.random.normal(k, shape, jnp.float32)

    def gain(k, shape):
        return 1.0 + 0.02 * nrm(k, shape)

    A, B = N_A_LAYERS, N_B_LAYERS
    return {
        'x_prompt': nrm(ks[0], (BATCH, SEQ, D_MODEL)),
        'x_sample': nrm(ks[1], (DEC_BATCH, DEC_SEQ, D_MODEL)),
        'cache_fox_k': nrm(ks[2], (A, DEC_BATCH, PAST_LEN, FOX_HEADS, FOX_HEAD_DIM)),
        'cache_fox_v': nrm(ks[3], (A, DEC_BATCH, PAST_LEN, FOX_HEADS, FOX_HEAD_DIM)),
        'cache_fox_logf': jax.nn.log_sigmoid(FOX_FORGET_BIAS + nrm(ks[4], (A, DEC_BATCH, PAST_LEN, FOX_HEADS))),
        'cache_mla_ckv': nrm(ks[5], (DEC_BATCH, PAST_LEN, KV_LORA_RANK)),
        'cache_mla_krope': nrm(ks[6], (DEC_BATCH, PAST_LEN, QK_ROPE_DIM)),
        'fox_norm_g': gain(ks[7], (A, D_MODEL)),
        'fox_w_in': nrm(ks[8], (A, D_MODEL, FOX_IN), D_MODEL ** -0.5),
        'fox_b_f': FOX_FORGET_BIAS + 0.5 * nrm(ks[9], (A, FOX_HEADS)),
        'fox_q_norm_g': gain(ks[10], (A, FOX_HEAD_DIM)),
        'fox_k_norm_g': gain(ks[11], (A, FOX_HEAD_DIM)),
        'fox_w_out': nrm(ks[12], (A, FOX_WIDTH, D_MODEL), FOX_WIDTH ** -0.5),
        'kv_norm_g': gain(ks[13], (D_MODEL,)),
        'mla_w_dkv': nrm(ks[14], (D_MODEL, KV_LORA_RANK + QK_ROPE_DIM), D_MODEL ** -0.5),
        'mla_ckv_norm_g': gain(ks[15], (KV_LORA_RANK,)),
        'mla_krope_norm_g': gain(ks[16], (QK_ROPE_DIM,)),
        'mla_w_ukv': nrm(ks[17], (KV_LORA_RANK, MLA_HEADS, QK_NOPE_DIM + V_HEAD_DIM), KV_LORA_RANK ** -0.5),
        'mla_knope_norm_g': gain(ks[18], (QK_NOPE_DIM,)),
        'mla_norm_g': gain(ks[19], (B, D_MODEL)),
        'mla_w_in': nrm(ks[20], (B, D_MODEL, MLA_IN), D_MODEL ** -0.5),
        'mla_qa_norm_g': gain(ks[21], (B, Q_LORA_RANK)),
        'mla_w_uq': nrm(ks[22], (B, Q_LORA_RANK, MLA_HEADS, QK_NOPE_DIM + QK_ROPE_DIM), Q_LORA_RANK ** -0.5),
        'mla_qnope_norm_g': gain(ks[23], (B, QK_NOPE_DIM)),
        'mla_qrope_norm_g': gain(ks[24], (B, QK_ROPE_DIM)),
        'mla_w_out': nrm(ks[25], (B, MLA_WIDTH, D_MODEL), MLA_WIDTH ** -0.5),
    }

def reference(x_prompt, x_sample, cache_fox_k, cache_fox_v, cache_fox_logf, cache_mla_ckv, cache_mla_krope,
              fox_norm_g, fox_w_in, fox_b_f, fox_q_norm_g, fox_k_norm_g, fox_w_out,
              kv_norm_g, mla_w_dkv, mla_ckv_norm_g, mla_krope_norm_g, mla_w_ukv, mla_knope_norm_g,
              mla_norm_g, mla_w_in, mla_qa_norm_g, mla_w_uq, mla_qnope_norm_g, mla_qrope_norm_g, mla_w_out):
    y_prompt, fk_p, fv_p, fl_p, ckv_p, kr_p = _trunk(
        x_prompt, None, None,
        fox_norm_g, fox_w_in, fox_b_f, fox_q_norm_g, fox_k_norm_g, fox_w_out,
        kv_norm_g, mla_w_dkv, mla_ckv_norm_g, mla_krope_norm_g, mla_w_ukv, mla_knope_norm_g,
        mla_norm_g, mla_w_in, mla_qa_norm_g, mla_w_uq, mla_qnope_norm_g, mla_qrope_norm_g, mla_w_out)
    y_sample, fk_s, fv_s, fl_s, ckv_s, kr_s = _trunk(
        x_sample, (cache_fox_k, cache_fox_v, cache_fox_logf), (cache_mla_ckv, cache_mla_krope),
        fox_norm_g, fox_w_in, fox_b_f, fox_q_norm_g, fox_k_norm_g, fox_w_out,
        kv_norm_g, mla_w_dkv, mla_ckv_norm_g, mla_krope_norm_g, mla_w_ukv, mla_knope_norm_g,
        mla_norm_g, mla_w_in, mla_qa_norm_g, mla_w_uq, mla_qnope_norm_g, mla_qrope_norm_g, mla_w_out)
    return (y_prompt, y_sample, fk_p, fv_p, fl_p, ckv_p, kr_p, fk_s, fv_s, fl_s, ckv_s, kr_s)


_drawn_inputs = setup_inputs


def setup_inputs(seed=0):
    import zlib

    import numpy as np

    out = dict(_drawn_inputs(seed))
    spreads = {}
    factors = {'cache_fox_logf': 4.756,
     'cache_mla_krope': 2.821,
     'fox_norm_g': 2.824,
     'fox_q_norm_g': 8.0,
     'kv_norm_g': 2.723,
     'mla_ckv_norm_g': 2.846,
     'mla_knope_norm_g': 8.0,
     'mla_norm_g': 8.0,
     'mla_qa_norm_g': 8.0,
     'mla_qnope_norm_g': 8.0,
     'mla_qrope_norm_g': 8.0}
    for name, (base, spread) in spreads.items():
        noise = np.random.default_rng([zlib.crc32(name.encode()), seed]).standard_normal(out[name].shape)
        drawn = base * np.exp(spread * noise) if base else spread * noise
        out[name] = __import__('jax').numpy.asarray(drawn.astype(out[name].dtype))
    for name, factor in factors.items():
        out[name] = (out[name] * factor).astype(out[name].dtype)
    return out
```

```python
from contextlib import ExitStack

import numpy as np

import concourse.bass as bass
from concourse import mybir

F32 = mybir.dt.float32
F32R = mybir.dt.float32r
BF16 = mybir.dt.bfloat16
ALU = mybir.AluOpType
ACT = mybir.ActivationFunctionType
AX = mybir.AxisListType

P = 128
D_MODEL, SEQ, NEW, PAST = 2048, 512, 64, 512
HEADS, HD = 16, 128
LAT, ROPE = 512, 64
CHUNK = 64
EPS = 1e-6
FOX_SCALE = float(HD) ** -0.5
MLA_SCALE = float(HD + ROPE) ** -0.5
THETA = 10000.0
MASKED = -1e30

NT = SEQ // P
TT = NT + 1
SM = NT
KT = D_MODEL // P
LT = LAT // P
UK = 2
RAW_FOX = 2
TIME = SEQ + PAST + NEW
SAMP = PAST + NEW
BR = HD + ROPE


class Sig:

    def __init__(self, sem, per=1, unit=1, credit=0):
        self.sem, self.per, self.unit, self.credit = sem, per, unit, credit

    def grant(self, eng):
        eng.sem_inc(self.sem, self.credit * self.unit)

    def wait(self, eng, step, k):
        v = (step * self.per + k + self.credit) * self.unit
        if not isinstance(v, int) or v > 0:
            eng.wait_ge(self.sem, v)


def rows(t):
    return P if t < SM else NEW


def turn(eng, out, x, ident, first):
    if first:
        return eng.matmul(out, x, ident, start=True, stop=True)
    return eng.transpose(out, x, ident)


def steps(eng, n, body):
    body(0, n == 1)
    if n > 2:
        with eng.Fori(1, n - 1) as i:
            body(i, False)
    if n > 1:
        body(n - 1, True)


class Core:

    def __init__(self, nc, ctx, dram):
        self.nc, self.ctx, self.dram = nc, ctx, dram
        self.base = (nc.sbuf_base + 63) // 64 * 64
        self.limit = nc.sbuf_usable_end
        self.X = self.base
        self.Y = self.X + 73728
        self.W = self.Y + 40960
        self.bank = [ctx.enter_context(nc.psum_tensor(f"bank{b}", [P, 512], F32)) for b in range(8)]
        self.used = []

    def at(self, name, shape, dt, offset):
        size = int(np.prod(shape[1:])) * (2 if dt == BF16 else 4)
        assert offset + size <= self.limit, (name, offset + size, self.limit)
        return self.nc.alloc_sbuf_tensor_at(name, list(shape), dt, offset=offset)

    def packer(self, offset):
        cur = [offset]

        def place(name, shape, dt=F32):
            t = self.at(name, shape, dt, cur[0])
            cur[0] += (int(np.prod(shape[1:])) * (2 if dt == BF16 else 4) + 63) // 64 * 64
            return t
        place.cur = cur
        return place

    def sem(self, name, per=1, unit=1, credit=0):
        handle = self.nc.alloc_semaphore(name)
        self.used.append(handle)
        return Sig(handle, per, unit, credit)

    def recycle(self):
        nums = sorted(h.num for h in self.used)
        starts = [n for n in nums if n - 1 not in nums]
        ends = [n + 1 for n in nums if n + 1 not in nums]
        with self.nc.Block() as block:
            @block.gpsimd
            def _(pool):
                for a, b in zip(starts, ends):
                    pool.sem_clear(range(a, b))
        for h in self.used:
            self.nc.release_semaphore(h)
        self.used = []


class Gemm:

    def __init__(self, c, tag, src, steps_, units, kk, n, raw, act, gain, place, slots=2):
        self.slots = slots
        self.c, self.src, self.steps, self.units, self.kk, self.n, self.raws = c, src, steps_, units, kk, n, raw
        self.hi, self.lo, self.smp = act
        self.gain = gain
        assert units % raw == 0 or raw >= units * steps_
        self.raw = [place(f"{tag}_raw{i}", [P, kk, n]) for i in range(raw)]
        self.whi = [place(f"{tag}_whi{i}", [P, kk, n], F32R) for i in range(slots)]
        self.wlo = [place(f"{tag}_wlo{i}", [P, kk, n], F32R) for i in range(slots)]
        self.arrived = [c.sem(f"{tag}_arrived{i}", units // raw, 16) for i in range(raw)]
        self.w_hi = c.sem(f"{tag}_w_hi", units)
        self.w_lo = c.sem(f"{tag}_w_lo", units)
        self.used = c.sem(f"{tag}_used", units)
        self.done = c.sem(f"{tag}_done", NT)

    def load(self, eng, h, u):
        self.w_lo.wait(eng, h, u - self.raws + 1)
        eng.dma_start(self.raw[u % self.raws][:], self.src[h, u]).then_inc(self.arrived[u % self.raws].sem, 16)

    def make_hi(self, eng, h, u):
        self.arrived[u % self.raws].wait(eng, h, u // self.raws + 1)
        self.used.wait(eng, h, u - self.slots + 1)
        raw, hi = self.raw[u % self.raws], self.whi[u % self.slots]
        if self.gain is None:
            op = eng.activation(hi[:], raw[:], ACT.Copy)
        else:
            for k in range(self.kk):
                K = u * self.kk + k
                op = eng.activation(hi[:, k, :], raw[:, k, :], ACT.Copy, scale=self.gain[:, K:K + 1])
        op.then_inc(self.w_hi.sem, 1)

    def make_lo(self, eng, h, u):
        self.w_hi.wait(eng, h, u + 1)
        raw, hi, lo = self.raw[u % self.raws], self.whi[u % self.slots], self.wlo[u % self.slots]
        hi32 = hi[:].bitcast(F32)
        if self.gain is None:
            op = eng.tensor_tensor(lo[:], raw[:], hi32, ALU.subtract)
        else:
            for k in range(self.kk):
                K = u * self.kk + k
                op = eng.scalar_tensor_tensor(lo[:, k, :], raw[:, k, :], self.gain[:, K:K + 1], hi32[:, k, :],
                                              ALU.mult, ALU.subtract)
        op.then_inc(self.w_lo.sem, 1)

    def multiply(self, eng, h, u, t):
        out = self.c.bank[t][:, 0:self.n]
        whi, wlo = self.whi[u % self.slots], self.wlo[u % self.slots]
        first, last = u == 0, u == self.units - 1
        for k in range(self.kk):
            K = u * self.kk + k
            if t < SM:
                a_hi, a_lo = self.hi[:, K, t * P:(t + 1) * P], self.lo[:, K, t * P:(t + 1) * P]
                pairs = [(a_hi, whi), (a_hi, wlo), (a_lo, whi)]
            else:
                pairs = [(self.smp[:, K, :], whi), (self.smp[:, K, :], wlo)]
            for i, (a, w) in enumerate(pairs):
                op = eng.matmul(out, a, w[:, k, :], start=(first and k == 0 and i == 0),
                                stop=(last and k == self.kk - 1 and i == len(pairs) - 1))
        if t == SM:
            op.then_inc(self.used.sem, 1)
        elif last:
            op.then_inc(self.done.sem, 1)


def three(hi_a, lo_a, hi_b, lo_b):
    return [(hi_a, hi_b), (hi_a, lo_b), (lo_a, hi_b)]


class Transposer:

    def __init__(self, c, tag, src, act, ident, kt, banks=(0, 1, 2, 3), smp_banks=(4, 5)):
        self.banks, self.smp_banks = banks, smp_banks
        self.c, self.src, self.ident, self.kt = c, src, ident, kt
        self.hi, self.lo, self.smp = act
        self.turned = c.sem(f"{tag}_turned")
        self.hi_out = c.sem(f"{tag}_hi_out")
        self.lo_out = c.sem(f"{tag}_lo_out")

    def jobs(self):
        out, last = [], {}
        for k in range(self.kt):
            out.append((self.banks[k % len(self.banks)], [k], False))
            if k % 4 == 3:
                out.append((self.smp_banks[(k // 4) % len(self.smp_banks)], list(range(k - 3, k + 1)), True))
        full = []
        for i, (b, ks, s) in enumerate(out):
            full.append((i, b, ks, s, last.get(b)))
            last[b] = i
        return full

    def views(self, b, ks, s):
        if not s:
            k = ks[0]
            return self.c.bank[b][:, :], self.hi[:, k, :], self.lo[:, k, :]
        src = self.c.bank[b][:, 0:4 * NEW].rearrange("p (k t) -> p k t", k=4)
        return src, self.smp[:, ks[0]:ks[0] + 4, 0:NEW], self.smp[:, ks[0]:ks[0] + 4, NEW:2 * NEW]

    def pe(self, eng):
        for i, b, ks, s, prev in self.jobs():
            if prev is not None:
                eng.wait_ge(self.lo_out.sem, prev + 1)
            for j, k in enumerate(ks):
                if s:
                    op = eng.transpose(self.c.bank[b][:, j * NEW:(j + 1) * NEW],
                                       self.src[0:NEW, SM, k * P:(k + 1) * P], self.ident[0:NEW, 0:NEW])
                else:
                    for t in range(NT):
                        op = eng.transpose(self.c.bank[b][:, t * P:(t + 1) * P],
                                           self.src[:, t, k * P:(k + 1) * P], self.ident[:, :])
            op.then_inc(self.turned.sem, 1)

    def act(self, eng):
        for i, b, ks, s, _ in self.jobs():
            src, hi, lo = self.views(b, ks, s)
            eng.wait_ge(self.turned.sem, i + 1)
            eng.activation(hi, src, ACT.Copy).then_inc(self.hi_out.sem, 1)

    def dve(self, eng):
        for i, b, ks, s, _ in self.jobs():
            src, hi, lo = self.views(b, ks, s)
            eng.wait_ge(self.hi_out.sem, i + 1)
            eng.tensor_tensor(lo, src, hi.bitcast(F32), ALU.subtract).then_inc(self.lo_out.sem, 1)


def block_a(c, K):
    nc, d = c.nc, c.dram
    place = c.packer(c.W)
    x = c.at("a_x", [P, TT, D_MODEL], F32, c.Y)
    act = K.act
    junk = place("a_junk", [P, D_MODEL])
    ss, rstd, half = place("a_ss", [P, TT]), place("a_rstd", [P, TT]), place("a_half", [P, TT])
    wf = place("a_wf", [P, KT, HEADS])
    wfs = place("a_wfs", [P, KT, 48], F32R)
    fb = place("a_fb", [HEADS, SEQ])
    fbs = place("a_fbs", [HEADS, 3, NEW])
    z = place("a_z", [HEADS, SEQ + NEW])
    e = place("a_e", [HEADS, SEQ + NEW])
    lf = place("a_lf", [HEADS, TIME])
    lft = place("a_lft", [P, TT, HEADS])
    one = place("a_one", [HEADS, TIME])
    F = place("a_F", [HEADS, TIME])
    T = Transposer(c, "a", x, act, K.ident, KT)
    consts = c.sem("a_consts", unit=16)
    x_in = [c.sem(f"a_x_in{t}", unit=16) for t in range(TT)]
    sq, r0, r1, zero, xh = c.sem("a_sq"), c.sem("a_r0"), c.sem("a_r1"), c.sem("a_zero"), c.sem("a_xh")
    wf_hi, wf_lo, f_mm, f_mv, f_sum = c.sem("a_wf_hi"), c.sem("a_wf_lo"), c.sem("a_f_mm"), c.sem("a_f_mv"), c.sem("a_f_sum")
    soft, logs, scan, f_hi, f_lo, f_t, f_tc, out = (c.sem(f"a_{n}") for n in
        ("soft", "logs", "scan", "f_hi", "f_lo", "f_t", "f_tc", "out"))
    with nc.Block() as block:
        @block.sync
        def _(sp):
            sp.dma_start(K.ident[:], d["ident"]).then_inc(consts.sem, 16)
            for t in range(TT):
                sp.dma_start(x[0:rows(t), t, :], d["x"][0:rows(t), t, :]).then_inc(x_in[t].sem, 16)
            for dst, name in K.loads:
                sp.dma_start(dst[:], d[name]).then_inc(consts.sem, 16)
            sp.dma_start(wf[:], d["w_f"]).then_inc(consts.sem, 16)
            sp.dma_start(lf[:, SEQ:SEQ + PAST], d["cache_logf"]).then_inc(consts.sem, 16)
            sp.wait_ge(f_tc.sem, 1)
            sp.dma_start(d["out_logf"][:, 0:NT, :], lft[:, 0:NT, :]).then_inc(out.sem, 16)
            sp.dma_start(d["out_logf"][0:NEW, SM, :], lft[0:NEW, SM, :]).then_inc(out.sem, 16)
            sp.wait_ge(out.sem, 32)

        n_const = 1 + len(K.loads) + 2

        @block.gpsimd
        def _(pool):
            pool.memset(ss[:], 1.0).then_inc(zero.sem, 1)
            pool.memset(half[:], -0.5).then_inc(zero.sem, 1)
            pool.memset(wfs[:].bitcast(F32), 0.0).then_inc(zero.sem, 1)
            pool.memset(one[:], 1.0).then_inc(zero.sem, 1)
            pool.memset(K.A[:].bitcast(F32), 0.0).then_inc(zero.sem, 1)
            pool.memset(K.B[:].bitcast(F32), 0.0).then_inc(zero.sem, 1)
            pool.wait_ge(sq.sem, TT)
            pool.wait_ge(zero.sem, 2)
            pool.tensor_scalar(ss[:], ss[:], 1.0 / D_MODEL, EPS, ALU.mult, ALU.add).then_inc(r0.sem, 1)
            pool.wait_ge(r0.sem, 1)
            pool.tensor_tensor(rstd[:], ss[:], half[:], ALU.pow).then_inc(r1.sem, 1)

        @block.scalar
        def _(act_):
            act_.wait_ge(zero.sem, 1)
            for t in range(TT):
                act_.wait_ge(x_in[t].sem, 16)
                if t:
                    act_.wait_ge(sq.sem, t)
                act_.activation(junk[0:rows(t), :], x[0:rows(t), t, :], ACT.Square,
                                accum_out=ss[0:rows(t), t:t + 1]).then_inc(sq.sem, 1)
            act_.wait_ge(consts.sem, 16 * n_const)
            act_.wait_ge(zero.sem, 3)
            act_.activation(K.ident_b[:], K.ident[:], ACT.Copy).then_inc(soft.sem, 1)
            act_.activation(K.mask_fox_b[:], K.mask_fox[:], ACT.Copy).then_inc(soft.sem, 1)
            act_.activation(K.mask_mla_b[:], K.mask_mla[:], ACT.Copy).then_inc(soft.sem, 1)
            for k in range(KT):
                op = act_.activation(wfs[:, k, 0:HEADS], wf[:, k, :], ACT.Copy, scale=K.g_fox[:, k:k + 1])
            op.then_inc(wf_hi.sem, 1)
            T.act(act_)
            act_.wait_ge(f_mm.sem, 1)
            act_.activation(fb[:], c.bank[6][32:32 + HEADS, :], ACT.Copy).then_inc(f_mv.sem, 1)
            act_.wait_ge(f_mm.sem, 2)
            act_.activation(fbs[:, 0, :], c.bank[7][0:HEADS, NEW:2 * NEW], ACT.Copy).then_inc(f_mv.sem, 1)
            act_.activation(fbs[:, 1, :], c.bank[7][32:32 + HEADS, 0:NEW], ACT.Copy).then_inc(f_mv.sem, 1)
            act_.activation(fbs[:, 2, :], c.bank[7][32:32 + HEADS, NEW:2 * NEW], ACT.Copy).then_inc(f_mv.sem, 1)
            act_.wait_ge(f_sum.sem, 6)
            act_.activation(e[:], e[:], ACT.Exp).then_inc(soft.sem, 1)
            act_.wait_ge(soft.sem, 4)
            act_.activation(e[:], e[:], ACT.Ln, bias=K.one_col[0:HEADS, :]).then_inc(soft.sem, 1)
            act_.wait_ge(scan.sem, 2)
            act_.wait_ge(zero.sem, 6)
            act_.activation(K.B[0:HEADS, :], F[:], ACT.Copy).then_inc(f_hi.sem, 1)
            act_.activation(K.A[64:64 + HEADS, 0:SEQ], F[:, 0:SEQ], ACT.Copy).then_inc(f_hi.sem, 1)
            act_.activation(K.A[64:64 + HEADS, SEQ:SEQ + NEW], F[:, SEQ + PAST:TIME], ACT.Copy).then_inc(f_hi.sem, 1)

        @block.vector
        def _(dve):
            dve.memset(K.one_col[:], 1.0).then_inc(wf_lo.sem, 1)
            dve.wait_ge(r1.sem, 1)
            for t in range(TT):
                dve.tensor_scalar(x[0:rows(t), t, :], x[0:rows(t), t, :], rstd[0:rows(t), t:t + 1], None,
                                  ALU.mult).then_inc(xh.sem, 1)
            dve.wait_ge(wf_hi.sem, 1)
            for k in range(KT):
                op = dve.scalar_tensor_tensor(wfs[:, k, 32:48], wf[:, k, :], K.g_fox[:, k:k + 1],
                                              wfs[:, k, 0:HEADS].bitcast(F32), ALU.mult, ALU.subtract)
            op.then_inc(wf_lo.sem, 1)
            T.dve(dve)
            dve.wait_ge(f_mv.sem, 4)
            dve.tensor_tensor(z[:, 0:SEQ], c.bank[6][0:HEADS, :], fb[:], ALU.add).then_inc(f_sum.sem, 1)
            dve.tensor_tensor(z[:, SEQ:], c.bank[7][0:HEADS, 0:NEW], fbs[:, 0, :], ALU.add).then_inc(f_sum.sem, 1)
            dve.wait_ge(f_sum.sem, 2)
            dve.tensor_tensor(z[:, SEQ:], z[:, SEQ:], fbs[:, 1, :], ALU.add).then_inc(f_sum.sem, 1)
            dve.wait_ge(f_sum.sem, 3)
            dve.tensor_tensor(z[:, SEQ:], z[:, SEQ:], fbs[:, 2, :], ALU.add).then_inc(f_sum.sem, 1)
            dve.wait_ge(f_sum.sem, 4)
            dve.tensor_scalar(z[:], z[:], K.b_f[:, 0:1], None, ALU.add).then_inc(f_sum.sem, 1)
            dve.wait_ge(f_sum.sem, 5)
            dve.scalar_tensor_tensor(e[:], z[:], -1.0, z[:], ALU.mult, ALU.min).then_inc(f_sum.sem, 1)
            dve.wait_ge(soft.sem, 5)
            dve.scalar_tensor_tensor(lf[:, 0:SEQ], z[:, 0:SEQ], 0.0, e[:, 0:SEQ], ALU.min, ALU.subtract).then_inc(logs.sem, 1)
            dve.scalar_tensor_tensor(lf[:, SEQ + PAST:], z[:, SEQ:], 0.0, e[:, SEQ:], ALU.min, ALU.subtract).then_inc(logs.sem, 1)
            dve.wait_ge(logs.sem, 2)
            dve.wait_ge(zero.sem, 4)
            dve.tensor_tensor_scan(F[:, 0:SEQ], one[:, 0:SEQ], lf[:, 0:SEQ], 0.0, ALU.mult, ALU.add).then_inc(scan.sem, 1)
            dve.tensor_tensor_scan(F[:, SEQ:], one[:, SEQ:], lf[:, SEQ:], 0.0, ALU.mult, ALU.add).then_inc(scan.sem, 1)
            dve.wait_ge(f_t.sem, 1)
            dve.tensor_copy(lft[:, 0:NT, :], c.bank[0][:, 0:NT * HEADS].rearrange("p (t h) -> p t h", t=NT))
            dve.tensor_copy(lft[0:NEW, SM, :], c.bank[0][0:NEW, NT * HEADS:TT * HEADS]).then_inc(f_tc.sem, 1)
            dve.wait_ge(f_hi.sem, 3)
            dve.tensor_tensor(K.B[32:32 + HEADS, :], F[:], K.B[0:HEADS, :].bitcast(F32), ALU.subtract).then_inc(f_lo.sem, 1)
            dve.tensor_tensor(K.A[96:96 + HEADS, 0:SEQ], F[:, 0:SEQ], K.B[0:HEADS, 0:SEQ].bitcast(F32),
                              ALU.subtract).then_inc(f_lo.sem, 1)
            dve.tensor_tensor(K.A[96:96 + HEADS, SEQ:SEQ + NEW], F[:, SEQ + PAST:],
                              K.B[0:HEADS, SEQ + PAST:].bitcast(F32), ALU.subtract).then_inc(f_lo.sem, 1)

        @block.tensor
        def _(pe):
            pe.wait_ge(consts.sem, 16 * n_const)
            pe.wait_ge(xh.sem, TT)
            T.pe(pe)
            pe.wait_ge(T.lo_out.sem, len(T.jobs()))
            pe.wait_ge(wf_lo.sem, 2)
            for k in range(KT):
                for i, a in enumerate((act[0], act[1])):
                    op = pe.matmul(c.bank[6][0:48, :], wfs[:, k, :], a[:, k, :], start=(k == 0 and i == 0),
                                   stop=(k == KT - 1 and i == 1))
            op.then_inc(f_mm.sem, 1)
            for k in range(KT):
                op = pe.matmul(c.bank[7][0:48, 0:2 * NEW], wfs[:, k, :], act[2][:, k, :], start=(k == 0), stop=(k == KT - 1))
            op.then_inc(f_mm.sem, 1)
            pe.wait_ge(logs.sem, 2)
            for t in range(TT):
                n, a = rows(t), (t * P if t < SM else SEQ + PAST)
                op = pe.transpose(c.bank[0][0:n, t * HEADS:(t + 1) * HEADS], lf[:, a:a + n], K.ident[0:HEADS, 0:HEADS])
            op.then_inc(f_t.sem, 1)


class Consts:

    def __init__(self, c):
        self.base = (c.limit - 12544) // 64 * 64
        place = c.packer(self.base)
        self.c = c
        self.ident = place("ident", [P, P])
        self.mask_fox, self.mask_mla = place("mask_fox", [P, P]), place("mask_mla", [P, P])
        self.ident_b, self.mask_fox_b, self.mask_mla_b = (place(n, [P, P], BF16) for n in ("ident_b", "mask_fox_b", "mask_mla_b"))
        self.g_fox, self.g_kv, self.g_mla = (place(n, [P, KT]) for n in ("g_fox", "g_kv", "g_mla"))
        self.g_qa = place("g_qa", [P, LT])
        self.b_f = place("b_f", [HEADS, 1])
        self.one_col = place("one_col", [P, 1])
        self.nsel, self.psel = place("nsel", [P, HEADS]), place("psel", [P, HEADS])
        self.gq, self.gk = place("gq", [P, P]), place("gk", [P, P])
        self.A = place("decay_q", [P, SEQ + NEW], F32R)
        self.B = place("decay_k", [P, TIME], F32R)
        self.end = place.cur[0]
        assert self.end <= c.limit, (self.end, c.limit)
        self.loads = [(self.mask_fox, "mask_fox"), (self.mask_mla, "mask_mla"), (self.g_fox, "g_fox"),
                      (self.g_kv, "g_kv"), (self.g_mla, "g_mla"), (self.g_qa, "g_qa"), (self.b_f, "b_f"),
                      (self.nsel, "nsel"), (self.psel, "psel"), (self.gq, "g_q"), (self.gk, "g_k")]
        self.o_fox = c.at("o_fox", [HD, HEADS, SEQ + NEW], F32, c.Y)
        self.act = (c.at("x_hi", [P, KT, SEQ], F32R, c.X), c.at("x_lo", [P, KT, SEQ], F32R, c.X + 32768),
                    c.at("x_smp", [P, KT, 2 * NEW], F32R, c.X + 65536))


class FoxHead:

    NAMES = ["new_qk", "q", "k", "s3", "s2", "s1", "s0", "sa", "sb", "p0", "p1", "p2", "p3", "pn", "o", "on",
             "g", "gn"]
    SLOTS = [8, 9, 10, 12, 14, 16, 18, 20, 21, 25, 27, 28, 29, 30, 33, 34, 35, 37]
    SPLITS = ["cache_k", "new_qk", "q", "k", "p0", "p1", "p2", "p3", "pn"]

    def __init__(self, c, K, place):
        self.c, self.K = c, K
        self.jobs = {n: (s, i) for i, (n, s) in enumerate(zip(self.NAMES, self.SLOTS))}
        self.raw = place("b_raw", [P, TT, 4, HD])
        self.qk2 = place("b_qk2", [P, TT, 2, HD])
        self.ss, self.rstd, self.half = place("b_ss", [P, 2 * TT]), place("b_rstd", [P, 2 * TT]), place("b_half", [P, 2 * TT])
        self.vhi, self.vlo = place("b_vhi", [P, TT, HD], F32R), place("b_vlo", [P, TT, HD], F32R)
        self.ck = place("b_ck", [HD, PAST])
        self.cv = place("b_cv", [P, NT, HD])
        self.cvhi, self.cvlo = place("b_cvhi", [P, NT, HD], F32R), place("b_cvlo", [P, NT, HD], F32R)
        self.qhi, self.qlo = place("b_qhi", [HD, SEQ], F32R), place("b_qlo", [HD, SEQ], F32R)
        self.khi, self.klo = place("b_khi", [HD, SEQ], F32R), place("b_klo", [HD, SEQ], F32R)
        self.nqhi, self.nqlo = place("b_nqhi", [HD, NEW], F32R), place("b_nqlo", [HD, NEW], F32R)
        self.nkhi, self.nklo = place("b_nkhi", [HD, SAMP], F32R), place("b_nklo", [HD, SAMP], F32R)
        self.p = [place(f"b_p{i}", [P, (i + 1) * P]) for i in range(NT)]
        self.pn = place("b_pn", [NEW, SAMP])
        self.first = [0, P, 2 * P, 2 * P]
        self.pt = [(place(f"b_pt{j}hi", [P, SEQ - f], F32R), place(f"b_pt{j}lo", [P, SEQ - f], F32R))
                   for j, f in enumerate(self.first)]
        self.ptn = (place("b_ptnhi", [P, 512], F32R), place("b_ptnlo", [P, 512], F32R))
        self.gate = place("b_gate", [P, TT, HD])
        self.o = place("b_o", [HD, SEQ + NEW])
        self.nm, self.rs, self.ri = place("b_nm", [P, TT]), place("b_rs", [P, TT]), place("b_ri", [P, TT])
        self.m2, self.r2 = place("b_m2", [NEW, 2]), place("b_r2", [NEW, 2])
        s = c.sem
        self.ready = [s(f"b_ready{b}", 6) for b in range(3)]
        self.free = [s(f"b_free{b}", 6, credit=1) for b in range(3)]
        self.took = s("b_took", NT)
        self.took_lo = s("b_took_lo")
        self.took_smp = s("b_took_smp")
        self.sq = s("b_sq")
        self.sums = s("b_sums")
        self.var, self.rst = s("b_var"), s("b_rst")
        self.sel = s("b_sel", 2)
        self.normed = s("b_normed")
        self.v_hi, self.v_lo = s("b_v_hi"), s("b_v_lo")
        self.tanh, self.gated, self.scaled = s("b_tanh"), s("b_gated"), s("b_scaled")
        self.hi_done = s("b_hi_done", len(self.SPLITS))
        self.ck_lo = s("b_ck_lo")
        self.new_max = s("b_new_max", 2)
        self.negmax = s("b_negmax", TT)
        self.inv = s("b_inv", 2)
        self.o_done = s("b_o_done", 2)
        self.ck_in, self.cv_in = s("b_ck_in", 1, 16), s("b_cv_in", 1, 16)
        self.out = s("b_out", 4, 16)
        self.zero = s("b_zero")

    def bank(self, name):
        return self.c.bank[5 + self.jobs[name][1] % 3]

    def _nth(self, name):
        i = self.jobs[name][1]
        return i % 3, i // 3 + 1

    def wait_ready(self, eng, g, name):
        b, k = self._nth(name)
        self.ready[b].wait(eng, g, k)

    def wait_free(self, eng, g, name):
        b, k = self._nth(name)
        self.free[b].wait(eng, g, k - 1)

    def wait_out_of(self, eng, g, name):
        b, k = self._nth(name)
        self.free[b].wait(eng, g, k)

    def end(self, op, name):
        op.then_inc(self.ready[self._nth(name)[0]].sem, 1)

    def release(self, op, name):
        op.then_inc(self.free[self._nth(name)[0]].sem, 1)

    def split_views(self, name):
        b = self.bank(name)
        if name == "new_qk":
            return [(b[:, 0:NEW], self.nqhi[:], self.nqlo[:]),
                    (b[:, NEW:2 * NEW], self.nkhi[:, PAST:], self.nklo[:, PAST:])]
        if name == "q":
            return [(b[:, :], self.qhi[:], self.qlo[:])]
        if name == "k":
            return [(b[:, :], self.khi[:], self.klo[:])]
        if name == "pn":
            hi, lo = self.ptn
            n = NT * NEW
            return [(b[:, 0:n], hi[:, 0:n], lo[:, 0:n]),
                    (b[0:NEW, n:n + NEW], hi[0:NEW, n:n + NEW], lo[0:NEW, n:n + NEW])]
        if name[0] == "p":
            j = int(name[1])
            hi, lo = self.pt[j]
            a = j * P - self.first[j]
            return [(b[:, j * P:], hi[:, a:], lo[:, a:])]
        raise KeyError(name)

    def act_split(self, eng, g, name):
        if name == "cache_k":
            self.ck_in.wait(eng, g, 1)
            eng.activation(self.nkhi[:, 0:PAST], self.ck[:], ACT.Copy).then_inc(self.hi_done.sem, 1)
            return
        self.wait_ready(eng, g, name)
        for src, hi, lo in self.split_views(name):
            op = eng.activation(hi, src, ACT.Copy)
        op.then_inc(self.hi_done.sem, 1)

    def dve_split(self, eng, g, name):
        self.hi_done.wait(eng, g, self.SPLITS.index(name) + 1)
        if name == "cache_k":
            eng.tensor_tensor(self.nklo[:, 0:PAST], self.ck[:], self.nkhi[:, 0:PAST].bitcast(F32),
                              ALU.subtract).then_inc(self.ck_lo.sem, 1)
            return
        for src, hi, lo in self.split_views(name):
            op = eng.tensor_tensor(lo, src, hi.bitcast(F32), ALU.subtract)
        self.release(op, name)

    def act_take(self, eng, h, t, gemm):
        if t < SM:
            gemm.done.wait(eng, h, t + 1)
            eng.activation(self.raw[:, t, :, :], self.c.bank[t][:, :].rearrange("p (s d) -> p s d", s=4),
                           ACT.Copy).then_inc(self.took.sem, 1)
        else:
            gemm.used.wait(eng, h, gemm.units)
            eng.activation(self.raw[0:NEW, SM, :, :],
                           self.c.bank[SM][NEW:2 * NEW, :].rearrange("p (s d) -> p s d", s=4),
                           ACT.Copy).then_inc(self.took_lo.sem, 1)

    def dve_take(self, eng, h):
        self.took_lo.wait(eng, h, 1)
        raw = self.raw[0:NEW, SM, :, :].rearrange("p s d -> p (s d)")
        eng.tensor_tensor(raw, self.c.bank[SM][0:NEW, :], raw, ALU.add).then_inc(self.took_smp.sem, 1)

    def act_squares(self, eng, g):
        self.took_smp.wait(eng, g, 1)
        self.took.wait(eng, g, NT)
        for n, t in ((P, slice(0, NT)), (NEW, slice(SM, TT))):
            op = eng.activation(self.qk2[0:n, t, :, :], self.raw[0:n, t, 0:2, :], ACT.Square)
        op.then_inc(self.sq.sem, 1)

    def act_values(self, eng, g):
        for n, t in ((P, slice(0, NT)), (NEW, slice(SM, TT))):
            op = eng.activation(self.vhi[0:n, t, :], self.raw[0:n, t, 2, :], ACT.Copy)
        self.cv_in.wait(eng, g, 1)
        op = eng.activation(self.cvhi[:], self.cv[:], ACT.Copy)
        op.then_inc(self.v_hi.sem, 1)

    def act_tanh(self, eng, g):
        for n, t in ((P, slice(0, NT)), (NEW, slice(SM, TT))):
            op = eng.activation(self.gate[0:n, t, :], self.raw[0:n, t, 3, :], ACT.Tanh, scale=0.5)
        op.then_inc(self.tanh.sem, 1)

    def act_exp(self, eng, g, name):
        b = self.bank(name)
        if name in ("sa", "sb"):
            i = ("sa", "sb").index(name)
            self.negmax.wait(eng, g, TT)
            op = eng.activation(self.pn[:, i * 288:(i + 1) * 288], b[0:NEW, 0:288], ACT.Exp, bias=self.nm[0:NEW, SM:TT],
                                accum_out=self.r2[:, i:i + 1])
        else:
            i = int(name[1])
            self.negmax.wait(eng, g, NT - i)
            op = eng.activation(self.p[i][:], b[:, 0:(i + 1) * P], ACT.Exp, bias=self.nm[:, i:i + 1],
                                accum_out=self.rs[:, i:i + 1])
        self.release(op, name)

    def act_o(self, eng, g, name):
        self.wait_ready(eng, g, name)
        a, n = (0, SEQ) if name == "o" else (SEQ, NEW)
        op = eng.activation(self.o[:, a:a + n], self.bank(name)[:, 0:n], ACT.Copy)
        self.release(op, name)

    def dve_sums(self, eng, g):
        self.sq.wait(eng, g, 1)
        for n, t in ((P, slice(0, NT)), (NEW, slice(SM, TT))):
            op = eng.tensor_reduce(self.ss[0:n, 2 * t.start:2 * t.stop], self.qk2[0:n, t, :, :].rearrange("p t s d -> p (t s) d"),
                                   AX.X, ALU.add)
        op.then_inc(self.sums.sem, 1)
        self.sums.wait(eng, g, 1)
        eng.tensor_scalar(self.ss[:], self.ss[:], 1.0 / HD, EPS, ALU.mult, ALU.add).then_inc(self.var.sem, 1)

    def dve_norm(self, eng, g):
        self.rst.wait(eng, g, 1)
        for t in range(TT):
            for s, gain in ((0, self.K.gq), (1, self.K.gk)):
                x = self.raw[0:rows(t), t, s, :]
                op = eng.scalar_tensor_tensor(x, x, self.rstd[0:rows(t), 2 * t + s:2 * t + s + 1], gain[0:rows(t), :],
                                              ALU.mult, ALU.mult)
        op.then_inc(self.normed.sem, 1)

    def dve_values(self, eng, g):
        self.v_hi.wait(eng, g, 1)
        for n, t in ((P, slice(0, NT)), (NEW, slice(SM, TT))):
            op = eng.tensor_tensor(self.vlo[0:n, t, :], self.raw[0:n, t, 2, :], self.vhi[0:n, t, :].bitcast(F32), ALU.subtract)
        op = eng.tensor_tensor(self.cvlo[:], self.cv[:], self.cvhi[:].bitcast(F32), ALU.subtract)
        op.then_inc(self.v_lo.sem, 1)

    def dve_gate(self, eng, g):
        self.tanh.wait(eng, g, 1)
        for n, t in ((P, slice(0, NT)), (NEW, slice(SM, TT))):
            y = self.gate[0:n, t, :]
            op = eng.scalar_tensor_tensor(y, y, 1.0, self.raw[0:n, t, 3, :], ALU.add, ALU.mult)
        op.then_inc(self.gated.sem, 1)

    def dve_max(self, eng, g, name):
        self.wait_ready(eng, g, name)
        b = self.bank(name)
        if name in ("sa", "sb"):
            i = ("sa", "sb").index(name)
            eng.tensor_reduce(self.m2[:, i:i + 1], b[0:NEW, 0:288], AX.X, ALU.max).then_inc(self.new_max.sem, 1)
            if i:
                self.new_max.wait(eng, g, 2)
                eng.tensor_reduce(self.nm[0:NEW, SM:TT], self.m2[:], AX.X, ALU.max, negate=True).then_inc(self.negmax.sem, 1)
        else:
            i = int(name[1])
            eng.tensor_reduce(self.nm[:, i:i + 1], b[:, 0:(i + 1) * P], AX.X, ALU.max, negate=True).then_inc(self.negmax.sem, 1)

    def dve_scale_gate(self, eng, g):
        self.wait_out_of(eng, g, "sb")
        eng.tensor_tensor(self.rs[0:NEW, SM:TT], self.r2[:, 0:1], self.r2[:, 1:2], ALU.add).then_inc(self.inv.sem, 1)
        self.inv.wait(eng, g, 1)
        eng.reciprocal(self.ri[:], self.rs[:]).then_inc(self.inv.sem, 1)
        self.inv.wait(eng, g, 2)
        self.gated.wait(eng, g, 1)
        for t in range(TT):
            y = self.gate[0:rows(t), t, :]
            op = eng.tensor_scalar(y, y, self.ri[0:rows(t), t:t + 1], 0.5, ALU.mult, ALU.mult)
        op.then_inc(self.scaled.sem, 1)

    def dve_o(self, eng, g, name, dst):
        self.wait_ready(eng, g, name)
        first = "o" if name == "g" else "on"
        self.wait_out_of(eng, g, first)
        a, n = (0, SEQ) if name == "g" else (SEQ, NEW)
        op = eng.tensor_tensor(dst[:, g, a:a + n], self.bank(name)[:, 0:n], self.o[:, a:a + n], ALU.mult)
        self.release(op, name)

    def pe_job(self, eng, g, name):
        K, b = self.K, self.bank(name)
        self.wait_free(eng, g, name)
        if name == "new_qk":
            self.normed.wait(eng, g, 1)
            for s in range(2):
                op = turn(eng, b[:, s * NEW:(s + 1) * NEW], self.raw[0:NEW, SM, s, :], K.ident[0:NEW, 0:NEW], s == 0)
        elif name in ("q", "k"):
            for t in range(NT):
                op = eng.transpose(b[:, t * P:(t + 1) * P], self.raw[:, t, "qk".index(name), :], K.ident[:, :])
        elif name in ("s0", "s1", "s2", "s3"):
            i = int(name[1])
            n = max(i + 1, 2) * P
            self.wait_out_of(eng, g, "q")
            self.wait_out_of(eng, g, "k")
            self.sel.wait(eng, g, 2)
            q = slice(i * P, (i + 1) * P)
            for m, (x, y) in enumerate(three(self.qhi, self.qlo, self.khi, self.klo)):
                eng.matmul(b[:, 0:n], x[:, q], y[:, 0:n], start=(m == 0), stop=False)
            eng.matmul(b[:, q], K.ident_b[:, :], K.mask_fox_b[:, :], start=False, stop=False, skip_group_check=True)
            op = eng.matmul(b[:, 0:n], K.A[:, q], K.B[:, 0:n], start=False, stop=True)
        elif name in ("sa", "sb"):
            i = ("sa", "sb").index(name)
            k = slice(i * 288, (i + 1) * 288)
            self.ck_lo.wait(eng, g, 1)
            self.wait_out_of(eng, g, "new_qk")
            for m, (x, y) in enumerate(three(self.nqhi, self.nqlo, self.nkhi, self.nklo)):
                eng.matmul(b[0:NEW, 0:288], x[:, :], y[:, k], start=(m == 0), stop=False)
            if i:
                eng.matmul(b[0:NEW, 224:288], K.ident_b[0:NEW, 0:NEW], K.mask_fox_b[0:NEW, 0:NEW], start=False,
                           stop=False, skip_group_check=True)
            op = eng.matmul(b[0:NEW, 0:288], K.A[:, SEQ:SEQ + NEW], K.B[:, SEQ + i * 288:SEQ + (i + 1) * 288],
                            start=False, stop=True)
        elif name == "pn":
            self.wait_out_of(eng, g, "sb")
            for t in range(TT):
                n = rows(t)
                op = turn(eng, b[0:n, t * NEW:(t + 1) * NEW], self.pn[:, t * P:t * P + n], K.ident[0:NEW, 0:NEW], t == 0)
        elif name[0] == "p":
            j = int(name[1])
            self.wait_out_of(eng, g, "s0")
            for i in range(j, NT):
                op = eng.transpose(b[:, i * P:(i + 1) * P], self.p[i][:, j * P:(j + 1) * P], K.ident[:, :])
        elif name == "o":
            for j in range(NT):
                self.wait_out_of(eng, g, f"p{j}")
            self.v_lo.wait(eng, g, 1)
            for j in range(NT):
                f = self.first[j]
                for m, (x, y) in enumerate(three(self.vhi, self.vlo, *self.pt[j])):
                    op = eng.matmul(b[:, f:], x[:, j, :], y[:, :], start=(j == 0 and m == 0), stop=(j == NT - 1 and m == 2))
        elif name == "on":
            self.wait_out_of(eng, g, "pn")
            for t in range(TT):
                v = (self.cvhi, self.cvlo) if t < SM else (self.vhi, self.vlo)
                n = rows(t)
                for m, (x, y) in enumerate(three(*v, *self.ptn)):
                    op = eng.matmul(b[:, 0:256], x[0:n, t, :], y[0:n, t * NEW:t * NEW + 256],
                                    start=(t == 0 and m == 0), stop=(t == SM and m == 2))
        elif name == "g":
            self.scaled.wait(eng, g, 1)
            for t in range(NT):
                op = eng.transpose(b[:, t * P:(t + 1) * P], self.gate[:, t, :], K.ident[:, :])
        elif name == "gn":
            op = turn(eng, b[:, 0:NEW], self.gate[0:NEW, SM, :], K.ident[0:NEW, 0:NEW], True)
        self.end(op, name)


def block_b(c, K):
    nc, d = c.nc, c.dram
    place = c.packer(c.W)
    act = K.act
    G = Gemm(c, "b", d["w_fox"], HEADS, KT // UK, UK, 512, RAW_FOX, act, K.g_fox, place)
    H = FoxHead(c, K, place)
    o_all = K.o_fox
    assert place.cur[0] <= K.base
    U, R = G.units, G.raws
    cached = "cache_k"
    zero = H.zero

    with nc.Block() as block:
        @block.sync
        def _(sp):
            def body(h, last, g):
                for u in range(U):
                    if h is not None and not (last and u + R >= U):
                        n = u + R
                        G.load(sp, h + n // U if n >= U else h, n % U)
                    if g is not None and u == 0:
                        H.took.wait(sp, g, NT)
                        H.took_smp.wait(sp, g, 1)
                        sp.dma_start(d["out_fv"][g][:, 0:NT, :], H.raw[:, 0:NT, 2, :]).then_inc(H.out.sem, 16)
                        sp.dma_start(d["out_fv"][g][0:NEW, SM, :], H.raw[0:NEW, SM, 2, :]).then_inc(H.out.sem, 16)
                        H.normed.wait(sp, g, 1)
                        sp.dma_start(d["out_fk"][g][:, 0:NT, :], H.raw[:, 0:NT, 1, :]).then_inc(H.out.sem, 16)
                        sp.dma_start(d["out_fk"][g][0:NEW, SM, :], H.raw[0:NEW, SM, 1, :]).then_inc(H.out.sem, 16)
                if h is not None:
                    if g is not None:
                        H.ck_lo.wait(sp, g, 1)
                        H.v_lo.wait(sp, g, 1)
                    sp.dma_start(H.ck[:], d["cache_k"][h]).then_inc(H.ck_in.sem, 16)
                    sp.dma_start(H.cv[:], d["cache_v"][h]).then_inc(H.cv_in.sem, 16)
            for u in range(R):
                G.load(sp, 0, u)
            body(0, False, None)
            with sp.Fori(1, HEADS - 1) as h:
                body(h, False, h - 1)
            body(HEADS - 1, True, HEADS - 2)
            body(None, True, HEADS - 1)
            sp.wait_ge(H.out.sem, HEADS * 4 * 16)

        @block.gpsimd
        def _(pool):
            pool.tensor_scalar(K.gq[:], K.gq[:], FOX_SCALE, None, ALU.mult).then_inc(zero.sem, 1)
            pool.memset(H.ss[:], 1.0).then_inc(zero.sem, 1)
            pool.memset(H.rs[:], 1.0).then_inc(zero.sem, 1)
            pool.memset(H.half[:], -0.5).then_inc(zero.sem, 1)
            for x in (*H.ptn, *H.pt[NT - 1]):
                pool.memset(x[:].bitcast(F32), 0.0).then_inc(zero.sem, 1)

            def head(g):
                if not isinstance(g, int) or g > 0:
                    H.wait_ready(pool, g - 1, "sb")
                H.rst.wait(pool, g, 0)
                pool.tensor_copy(K.A[0:64, :], K.nsel[0:64, bass.ds(g, 1)].broadcast_to([64, SEQ + NEW])).then_inc(H.sel.sem, 1)
                H.sel.wait(pool, g, 1)
                pool.tensor_copy(K.B[64:P, :], K.psel[64:P, bass.ds(g, 1)].broadcast_to([64, TIME])).then_inc(H.sel.sem, 1)
                H.sel.wait(pool, g, 2)
                H.var.wait(pool, g, 1)
                pool.tensor_tensor(H.rstd[:], H.ss[:], H.half[:], ALU.pow).then_inc(H.rst.sem, 1)
            pool.wait_ge(zero.sem, 8)
            steps(pool, HEADS, lambda g, last: head(g))

        @block.scalar
        def _(act_):
            act_.wait_ge(zero.sem, 8)

            def body(h, last, g):
                for s in range(5 * U):
                    if g is not None:
                        if s == 0:
                            H.act_squares(act_, g)
                            H.act_split(act_, g, cached)
                        if s == 3:
                            H.act_values(act_, g)
                        if s == 4:
                            H.act_tanh(act_, g)
                        for name, (slot, _) in H.jobs.items():
                            if slot + 1 == s:
                                if name in H.SPLITS:
                                    H.act_split(act_, g, name)
                                elif name == "sb":
                                    H.act_exp(act_, g, "sa")
                                    H.act_exp(act_, g, "sb")
                                elif name[0] == "s" and name != "sa":
                                    H.act_exp(act_, g, name)
                                elif name in ("o", "on"):
                                    H.act_o(act_, g, name)
                    if h is not None and s % 5 == 1 and not (last and s // 5 == U - 1):
                        n = s // 5 + 1
                        G.make_hi(act_, h + n // U if n >= U else h, n % U)
                    if h is not None and s >= 5 * (U - 1) + 1:
                        t = s - 5 * (U - 1) - 1
                        if t == 0 and g is not None:
                            H.v_lo.wait(act_, g, 1)
                            H.gated.wait(act_, g, 1)
                            H.out.wait(act_, g, 4)
                        H.act_take(act_, h, t, G)
                if h is not None:
                    H.act_take(act_, h, SM, G)
            G.make_hi(act_, 0, 0)
            body(0, False, None)
            with act_.Fori(1, HEADS - 1) as h:
                body(h, False, h - 1)
            body(HEADS - 1, True, HEADS - 2)
            body(None, True, HEADS - 1)

        @block.vector
        def _(dve):
            dve.wait_ge(zero.sem, 8)
            for bank_free in H.free:
                bank_free.grant(dve)

            def body(h, last, g):
                for s in range(5 * U):
                    if g is not None:
                        if s == 0:
                            H.dve_sums(dve, g)
                            H.dve_split(dve, g, cached)
                        if s == 2:
                            H.dve_norm(dve, g)
                        if s == 4:
                            H.dve_values(dve, g)
                        if s == 5:
                            H.dve_gate(dve, g)
                        for name, (slot, _) in H.jobs.items():
                            if slot + 1 == s:
                                if name in H.SPLITS:
                                    H.dve_split(dve, g, name)
                                elif name[0] == "s":
                                    H.dve_max(dve, g, name)
                                elif name in ("g", "gn"):
                                    H.dve_o(dve, g, name, o_all)
                        if s == H.jobs["sb"][0] + 3:
                            H.dve_scale_gate(dve, g)
                    if h is not None and s % 5 == 1 and not (last and s // 5 == U - 1):
                        n = s // 5 + 1
                        G.make_lo(dve, h + n // U if n >= U else h, n % U)
                if h is not None:
                    H.dve_take(dve, h)
            G.make_lo(dve, 0, 0)
            body(0, False, None)
            with dve.Fori(1, HEADS - 1) as h:
                body(h, False, h - 1)
            body(HEADS - 1, True, HEADS - 2)
            body(None, True, HEADS - 1)

        @block.tensor
        def _(pe):
            pe.wait_ge(zero.sem, 8)

            def body(h, last, g):
                for s in range(5 * U):
                    u, t = s // 5, s % 5
                    if h is not None:
                        if t == 0:
                            G.w_lo.wait(pe, h, u + 1)
                        if u == 0 and g is not None:
                            if t < SM:
                                H.took.wait(pe, g, t + 1)
                            else:
                                H.took_smp.wait(pe, g, 1)
                        G.multiply(pe, h, u, t)
                    if g is not None:
                        for name, (slot, _) in H.jobs.items():
                            if slot == s:
                                H.pe_job(pe, g, name)
            body(0, False, None)
            with pe.Fori(1, HEADS - 1) as h:
                body(h, False, h - 1)
            body(HEADS - 1, True, HEADS - 2)
            body(None, True, HEADS - 1)


def out_proj(c, K, tag, w, o, act, resid, base, finish):
    nc, d = c.nc, c.dram
    place = c.packer(base)
    G = Gemm(c, tag, w, D_MODEL // 512, KT // UK, UK, 512, 4, act, None, place)
    U, R, N = G.units, G.raws, G.steps
    res = [place(f"{tag}_res{i}", [P, TT, 512]) for i in range(2)]
    tmp = place(f"{tag}_tmp", [NEW, 512])
    hi_o, lo_o = c.sem(f"{tag}_hi_o"), c.sem(f"{tag}_lo_o")
    res_in = c.sem(f"{tag}_res_in", 2, 16)
    moved, summed, rows_out = c.sem(f"{tag}_moved"), c.sem(f"{tag}_summed"), c.sem(f"{tag}_rows_out", TT)
    F = finish(c, K, tag, place, rows_out)
    hi, lo, smp = act

    with nc.Block() as block:
        @block.sync
        def _(sp):
            def load_res(n):
                if not isinstance(n, int) or n >= 2:
                    rows_out.wait(sp, n - 2, TT)
                for q, t in ((P, slice(0, NT)), (NEW, slice(SM, TT))):
                    sp.dma_start(res[n % 2][0:q, t, :], resid[0:q, t, n * 512:(n + 1) * 512]).then_inc(res_in.sem, 16)
            for u in range(R):
                G.load(sp, 0, u)
            load_res(0)
            load_res(1)
            for n in range(N):
                for u in range(U):
                    if n * U + u + R < N * U:
                        G.load(sp, n + (u + R) // U, (u + R) % U)
                    if u == 1 and n >= 1:
                        F.sp_step(sp, n - 1)
                        if n + 1 < N:
                            load_res(n + 1)
            F.sp_step(sp, N - 1)
            F.sp_tail(sp)

        @block.gpsimd
        def _(pool):
            F.pool(pool)

        @block.scalar
        def _(act_):
            for n in range(N):
                for u in range(U):
                    if n == 0:
                        k = slice(u * UK, (u + 1) * UK)
                        act_.activation(hi[:, k, :], o[:, k, 0:SEQ], ACT.Copy)
                        act_.activation(smp[:, k, 0:NEW], o[:, k, SEQ:SEQ + NEW], ACT.Copy).then_inc(hi_o.sem, 1)
                        G.make_hi(act_, 0, u)
                    elif u:
                        G.make_hi(act_, n, u)
                G.used.wait(act_, n, U)
                if n:
                    rows_out.wait(act_, n - 1, TT)
                act_.activation(tmp[:], c.bank[SM][NEW:2 * NEW, :], ACT.Copy).then_inc(moved.sem, 1)
                if n + 1 < N:
                    G.make_hi(act_, n + 1, 0)
                F.act_step(act_, n)
            F.act_tail(act_)

        @block.vector
        def _(dve):
            F.dve_head(dve)
            for n in range(N):
                for u in range(U):
                    if n == 0:
                        k = slice(u * UK, (u + 1) * UK)
                        dve.wait_ge(hi_o.sem, u + 1)
                        dve.tensor_tensor(lo[:, k, :], o[:, k, 0:SEQ], hi[:, k, :].bitcast(F32), ALU.subtract)
                        dve.tensor_tensor(smp[:, k, NEW:2 * NEW], o[:, k, SEQ:SEQ + NEW], smp[:, k, 0:NEW].bitcast(F32),
                                          ALU.subtract).then_inc(lo_o.sem, 1)
                        G.make_lo(dve, 0, u)
                    elif u:
                        G.make_lo(dve, n, u)
                res_in.wait(dve, n, 2)
                F.dve_ready(dve, n)
                for t in range(NT):
                    G.done.wait(dve, n, t + 1)
                    dve.tensor_tensor(F.dst(n, t), c.bank[t][:, :], res[n % 2][:, t, :], ALU.add).then_inc(rows_out.sem, 1)
                moved.wait(dve, n, 1)
                dve.tensor_tensor(tmp[:], tmp[:], res[n % 2][0:NEW, SM, :], ALU.add).then_inc(summed.sem, 1)
                summed.wait(dve, n, 1)
                dve.tensor_tensor(F.dst(n, SM), c.bank[SM][0:NEW, :], tmp[:], ALU.add).then_inc(rows_out.sem, 1)
                if n + 1 < N:
                    G.make_lo(dve, n + 1, 0)
                F.dve_step(dve, n)
            F.dve_tail(dve)

        @block.tensor
        def _(pe):
            for n in range(N):
                for u in range(U):
                    G.w_lo.wait(pe, n, u + 1)
                    if n == 0:
                        pe.wait_ge(lo_o.sem, u + 1)
                    for t in range(TT):
                        if u == 0 and n:
                            rows_out.wait(pe, n - 1, t + 1)
                        G.multiply(pe, n, u, t)
            F.pe_tail(pe)


class FinishC:

    def __init__(self, c, K, tag, place, rows_out):
        self.c, self.K, self.rows_out = c, K, rows_out
        self.x1 = c.at("x1", [P, TT, D_MODEL], F32, c.Y)
        self.sq = place("c_squares", [P, TT, 512])
        self.ss4, self.ss = place("c_ss4", [P, TT, 4]), place("c_ss", [P, TT])
        self.rstd, self.half = place("c_rstd", [P, TT]), place("c_half", [P, TT])
        self.T = Transposer(c, "c", self.x1, K.act, K.ident, KT)
        self.squared, self.reduced = c.sem("c_squared"), c.sem("c_reduced")
        self.stored = c.sem("c_stored", 2, 16)
        self.init, self.total, self.var, self.rst, self.xh = (c.sem(f"c_{n}") for n in ("init", "total", "var", "rst", "xh"))

    def dst(self, n, t):
        return self.x1[0:rows(t), t, n * 512:(n + 1) * 512]

    def sp_step(self, sp, n):
        self.rows_out.wait(sp, n, TT)
        for q, t in ((P, slice(0, NT)), (NEW, slice(SM, TT))):
            sp.dma_start(self.c.dram["x1"][0:q, t, n * 512:(n + 1) * 512],
                         self.x1[0:q, t, n * 512:(n + 1) * 512]).then_inc(self.stored.sem, 16)

    def sp_tail(self, sp):
        sp.wait_ge(self.stored.sem, 8 * 16)

    def pool(self, pool):
        pool.memset(self.ss4[:], 1.0).then_inc(self.init.sem, 1)
        pool.memset(self.half[:], -0.5).then_inc(self.init.sem, 1)
        pool.wait_ge(self.init.sem, 2)
        pool.wait_ge(self.total.sem, 1)
        pool.tensor_scalar(self.ss[:], self.ss[:], 1.0 / D_MODEL, EPS, ALU.mult, ALU.add).then_inc(self.var.sem, 1)
        pool.wait_ge(self.var.sem, 1)
        pool.tensor_tensor(self.rstd[:], self.ss[:], self.half[:], ALU.pow).then_inc(self.rst.sem, 1)

    def act_step(self, act_, n):
        self.rows_out.wait(act_, n, TT)
        if n:
            self.reduced.wait(act_, n - 1, 1)
        for q, t in ((P, slice(0, NT)), (NEW, slice(SM, TT))):
            op = act_.activation(self.sq[0:q, t, :], self.x1[0:q, t, n * 512:(n + 1) * 512], ACT.Square)
        op.then_inc(self.squared.sem, 1)

    def act_tail(self, act_):
        self.T.act(act_)

    def dve_head(self, dve):
        dve.wait_ge(self.init.sem, 2)

    def dve_ready(self, dve, n):
        pass

    def dve_step(self, dve, n):
        self.squared.wait(dve, n, 1)
        for q, t in ((P, slice(0, NT)), (NEW, slice(SM, TT))):
            op = dve.tensor_reduce(self.ss4[0:q, t, n:n + 1], self.sq[0:q, t, :], AX.X, ALU.add)
        op.then_inc(self.reduced.sem, 1)

    def dve_tail(self, dve):
        dve.wait_ge(self.reduced.sem, 4)
        dve.tensor_reduce(self.ss[:], self.ss4[:], AX.X, ALU.add).then_inc(self.total.sem, 1)
        dve.wait_ge(self.rst.sem, 1)
        dve.wait_ge(self.stored.sem, 8 * 16)
        for t in range(TT):
            x = self.x1[0:rows(t), t, :]
            dve.tensor_scalar(x, x, self.rstd[0:rows(t), t:t + 1], None, ALU.mult).then_inc(self.xh.sem, 1)
        self.T.dve(dve)

    def pe_tail(self, pe):
        pe.wait_ge(self.rows_out.sem, 4 * TT)
        pe.wait_ge(self.xh.sem, TT)
        self.T.pe(pe)


class FinishG:

    def __init__(self, c, K, tag, place, rows_out):
        self.c, self.rows_out = c, rows_out
        self.y = [place(f"y{i}", [P, TT, 512]) for i in range(2)]
        self.stored = c.sem("g_stored", 2, 16)

    def dst(self, n, t):
        return self.y[n % 2][0:rows(t), t, :]

    def sp_step(self, sp, n):
        self.rows_out.wait(sp, n, TT)
        for q, t in ((P, slice(0, NT)), (NEW, slice(SM, TT))):
            sp.dma_start(self.c.dram["out_y"][0:q, t, n * 512:(n + 1) * 512], self.y[n % 2][0:q, t, :]).then_inc(self.stored.sem, 16)

    def sp_tail(self, sp):
        sp.wait_ge(self.stored.sem, 8 * 16)

    def dve_ready(self, dve, n):
        if n >= 2:
            self.stored.wait(dve, n - 2, 2)

    def pool(self, pool):
        pass

    act_step = dve_step = lambda self, eng, n: None
    act_tail = dve_head = dve_tail = pe_tail = lambda self, eng: None


def block_c(c, K):
    o = K.o_fox
    out_proj(c, K, "c", c.dram["w_out1"], o, K.act, c.dram["x"], c.W, FinishC)


class Shared:

    def __init__(self, c):
        y = c.packer(c.Y)
        self.c = (y("c_hi", [P, LT, SEQ], F32R), y("c_lo", [P, LT, SEQ], F32R), y("c_smp", [P, LT, 2 * NEW], F32R))
        self.pc = (y("pc_hi", [P, LT, PAST], F32R), y("pc_lo", [P, LT, PAST], F32R))
        self.g_ckv = y("g_ckv", [P, LAT])
        self.cos, self.sin = y("cos", [P, 2, TT, ROPE // 2]), y("sin", [P, 2, TT, ROPE // 2])
        w = c.packer(max(c.W, y.cur[0]))
        self.gkr = w("g_kr", [P, ROPE])
        self.gqr, self.gkn, self.gqn = w("g_qr", [P, ROPE]), w("g_kn", [P, HD]), w("g_qn", [P, HD])
        self.kr = (w("kr_hi", [ROPE, TIME], F32R), w("kr_lo", [ROPE, TIME], F32R))
        self.f_base = w.cur[0]
        self.ql = (w("ql_hi", [P, LT, SEQ], F32R), w("ql_lo", [P, LT, SEQ], F32R), w("ql_smp", [P, LT, 2 * NEW], F32R))
        self.base = w.cur[0]


def rotate(eng, dst, x, cos, sin, tmp, wait_tmp, sig):
    H = ROPE // 2
    x1, x2 = x[..., 0:H], x[..., H:ROPE]
    for i, (a, b) in enumerate(((x1, cos), (x2, sin), (x2, cos), (x1, sin))):
        op = eng.tensor_tensor(tmp[i], a, b, ALU.mult)
    op.then_inc(sig.sem, 1)
    wait_tmp(eng)
    eng.tensor_tensor(dst[..., 0:H], tmp[0], tmp[1], ALU.subtract)
    return eng.tensor_tensor(dst[..., H:ROPE], tmp[2], tmp[3], ALU.add)


def block_d(c, K, S):
    nc, d = c.nc, c.dram
    place = c.packer(S.base)
    Gd = Gemm(c, "d", d["w_dkv"], 2, KT // UK, UK, 288, 2, K.act, K.g_kv, place)
    Gm = Gemm(c, "m", d["w_mla"], 5, KT // UK, UK, 512, 2, K.act, K.g_mla, place)
    U = KT // UK
    raw = place("d_raw", [P, TT, LAT + ROPE])
    sq = c.at("d_sq", [P, TT, LAT + ROPE], F32, S.base)
    ss, rstd, half = place("d_ss", [P, 2 * TT]), place("d_rstd", [P, 2 * TT]), place("d_half", [P, 2 * TT])
    kr = place("d_kr", [P, TT, ROPE])
    rt = place("d_rt", [P, 4, TT, ROPE // 2])
    lat_lo = place("d_lo", [NEW, 512])
    pkr = place("d_pkr", [ROPE, PAST])
    gate_at = place.cur[0]
    gate = place("d_gate", [P, TT, 512])
    assert place.cur[0] <= K.base, (place.cur[0], K.base)
    pc = c.at("d_pc", [P, LT, PAST], F32, gate_at)
    Tc = Transposer(c, "tc", raw, S.c, K.ident, LT, banks=(5, 6), smp_banks=(7,))
    Tq = Transposer(c, "tq", raw, S.ql, K.ident, LT, banks=(5, 6), smp_banks=(7,))
    s = c.sem
    init, loads = s("d_init"), s("d_loads", unit=16)
    took, took_lo, took_smp = s("d_took", NT), s("d_took_lo"), s("d_took_smp")
    sqd, sums, var, rst = s("d_sqd"), s("d_sums"), s("d_var", 2), s("d_rst")
    normed, scaled_kr, prods, kr_done = s("d_normed"), s("d_scaled_kr"), s("d_prods"), s("d_kr_done")
    out = s("d_out", unit=16)
    past_hi, past_lo = s("d_past_hi"), s("d_past_lo")
    kr_t, kr_hi, kr_lo = s("d_kr_t"), s("d_kr_hi"), s("d_kr_lo")
    th, gated = s("d_tanh", TT), s("d_gated", TT)
    g_lo, g_sum = s("d_g_lo"), s("d_g_sum")
    g_out = s("d_g_out", 8, 16)
    order = [(Gd, 0), (Gd, 1)] + [(Gm, n) for n in range(5)]
    flat = [(i, G, n, u) for i, (G, n) in enumerate(order) for u in range(U)]
    n_loads = 9

    def store_gate(sp, g):
        gated.wait(sp, g, TT)
        for q, t in ((P, slice(0, NT)), (NEW, slice(SM, TT))):
            for j in range(4):
                sp.dma_start(d["gates"][4 * g + j, 0:q, t, :], gate[0:q, t, j * HD:(j + 1) * HD]).then_inc(g_out.sem, 16)

    with nc.Block() as block:
        @block.sync
        def _(sp):
            for u in range(2):
                Gd.load(sp, 0, u)
            for dst, name in ((S.g_ckv, "g_ckv"), (S.gkr, "g_kr"), (S.gqr, "g_qr"), (S.gkn, "g_kn"), (S.gqn, "g_qn"),
                              (S.cos, "cos"), (S.sin, "sin"), (pc, "cache_ckv"), (pkr, "cache_kr")):
                sp.dma_start(dst[:], d[name]).then_inc(loads.sem, 16)
            for u in range(2):
                Gm.load(sp, 0, u)
            for i, G, n, u in flat:
                m = n * U + u + 2
                if m < G.steps * U:
                    G.load(sp, m // U, m % U)
                if i == 2 and u == 4:
                    sp.wait_ge(normed.sem, 1)
                    sp.dma_start(d["out_ckv"][:, 0:NT, :], raw[:, 0:NT, 0:LAT]).then_inc(out.sem, 16)
                    sp.dma_start(d["out_ckv"][0:NEW, SM, :], raw[0:NEW, SM, 0:LAT]).then_inc(out.sem, 16)
                    sp.wait_ge(kr_done.sem, 1)
                    sp.dma_start(d["out_kr"][:, 0:NT, :], kr[:, 0:NT, :]).then_inc(out.sem, 16)
                    sp.dma_start(d["out_kr"][0:NEW, SM, :], kr[0:NEW, SM, :]).then_inc(out.sem, 16)
                if i >= 4 and u == 2:
                    store_gate(sp, i - 4)
            store_gate(sp, 3)
            sp.wait_ge(out.sem, 64)
            g_out.wait(sp, 3, 8)

        @block.gpsimd
        def _(pool):
            pool.memset(raw[:, SM, :], 0.0).then_inc(init.sem, 1)
            pool.memset(half[:], -0.5).then_inc(init.sem, 1)
            pool.wait_ge(init.sem, 2)
            for g in range(2):
                sums.wait(pool, g, 1)
                if g:
                    rst.wait(pool, 0, 1)
                pool.tensor_scalar(ss[:, 0:TT], ss[:, 0:TT], 1.0 / LAT, EPS, ALU.mult, ALU.add).then_inc(var.sem, 1)
                pool.tensor_scalar(ss[:, TT:], ss[:, TT:], 1.0 / ROPE, EPS, ALU.mult, ALU.add).then_inc(var.sem, 1)
                var.wait(pool, g, 2)
                pool.tensor_tensor(rstd[:], ss[:], half[:], ALU.pow).then_inc(rst.sem, 1)

        @block.scalar
        def _(act_):
            act_.wait_ge(init.sem, 2)
            Gd.make_hi(act_, 0, 0)
            for i, G, n, u in flat:
                if (i, u) != (0, 0) and u:
                    G.make_hi(act_, n, u)
                if i in (2, 3) and u == 1:
                    g = i - 2
                    took.wait(act_, i - 1, NT)
                    took_smp.wait(act_, i - 1, 1)
                    w = LAT + ROPE if g == 0 else LAT
                    act_.activation(sq[:, :, 0:w], raw[:, :, 0:w], ACT.Square).then_inc(sqd.sem, 1)
                if i == 2 and u == 3:
                    act_.wait_ge(loads.sem, 16 * n_loads)
                    act_.activation(S.pc[0][:], pc[:], ACT.Copy)
                    act_.activation(S.kr[0][:, SEQ:SEQ + PAST], pkr[:], ACT.Copy).then_inc(past_hi.sem, 1)
                if i == 2 and u == 6:
                    Tc.act(act_)
                    act_.wait_ge(kr_t.sem, 2)
                    act_.activation(S.kr[0][:, 0:SEQ], c.bank[5][0:ROPE, 0:SEQ], ACT.Copy)
                    act_.activation(S.kr[0][:, SEQ + PAST:], c.bank[6][0:ROPE, 0:NEW], ACT.Copy).then_inc(kr_hi.sem, 1)
                if i == 3 and u == 6:
                    Tq.act(act_)
                if u == U - 1:
                    if i + 1 < len(order):
                        order[i + 1][0].make_hi(act_, order[i + 1][1], 0)
                    if i <= 2:
                        a, w = (i * 288, 288) if i < 2 else (0, LAT)
                        if i == 2:
                            act_.wait_ge(out.sem, 64)
                            act_.wait_ge(kr_lo.sem, 1)
                        for t in range(NT):
                            G.done.wait(act_, n, t + 1)
                            act_.activation(raw[:, t, a:a + w], c.bank[t][:, 0:w], ACT.Copy).then_inc(took.sem, 1)
                        G.used.wait(act_, n, U)
                        act_.activation(raw[0:NEW, SM, a:a + w], c.bank[SM][NEW:2 * NEW, 0:w], ACT.Copy).then_inc(took_lo.sem, 1)
                    else:
                        g = i - 3
                        if g:
                            g_out.wait(act_, g - 1, 8)
                        else:
                            act_.wait_ge(past_lo.sem, 1)
                        for t in range(NT):
                            G.done.wait(act_, n, t + 1)
                            act_.activation(gate[:, t, :], c.bank[t][:, :], ACT.Tanh,
                                            scale=0.5).then_inc(th.sem, 1)
                        G.used.wait(act_, n, U)
                        if g:
                            gated.wait(act_, g - 1, TT)
                        act_.activation(lat_lo[:], c.bank[SM][NEW:2 * NEW, :], ACT.Copy).then_inc(g_lo.sem, 1)
                        g_sum.wait(act_, g, 1)
                        act_.activation(gate[0:NEW, SM, :], lat_lo[:], ACT.Tanh,
                                        scale=0.5).then_inc(th.sem, 1)

        @block.vector
        def _(dve):
            dve.wait_ge(init.sem, 2)
            Gd.make_lo(dve, 0, 0)
            for i, G, n, u in flat:
                if (i, u) != (0, 0) and u:
                    G.make_lo(dve, n, u)
                if i in (2, 3) and u == 2:
                    g = i - 2
                    sqd.wait(dve, g, 1)
                    if g == 0:
                        dve.tensor_reduce(ss[:, TT:], sq[:, :, LAT:], AX.X, ALU.add)
                    dve.tensor_reduce(ss[:, 0:TT], sq[:, :, 0:LAT], AX.X, ALU.add).then_inc(sums.sem, 1)
                    rst.wait(dve, g, 1)
                    dve.wait_ge(loads.sem, 16 * n_loads)
                    for t in range(TT):
                        x = raw[:, t, 0:LAT]
                        if g == 0:
                            op = dve.scalar_tensor_tensor(x, x, rstd[:, t:t + 1], S.g_ckv[:], ALU.mult, ALU.mult)
                        else:
                            op = dve.tensor_scalar(x, x, rstd[:, t:t + 1], None, ALU.mult)
                    op.then_inc(normed.sem, 1)
                if i == 2 and u == 3:
                    for t in range(TT):
                        x = raw[:, t, LAT:]
                        op = dve.scalar_tensor_tensor(x, x, rstd[:, TT + t:TT + t + 1], S.gkr[:], ALU.mult, ALU.mult)
                    op.then_inc(scaled_kr.sem, 1)
                    dve.wait_ge(scaled_kr.sem, 1)
                    rotate(dve, kr[:, :, :], raw[:, :, LAT:], S.cos[:, 0, :, :], S.sin[:, 0, :, :],
                           [rt[:, q, :, :] for q in range(4)], lambda e: e.wait_ge(prods.sem, 1), prods).then_inc(kr_done.sem, 1)
                if i == 2 and u == 4:
                    dve.wait_ge(past_hi.sem, 1)
                    dve.tensor_tensor(S.pc[1][:], pc[:], S.pc[0][:].bitcast(F32), ALU.subtract)
                    dve.tensor_tensor(S.kr[1][:, SEQ:SEQ + PAST], pkr[:], S.kr[0][:, SEQ:SEQ + PAST].bitcast(F32),
                                      ALU.subtract).then_inc(past_lo.sem, 1)
                if i == 2 and u == 6:
                    Tc.dve(dve)
                    dve.wait_ge(kr_hi.sem, 1)
                    dve.tensor_tensor(S.kr[1][:, 0:SEQ], c.bank[5][0:ROPE, 0:SEQ], S.kr[0][:, 0:SEQ].bitcast(F32), ALU.subtract)
                    dve.tensor_tensor(S.kr[1][:, SEQ + PAST:], c.bank[6][0:ROPE, 0:NEW], S.kr[0][:, SEQ + PAST:].bitcast(F32),
                                      ALU.subtract).then_inc(kr_lo.sem, 1)
                if i == 3 and u == 6:
                    Tq.dve(dve)
                if u == U - 1:
                    if i + 1 < len(order):
                        order[i + 1][0].make_lo(dve, order[i + 1][1], 0)
                    if i <= 2:
                        a, w = (i * 288, 288) if i < 2 else (0, LAT)
                        took_lo.wait(dve, i, 1)
                        x = raw[0:NEW, SM, a:a + w]
                        dve.tensor_tensor(x, c.bank[SM][0:NEW, 0:w], x, ALU.add).then_inc(took_smp.sem, 1)
                    else:
                        g = i - 3
                        for t in range(NT):
                            th.wait(dve, g, t + 1)
                            y = gate[:, t, :]
                            dve.scalar_tensor_tensor(y, y, 1.0, c.bank[t][:, :], ALU.add,
                                                     ALU.mult).then_inc(gated.sem, 1)
                        g_lo.wait(dve, g, 1)
                        dve.tensor_tensor(lat_lo[:], c.bank[SM][0:NEW, :], lat_lo[:], ALU.add).then_inc(g_sum.sem, 1)
                        th.wait(dve, g, TT)
                        y = gate[0:NEW, SM, :]
                        dve.scalar_tensor_tensor(y, y, 1.0, lat_lo[:], ALU.add,
                                                 ALU.mult).then_inc(gated.sem, 1)

        @block.tensor
        def _(pe):
            for i, G, n, u in flat:
                G.w_lo.wait(pe, n, u + 1)
                for t in range(TT):
                    if u == 0 and i:
                        if i <= 3:
                            took.wait(pe, i - 1, t + 1) if t < SM else took_smp.wait(pe, i - 1, 1)
                        else:
                            gated.wait(pe, i - 4, t + 1)
                    G.multiply(pe, n, u, t)
                if i == 2 and u == 5:
                    pe.wait_ge(normed.sem, 1)
                    Tc.pe(pe)
                    pe.wait_ge(Tc.lo_out.sem, len(Tc.jobs()))
                    pe.wait_ge(kr_done.sem, 1)
                    for t in range(NT):
                        op = pe.transpose(c.bank[5][0:ROPE, t * P:(t + 1) * P], kr[:, t, :], K.ident[:, :])
                    op.then_inc(kr_t.sem, 1)
                    pe.transpose(c.bank[6][0:ROPE, 0:NEW], kr[0:NEW, SM, :], K.ident[0:NEW, 0:NEW]).then_inc(kr_t.sem, 1)
                if i == 3 and u == 5:
                    pe.wait_ge(normed.sem, 2)
                    pe.wait_ge(kr_lo.sem, 1)
                    Tq.pe(pe)


def block_e(c, K, S):
    nc, d = c.nc, c.dram
    place = c.packer(c.X)
    W2 = 2 * BR
    N = HEADS // 2
    G = Gemm(c, "e", d["w_uq"], N, 2, 2, W2, 2, S.ql, K.g_qa, place)
    raw, sq, q = (place(f"e_{n}", [P, 2, TT, BR]) for n in ("raw", "sq", "q"))
    rt = place("e_rt", [P, 4, 2, TT, ROPE // 2])
    M = 2 * TT
    ss, rstd, half = place("e_ss", [P, 2 * M]), place("e_rstd", [P, 2 * M]), place("e_half", [P, 2 * M])
    assert place.cur[0] <= c.Y
    s = c.sem
    init, took, took_lo, took_smp = s("e_init"), s("e_took", NT), s("e_took_lo"), s("e_took_smp")
    sqd, sums, var, rst = s("e_sqd"), s("e_sums"), s("e_var", 2), s("e_rst")
    sc, gr, prods, done, out = s("e_scaled", 2), s("e_gained"), s("e_prods"), s("e_turned"), s("e_out", 2, 16, credit=1)
    U = 2
    wide = lambda x, n: x.rearrange("p (m o) -> p m o", o=1).broadcast_to([P, M, n])

    with nc.Block() as block:
        @block.sync
        def _(sp):
            def body(h, last, first=False):
                for u in range(U):
                    if not last:
                        G.load(sp, h + 1, u)
                    if u == 1 and not first:
                        store(sp, h - 1)
            def store(sp, g):
                done.wait(sp, g, 1)
                for j in range(2):
                    sp.dma_start(d["queries"][2 * g + j], q[:, j, :, :]).then_inc(out.sem, 16)
            for u in range(U):
                G.load(sp, 0, u)
            body(0, False, True)
            with sp.Fori(1, N - 1) as h:
                body(h, False)
            body(N - 1, True)
            store(sp, N - 1)
            out.wait(sp, N - 1, 2)

        @block.gpsimd
        def _(pool):
            pool.memset(raw[:, :, SM, :], 0.0).then_inc(init.sem, 1)
            pool.memset(half[:], -0.5).then_inc(init.sem, 1)
            pool.tensor_scalar(S.gqr[:], S.gqr[:], MLA_SCALE, None, ALU.mult).then_inc(init.sem, 1)
            pool.tensor_scalar(S.gkn[:], S.gkn[:], MLA_SCALE, None, ALU.mult).then_inc(init.sem, 1)
            pool.wait_ge(init.sem, 4)
            pool.tensor_tensor(S.gkn[:], S.gkn[:], S.gqn[:], ALU.mult).then_inc(init.sem, 1)
            pool.wait_ge(init.sem, 5)

            def body(g, last):
                rst.wait(pool, g, 0)
                var.wait(pool, g, 2)
                pool.tensor_tensor(rstd[:], ss[:], half[:], ALU.pow).then_inc(rst.sem, 1)
            steps(pool, N, body)

        @block.scalar
        def _(act_):
            act_.wait_ge(init.sem, 5)

            def squares(g):
                took_smp.wait(act_, g, 1)
                took.wait(act_, g, NT)
                act_.activation(sq[:], raw[:], ACT.Square).then_inc(sqd.sem, 1)

            def body(h, last, first=False):
                if not first:
                    squares(h - 1)
                G.make_hi(act_, h, 1)
                if not last:
                    G.make_hi(act_, h + 1, 0)
                if not first:
                    sc.wait(act_, h - 1, 2)
                    done.wait(act_, h - 1, 1)
                for t in range(NT):
                    G.done.wait(act_, h, t + 1)
                    act_.activation(raw[:, :, t, :], c.bank[t][:, 0:W2].rearrange("p (h d) -> p h d", h=2),
                                    ACT.Copy).then_inc(took.sem, 1)
                G.used.wait(act_, h, U)
                act_.activation(raw[0:NEW, :, SM, :], c.bank[SM][NEW:2 * NEW, 0:W2].rearrange("p (h d) -> p h d", h=2),
                                ACT.Copy).then_inc(took_lo.sem, 1)
            G.make_hi(act_, 0, 0)
            body(0, False, True)
            with act_.Fori(1, N - 1) as h:
                body(h, False)
            body(N - 1, True)
            squares(N - 1)

        @block.vector
        def _(dve):
            dve.wait_ge(init.sem, 5)
            out.grant(dve)

            def sum_up(g):
                sqd.wait(dve, g, 1)
                v = sq[:].rearrange("p h t d -> p (h t) d")
                dve.tensor_reduce(ss[:, 0:M], v[:, :, 0:HD], AX.X, ALU.add)
                dve.tensor_reduce(ss[:, M:], v[:, :, HD:], AX.X, ALU.add).then_inc(sums.sem, 1)
                sums.wait(dve, g, 1)
                dve.tensor_scalar(ss[:, 0:M], ss[:, 0:M], 1.0 / HD, EPS, ALU.mult, ALU.add).then_inc(var.sem, 1)
                dve.tensor_scalar(ss[:, M:], ss[:, M:], 1.0 / ROPE, EPS, ALU.mult, ALU.add).then_inc(var.sem, 1)

            def finish(g):
                rst.wait(dve, g, 1)
                out.wait(dve, g - 1, 2)
                v, o = raw[:].rearrange("p h t d -> p (h t) d"), q[:].rearrange("p h t d -> p (h t) d")
                x = v[:, :, HD:]
                dve.tensor_tensor(x, x, wide(rstd[:, M:], ROPE), ALU.mult).then_inc(sc.sem, 1)
                dve.tensor_tensor(o[:, :, 0:HD], v[:, :, 0:HD], wide(rstd[:, 0:M], HD), ALU.mult).then_inc(sc.sem, 1)
                sc.wait(dve, g, 1)
                dve.tensor_tensor(x, x, S.gqr[:].rearrange("p (o d) -> p o d", o=1).broadcast_to([P, M, ROPE]),
                                  ALU.mult).then_inc(gr.sem, 1)
                gr.wait(dve, g, 1)
                flat = lambda y: y.rearrange("p h t d -> p (h t) d")
                rotate(dve, o[:, :, HD:], x, flat(S.cos[:]), flat(S.sin[:]), [flat(rt[:, i, :, :, :]) for i in range(4)],
                       lambda e: prods.wait(e, g, 1), prods).then_inc(done.sem, 1)

            def body(h, last, first=False):
                G.make_lo(dve, h, 1)
                if not first:
                    sum_up(h - 1)
                if not last:
                    G.make_lo(dve, h + 1, 0)
                if not first:
                    finish(h - 1)
                take(h)

            def take(h):
                took_lo.wait(dve, h, 1)
                x = raw[0:NEW, :, SM, :]
                dve.tensor_tensor(x, c.bank[SM][0:NEW, 0:W2].rearrange("p (h d) -> p h d", h=2), x, ALU.add).then_inc(took_smp.sem, 1)
            G.make_lo(dve, 0, 0)
            body(0, False, True)
            with dve.Fori(1, N - 1) as h:
                body(h, False)
            body(N - 1, True)
            sum_up(N - 1)
            finish(N - 1)

        @block.tensor
        def _(pe):
            def body(h, last, first=False):
                for u in range(U):
                    G.w_lo.wait(pe, h, u + 1)
                    for t in range(TT):
                        if u == 0 and not first:
                            took.wait(pe, h - 1, t + 1) if t < SM else took_smp.wait(pe, h - 1, 1)
                        G.multiply(pe, h, u, t)
            body(0, False, True)
            with pe.Fori(1, N - 1) as h:
                body(h, False)
            body(N - 1, True)


class MlaHead:

    ORDER = ["qn", "T0", "qr", "T1", "new", "T2", "kp", "T3", "ka", "T4", "s3", "T5", "s2", "T6", "s1", "T7", "s0", "T8",
             "sa", "sb", "p3", "p2", "p1", "p0", "pn", "o", "on", "g", "gn"]
    JOBS = [n for n in ORDER if n[0] != "T"]
    SPLITS = ["qn", "qr", "new", "kp", "ka", "p3", "p2", "p1", "p0", "pn"]
    KV = 2 * NT + 1

    def __init__(self, c, K, S, wplace, xplace):
        self.c, self.K, self.S = c, K, S
        place = wplace
        self.G = Gemm(c, "f", c.dram["w_ukv"], HEADS, 1, LT, 2 * HD, 1, (None, None, None), None, place, slots=1)
        self.vhi, self.vlo = place("f_vhi", [P, self.KV, HD], F32R), place("f_vlo", [P, self.KV, HD], F32R)
        self.k = place("f_k", [P, self.KV, HD])
        self.sq = place("f_sq", [P, self.KV, HD])
        self.kv_new = place("f_kv_new", [NEW, 2 * HD])
        self.ss, self.rstd, self.half = (place(f"f_{n}", [P, self.KV]) for n in ("ss", "rstd", "half"))
        self.q = place("f_q", [P, TT, BR])
        self.gate = place("f_gate", [P, TT, HD])
        self.qn = (place("f_qnhi", [HD, SEQ], F32R), place("f_qnlo", [HD, SEQ], F32R))
        self.qr = (place("f_qrhi", [ROPE, SEQ], F32R), place("f_qrlo", [ROPE, SEQ], F32R))
        self.nqn = (place("f_nqnhi", [HD, NEW], F32R), place("f_nqnlo", [HD, NEW], F32R))
        self.nqr = (place("f_nqrhi", [ROPE, NEW], F32R), place("f_nqrlo", [ROPE, NEW], F32R))
        place = xplace
        self.kp = (place("f_kphi", [HD, SEQ], F32R), place("f_kplo", [HD, SEQ], F32R))
        self.kn = (place("f_knhi", [HD, SAMP], F32R), place("f_knlo", [HD, SAMP], F32R))
        self.p = [place(f"f_p{i}", [P, (i + 1) * P]) for i in range(NT)]
        self.pn = place("f_pn", [NEW, SAMP])
        self.first = [0, P, 2 * P, 2 * P]
        self.pt = [(place(f"f_pt{j}hi", [P, SEQ - f], F32R), place(f"f_pt{j}lo", [P, SEQ - f], F32R))
                   for j, f in enumerate(self.first)]
        self.ptn = (place("f_ptnhi", [P, 512], F32R), place("f_ptnlo", [P, 512], F32R))
        self.o = place("f_o", [HD, SEQ + NEW])
        self.nm, self.rs, self.ri = place("f_nm", [P, TT]), place("f_rs", [P, TT]), place("f_ri", [P, TT])
        self.m2, self.r2 = place("f_m2", [NEW, 2]), place("f_r2", [NEW, 2])
        s = c.sem
        self.use = [sum(1 for i in range(len(self.JOBS)) if i % 3 == b) for b in range(3)]
        self.ready = [s(f"f_ready{b}", n) for b, n in enumerate(self.use)]
        self.free = [s(f"f_free{b}", n, credit=1) for b, n in enumerate(self.use)]
        self.kv_done = s("f_kv_done", NT)
        self.squared = s("f_squared")
        self.new_lo, self.new_sum = s("f_new_lo"), s("f_new_sum")
        self.sums, self.var, self.rst = s("f_sums"), s("f_var"), s("f_rst")
        self.keys = s("f_keys")
        self.v_hi = s("f_v_hi", TT)
        self.v_lo = s("f_v_lo", TT)
        self.hi_done = s("f_hi_done", len(self.SPLITS))
        self.new_max, self.negmax = s("f_new_max", 2), s("f_negmax", TT)
        self.inv, self.scaled = s("f_inv", 2), s("f_scaled")
        self.q_in, self.g_in = s("f_q_in", 1, 16), s("f_g_in", 2, 16)
        self.zero = s("f_zero")

    def job(self, name):
        i = self.JOBS.index(name)
        return i % 3, i // 3 + 1

    def bank(self, name):
        return self.c.bank[5 + self.job(name)[0]]

    def wait_ready(self, eng, g, name):
        b, k = self.job(name)
        self.ready[b].wait(eng, g, k)

    FROM = {**{f"s{i}": ("qn", "qr", "kp") for i in range(4)}, "sa": ("new", "ka"), "sb": ("new", "ka"),
            **{f"p{j}": (f"s{j}",) for j in range(4)}, "pn": ("sb",), "o": ("p0", "p1", "p2", "p3"), "on": ("pn",)}

    def wait_operands(self, eng, g, name):
        own, k = self.job(name)
        count = {own: k - 1}
        for b, k in map(self.job, self.FROM.get(name, ())):
            count[b] = max(count.get(b, k), k)
        for b, k in count.items():
            self.free[b].wait(eng, g, k)

    def wait_out_of(self, eng, g, name):
        b, k = self.job(name)
        self.free[b].wait(eng, g, k)

    def end(self, op, name):
        op.then_inc(self.ready[self.job(name)[0]].sem, 1)

    def release(self, op, name):
        op.then_inc(self.free[self.job(name)[0]].sem, 1)

    def split_views(self, name):
        b = self.bank(name)
        full = {"qn": (self.qn, HD), "qr": (self.qr, ROPE), "kp": (self.kp, HD)}
        if name in full:
            (hi, lo), n = full[name]
            return [(b[0:n, :], hi[:], lo[:])]
        if name == "ka":
            return [(b[:, :], self.kn[0][:, 0:PAST], self.kn[1][:, 0:PAST])]
        if name == "new":
            return [(b[:, 0:NEW], self.nqn[0][:], self.nqn[1][:]),
                    (b[:, NEW:2 * NEW], self.kn[0][:, PAST:], self.kn[1][:, PAST:]),
                    (b[0:ROPE, 2 * NEW:3 * NEW], self.nqr[0][:], self.nqr[1][:])]
        if name == "pn":
            hi, lo = self.ptn
            n = NT * NEW
            return [(b[:, 0:n], hi[:, 0:n], lo[:, 0:n]),
                    (b[0:NEW, n:n + NEW], hi[0:NEW, n:n + NEW], lo[0:NEW, n:n + NEW])]
        j = int(name[1])
        hi, lo = self.pt[j]
        a = j * P - self.first[j]
        return [(b[:, j * P:], hi[:, a:], lo[:, a:])]

    def pe_tile(self, eng, h, tau):
        S, G = self.S, self.G
        whi, wlo = G.whi[0], G.wlo[0]
        bank = self.c.bank[tau // 2]
        if tau == 0:
            G.w_lo.wait(eng, h, 1)
        if tau % 2 == 0:
            self.v_lo.wait(eng, h, tau // 2 + 1 - TT)
        out = bank[:, (tau % 2) * 256:(tau % 2) * 256 + 256]
        for k in range(LT):
            if tau < 2 * NT:
                hi, lo = (S.c[0], S.c[1]) if tau < NT else S.pc
                a = slice((tau % NT) * P, (tau % NT + 1) * P)
                pairs = three(hi[:, k, a], lo[:, k, a], whi[:, k, :], wlo[:, k, :])
            else:
                pairs = [(S.c[2][:, k, :], whi[:, k, :]), (S.c[2][:, k, :], wlo[:, k, :])]
            for i, (x, w) in enumerate(pairs):
                op = eng.matmul(out, x, w, start=(k == 0 and i == 0), stop=(k == LT - 1 and i == len(pairs) - 1))
        if tau == 2 * NT:
            op.then_inc(G.used.sem, 1)
        elif tau % 2:
            op.then_inc(self.kv_done.sem, 1)

    def pe_job(self, eng, g, name):
        K, S, b = self.K, self.S, self.bank(name)
        self.wait_operands(eng, g, name)
        I = K.ident
        if name in ("qn", "qr"):
            if name == "qn":
                self.q_in.wait(eng, g, 1)
            n, a = (HD, 0) if name == "qn" else (ROPE, HD)
            for t in range(NT):
                op = turn(eng, b[0:n, t * P:(t + 1) * P], self.q[:, t, a:a + n], I[:, :], name == "qr" and t == 0)
        elif name == "new":
            self.keys.wait(eng, g, 1)
            turn(eng, b[:, 0:NEW], self.q[0:NEW, SM, 0:HD], I[0:NEW, 0:NEW], True)
            eng.transpose(b[:, NEW:2 * NEW], self.k[0:NEW, 2 * NT, :], I[0:NEW, 0:NEW])
            op = eng.transpose(b[0:ROPE, 2 * NEW:3 * NEW], self.q[0:NEW, SM, HD:BR], I[0:NEW, 0:NEW])
        elif name in ("kp", "ka"):
            t0 = 0 if name == "kp" else NT
            for t in range(NT):
                op = eng.transpose(b[:, t * P:(t + 1) * P], self.k[:, t0 + t, :], I[:, :])
        elif name in ("s0", "s1", "s2", "s3"):
            i = int(name[1])
            n = max(i + 1, 2) * P
            q = slice(i * P, (i + 1) * P)
            for m, (x, y) in enumerate(three(*self.qn, *self.kp)):
                eng.matmul(b[:, 0:n], x[:, q], y[:, 0:n], start=(m == 0), stop=False)
            eng.matmul(b[:, q], K.ident_b[:, :], K.mask_mla_b[:, :], start=False, stop=False, skip_group_check=True)
            for m, (x, y) in enumerate(three(*self.qr, *S.kr)):
                op = eng.matmul(b[:, 0:n], x[:, q], y[:, 0:n], start=False, stop=(m == 2))
        elif name in ("sa", "sb"):
            i = ("sa", "sb").index(name)
            for m, (x, y) in enumerate(three(*self.nqn, *self.kn)):
                eng.matmul(b[0:NEW, 0:288], x[:, :], y[:, i * 288:(i + 1) * 288], start=(m == 0), stop=False)
            for m, (x, y) in enumerate(three(*self.nqr, *S.kr)):
                op = eng.matmul(b[0:NEW, 0:288], x[:, :], y[:, SEQ + i * 288:SEQ + (i + 1) * 288], start=False, stop=(m == 2))
        elif name == "pn":
            for t in range(TT):
                n = rows(t)
                op = turn(eng, b[0:n, t * NEW:(t + 1) * NEW], self.pn[:, t * P:t * P + n], I[0:NEW, 0:NEW], t == 0)
        elif name[0] == "p":
            j = int(name[1])
            for i in range(j, NT):
                op = eng.transpose(b[:, i * P:(i + 1) * P], self.p[i][:, j * P:(j + 1) * P], I[:, :])
        elif name == "o":
            self.v_lo.wait(eng, g, TT)
            for j in range(NT):
                f = self.first[j]
                for m, (x, y) in enumerate(three(self.vhi, self.vlo, *self.pt[j])):
                    op = eng.matmul(b[:, f:], x[:, j, :], y[:, :], start=(j == 0 and m == 0), stop=(j == NT - 1 and m == 2))
        elif name == "on":
            for t in range(TT):
                n = rows(t)
                for m, (x, y) in enumerate(three(self.vhi, self.vlo, *self.ptn)):
                    op = eng.matmul(b[:, 0:256], x[0:n, NT + t, :], y[0:n, t * NEW:t * NEW + 256],
                                    start=(t == 0 and m == 0), stop=(t == SM and m == 2))
        elif name == "g":
            self.scaled.wait(eng, g, 1)
            for t in range(NT):
                op = eng.transpose(b[:, t * P:(t + 1) * P], self.gate[:, t, :], I[:, :])
        elif name == "gn":
            op = turn(eng, b[:, 0:NEW], self.gate[0:NEW, SM, :], I[0:NEW, 0:NEW], True)
        self.end(op, name)

    def act_job(self, eng, g, name):
        if name == "sa":
            return
        if name == "sb":
            self.act_exp(eng, g, "sa")
            self.act_exp(eng, g, "sb")
        elif name in self.SPLITS:
            self.wait_ready(eng, g, name)
            for src, hi, lo in self.split_views(name):
                op = eng.activation(hi, src, ACT.Copy)
            op.then_inc(self.hi_done.sem, 1)
        elif name[0] == "s":
            self.act_exp(eng, g, name)
        elif name in ("o", "on"):
            self.wait_ready(eng, g, name)
            a, n = (0, SEQ) if name == "o" else (SEQ, NEW)
            self.release(eng.activation(self.o[:, a:a + n], self.bank(name)[:, 0:n], ACT.Copy), name)

    def act_exp(self, eng, g, name):
        b = self.bank(name)
        if name in ("sa", "sb"):
            i = ("sa", "sb").index(name)
            self.negmax.wait(eng, g, TT)
            op = eng.activation(self.pn[:, i * 288:(i + 1) * 288], b[0:NEW, 0:288], ACT.Exp, bias=self.nm[0:NEW, SM:TT],
                                accum_out=self.r2[:, i:i + 1])
        else:
            i = int(name[1])
            self.negmax.wait(eng, g, NT - i)
            op = eng.activation(self.p[i][:], b[:, 0:(i + 1) * P], ACT.Exp, bias=self.nm[:, i:i + 1],
                                accum_out=self.rs[:, i:i + 1])
        self.release(op, name)

    def act_keys(self, eng, h, b):
        if b < NT:
            self.kv_done.wait(eng, h, b + 1)
            src = self.c.bank[b][:, :].rearrange("p (t n) -> p t n", t=2)[:, :, 0:HD]
            eng.activation(self.sq[:, 2 * b:2 * b + 2, :], src, ACT.Square)
        else:
            self.G.used.wait(eng, h, 1)
            eng.activation(self.kv_new[:], self.c.bank[SM][NEW:2 * NEW, 0:256], ACT.Copy).then_inc(self.new_lo.sem, 1)
            self.new_sum.wait(eng, h, 1)
            eng.activation(self.sq[0:NEW, 2 * NT, :], self.kv_new[:, 0:HD], ACT.Square).then_inc(self.squared.sem, 1)

    def act_values(self, eng, h, b):
        if b < NT:
            src = self.c.bank[b][:, :].rearrange("p (t n) -> p t n", t=2)[:, :, HD:]
            op = eng.activation(self.vhi[:, 2 * b:2 * b + 2, :], src, ACT.Copy)
        else:
            op = eng.activation(self.vhi[0:NEW, 2 * NT, :], self.kv_new[:, HD:], ACT.Copy)
        op.then_inc(self.v_hi.sem, 1)

    def dve_job(self, eng, g, name, dst):
        b = self.bank(name)
        if name in self.SPLITS:
            self.hi_done.wait(eng, g, self.SPLITS.index(name) + 1)
            for src, hi, lo in self.split_views(name):
                op = eng.tensor_tensor(lo, src, hi.bitcast(F32), ALU.subtract)
            self.release(op, name)
        elif name in ("sa", "sb"):
            self.wait_ready(eng, g, name)
            i = ("sa", "sb").index(name)
            eng.tensor_reduce(self.m2[:, i:i + 1], b[0:NEW, 0:288], AX.X, ALU.max).then_inc(self.new_max.sem, 1)
            if i:
                self.new_max.wait(eng, g, 2)
                eng.tensor_reduce(self.nm[0:NEW, SM:TT], self.m2[:], AX.X, ALU.max, negate=True).then_inc(self.negmax.sem, 1)
        elif name[0] == "s":
            self.wait_ready(eng, g, name)
            i = int(name[1])
            eng.tensor_reduce(self.nm[:, i:i + 1], b[:, 0:(i + 1) * P], AX.X, ALU.max, negate=True).then_inc(self.negmax.sem, 1)
        elif name == "o":
            self.wait_out_of(eng, g, "sb")
            eng.tensor_tensor(self.rs[0:NEW, SM:TT], self.r2[:, 0:1], self.r2[:, 1:2], ALU.add).then_inc(self.inv.sem, 1)
            self.inv.wait(eng, g, 1)
            eng.reciprocal(self.ri[:], self.rs[:]).then_inc(self.inv.sem, 1)
            self.inv.wait(eng, g, 2)
            self.g_in.wait(eng, g, 2)
            for t in range(TT):
                y = self.gate[0:rows(t), t, :]
                op = eng.tensor_scalar(y, y, self.ri[0:rows(t), t:t + 1], 0.5, ALU.mult, ALU.mult)
            op.then_inc(self.scaled.sem, 1)
        elif name in ("g", "gn"):
            self.wait_ready(eng, g, name)
            self.wait_out_of(eng, g, "o" if name == "g" else "on")
            a, n = (0, SEQ) if name == "g" else (SEQ, NEW)
            op = eng.tensor_tensor(dst[:, g, a:a + n], b[:, 0:n], self.o[:, a:a + n], ALU.mult)
            self.release(op, name)

    def dve_new(self, eng, h):
        self.new_lo.wait(eng, h, 1)
        eng.tensor_tensor(self.kv_new[:], self.c.bank[SM][0:NEW, 0:256], self.kv_new[:], ALU.add).then_inc(self.new_sum.sem, 1)

    def dve_sums(self, eng, h):
        self.squared.wait(eng, h, 1)
        eng.tensor_reduce(self.ss[:, 0:2 * NT], self.sq[:, 0:2 * NT, :], AX.X, ALU.add)
        eng.tensor_reduce(self.ss[0:NEW, 2 * NT:], self.sq[0:NEW, 2 * NT:, :], AX.X, ALU.add).then_inc(self.sums.sem, 1)
        self.sums.wait(eng, h, 1)
        eng.tensor_scalar(self.ss[:], self.ss[:], 1.0 / HD, EPS, ALU.mult, ALU.add).then_inc(self.var.sem, 1)

    def dve_keys(self, eng, h):
        self.rst.wait(eng, h, 1)
        for t in range(self.KV):
            n = P if t < 2 * NT else NEW
            src = self.c.bank[t // 2][:, (t % 2) * 256:(t % 2) * 256 + HD] if t < 2 * NT else self.kv_new[:, 0:HD]
            op = eng.scalar_tensor_tensor(self.k[0:n, t, :], src, self.rstd[0:n, t:t + 1], self.S.gkn[0:n, :], ALU.mult, ALU.mult)
        op.then_inc(self.keys.sem, 1)

    def dve_values(self, eng, h, b):
        self.v_hi.wait(eng, h, b + 1)
        if b < NT:
            src = self.c.bank[b][:, :].rearrange("p (t n) -> p t n", t=2)[:, :, HD:]
            hi, lo = self.vhi[:, 2 * b:2 * b + 2, :], self.vlo[:, 2 * b:2 * b + 2, :]
        else:
            src, hi, lo = self.kv_new[:, HD:], self.vhi[0:NEW, 2 * NT, :], self.vlo[0:NEW, 2 * NT, :]
        eng.tensor_tensor(lo, src, hi.bitcast(F32), ALU.subtract).then_inc(self.v_lo.sem, 1)


def block_f(c, K, S):
    nc, d = c.nc, c.dram
    o_all = c.at("o_mla", [HD, HEADS, SEQ + NEW], F32, c.X)
    wplace, xplace = c.packer(S.f_base), c.packer(c.X + 36864)
    H = MlaHead(c, K, S, wplace, xplace)
    assert wplace.cur[0] <= K.base and xplace.cur[0] <= c.Y, (wplace.cur[0], K.base, xplace.cur[0], c.Y)
    G = H.G
    started = lambda g: not isinstance(g, int) or g > 0

    with nc.Block() as block:
        @block.sync
        def _(sp):
            def load_head(g):
                if started(g):
                    H.wait_ready(sp, g - 1, "new")
                sp.dma_start(H.q[:], d["queries"][g]).then_inc(H.q_in.sem, 16)
                if started(g):
                    H.wait_ready(sp, g - 1, "gn")
                for q, t in ((P, slice(0, NT)), (NEW, slice(SM, TT))):
                    sp.dma_start(H.gate[0:q, t, :], d["gates"][g, 0:q, t, :]).then_inc(H.g_in.sem, 16)

            def body(h, last):
                if not last:
                    G.load(sp, h + 1, 0)
                load_head(h)
            G.load(sp, 0, 0)
            steps(sp, HEADS, body)

        @block.gpsimd
        def _(pool):
            pool.memset(H.ss[:], 1.0).then_inc(H.zero.sem, 1)
            pool.memset(H.rs[:], 1.0).then_inc(H.zero.sem, 1)
            pool.memset(H.half[:], -0.5).then_inc(H.zero.sem, 1)
            for x in (*H.ptn, *H.pt[NT - 1]):
                pool.memset(x[:].bitcast(F32), 0.0).then_inc(H.zero.sem, 1)
            pool.wait_ge(H.zero.sem, 7)

            def body(h, last):
                H.rst.wait(pool, h, 0)
                H.var.wait(pool, h, 1)
                pool.tensor_tensor(H.rstd[:], H.ss[:], H.half[:], ALU.pow).then_inc(H.rst.sem, 1)
            steps(pool, HEADS, body)

        @block.scalar
        def _(act_):
            act_.wait_ge(H.zero.sem, 7)

            def body(h, last, g):
                for name in H.ORDER:
                    if name[0] != "T":
                        if g is not None:
                            H.act_job(act_, g, name)
                    elif h is not None:
                        tau = int(name[1])
                        if tau % 2 or tau == 2 * NT:
                            H.act_keys(act_, h, tau // 2)
                    if name == "p2" and h is not None and not last:
                        G.make_hi(act_, h + 1, 0)
                    if name == "on" and h is not None:
                        H.keys.wait(act_, h, 1)
                        for b in range(TT):
                            H.act_values(act_, h, b)
            G.make_hi(act_, 0, 0)
            body(0, False, None)
            with act_.Fori(1, HEADS - 1) as h:
                body(h, False, h - 1)
            body(HEADS - 1, True, HEADS - 2)
            body(None, True, HEADS - 1)

        @block.vector
        def _(dve):
            dve.wait_ge(H.zero.sem, 7)
            for bank_free in H.free:
                bank_free.grant(dve)

            def body(h, last, g):
                for name in H.ORDER:
                    if name[0] != "T":
                        if g is not None:
                            H.dve_job(dve, g, name, o_all)
                    elif name == "T8" and h is not None:
                        H.dve_new(dve, h)
                    if h is not None:
                        if name == "sb":
                            H.dve_sums(dve, h)
                        if name == "p3":
                            H.dve_keys(dve, h)
                        if name == "p2" and not last:
                            G.make_lo(dve, h + 1, 0)
                        if name == "on":
                            for b in range(TT):
                                H.dve_values(dve, h, b)
            G.make_lo(dve, 0, 0)
            body(0, False, None)
            with dve.Fori(1, HEADS - 1) as h:
                body(h, False, h - 1)
            body(HEADS - 1, True, HEADS - 2)
            body(None, True, HEADS - 1)

        @block.tensor
        def _(pe):
            pe.wait_ge(H.zero.sem, 7)

            def body(h, last, g):
                for name in H.ORDER:
                    if name[0] != "T":
                        if g is not None:
                            H.pe_job(pe, g, name)
                    elif h is not None:
                        H.pe_tile(pe, h, int(name[1]))
            body(0, False, None)
            with pe.Fori(1, HEADS - 1) as h:
                body(h, False, h - 1)
            body(HEADS - 1, True, HEADS - 2)
            body(None, True, HEADS - 1)
    return o_all


def block_g(c, K, o):
    place = c.packer(c.X + 36864)
    act = (place("g_ohi", [P, KT, SEQ], F32R), place("g_olo", [P, KT, SEQ], F32R), place("g_osmp", [P, KT, 2 * NEW], F32R))
    out_proj(c, K, "g", c.dram["w_out2"], o, act, c.dram["x1"], place.cur[0], FinishG)


def program(nc, dram):
    with ExitStack() as ctx:
        c = Core(nc, ctx, dram)
        K = Consts(c)
        block_a(c, K)
        block_b(c, K)
        c.recycle()
        block_c(c, K)
        S = Shared(c)
        block_d(c, K, S)
        block_e(c, K, S)
        c.recycle()
        block_g(c, K, block_f(c, K, S))


BACC = {"dynamic_dma_scratch_size": 1024}


def unit_layout(w, cols, units, kk):
    k, n = w.shape
    return w.reshape(units, kk, P, n // cols, cols).transpose(3, 0, 2, 1, 4)


def lay_out(a):
    g = {n: np.asarray(v) for n, v in a.items()}
    out = {}
    rows_ = np.zeros((TT * P, D_MODEL), np.float32)
    rows_[:SEQ], rows_[SEQ:SEQ + NEW] = g["x_prompt"][0], g["x_sample"][0]
    out["x"] = rows_.reshape(TT, P, D_MODEL).transpose(1, 0, 2)
    w = g["fox_w_in"][0]
    blocks = w[:, :4 * D_MODEL].reshape(D_MODEL, 4, HEADS, HD).transpose(0, 2, 1, 3).reshape(D_MODEL, HEADS * 4 * HD)
    out["w_fox"] = unit_layout(blocks, 512, KT // UK, UK)
    out["w_f"] = w[:, 4 * D_MODEL:].reshape(KT, P, HEADS).transpose(1, 0, 2)
    out["g_fox"] = g["fox_norm_g"][0].reshape(KT, P).T
    out["g_kv"] = g["kv_norm_g"].reshape(KT, P).T
    out["g_mla"] = g["mla_norm_g"][0].reshape(KT, P).T
    out["g_qa"] = g["mla_qa_norm_g"][0].reshape(LT, P).T
    out["b_f"] = g["fox_b_f"][0].reshape(HEADS, 1)
    out["g_q"] = np.broadcast_to(g["fox_q_norm_g"][0], (P, HD))
    out["g_k"] = np.broadcast_to(g["fox_k_norm_g"][0], (P, HD))
    out["cache_logf"] = g["cache_fox_logf"][0, 0].T
    out["cache_k"] = g["cache_fox_k"][0, 0].transpose(1, 2, 0)
    out["cache_v"] = g["cache_fox_v"][0, 0].reshape(NT, P, HEADS, HD).transpose(2, 1, 0, 3)
    out["w_out1"] = unit_layout(g["fox_w_out"][0], 512, KT // UK, UK)
    out["w_dkv"] = unit_layout(g["mla_w_dkv"], 288, KT // UK, UK)
    out["w_mla"] = unit_layout(g["mla_w_in"][0], 512, KT // UK, UK)
    out["w_uq"] = unit_layout(g["mla_w_uq"][0].reshape(LAT, HEADS * BR), 2 * BR, LT // UK, UK)
    for n, k in (("g_ckv", "mla_ckv_norm_g"), ("g_kr", "mla_krope_norm_g"), ("g_kn", "mla_knope_norm_g")):
        out[n] = np.broadcast_to(g[k], (P, g[k].shape[-1]))
    for n, k in (("g_qr", "mla_qrope_norm_g"), ("g_qn", "mla_qnope_norm_g")):
        out[n] = np.broadcast_to(g[k][0], (P, g[k].shape[-1]))
    out["w_ukv"] = unit_layout(g["mla_w_ukv"].reshape(LAT, HEADS * 2 * HD), 2 * HD, 1, LT)
    out["w_out2"] = unit_layout(g["mla_w_out"][0], 512, KT // UK, UK)
    out["cache_ckv"] = g["cache_mla_ckv"][0].T.reshape(LT, P, PAST).transpose(1, 0, 2)
    out["cache_kr"] = g["cache_mla_krope"][0].T
    pos = np.arange(TT * P, dtype=np.float32)
    pos[SEQ:] += PAST - SEQ
    inv = np.float32(THETA) ** (-np.arange(ROPE // 2, dtype=np.float32) / np.float32(ROPE // 2))
    ang = (pos[:, None] * inv[None, :]).astype(np.float32).reshape(TT, P, ROPE // 2).transpose(1, 0, 2)
    out["cos"], out["sin"] = (np.broadcast_to(f(ang)[:, None], (P, 2, TT, ROPE // 2)) for f in (np.cos, np.sin))
    r = np.arange(P)
    out["ident"] = np.eye(P, dtype=np.float32)
    out["mask_fox"] = np.where(r[None, :] > r[:, None], MASKED, 0.0).astype(np.float32)
    out["mask_mla"] = np.where(r[None, :] // CHUNK > r[:, None] // CHUNK, MASKED, 0.0).astype(np.float32)
    heads = np.arange(HEADS)
    neg, pos = np.zeros((P, HEADS), np.float32), np.zeros((P, HEADS), np.float32)
    neg[heads, heads] = neg[32 + heads, heads] = -1.0
    pos = np.zeros((P, HEADS), np.float32)
    pos[64 + heads, heads] = pos[96 + heads, heads] = 1.0
    out["nsel"], out["psel"] = neg, pos
    return {n: np.ascontiguousarray(v) for n, v in out.items()}


OUTS = {
    "out_logf": [P, TT, HEADS],
    "out_fk": [HEADS, P, TT, HD],
    "out_fv": [HEADS, P, TT, HD],
    "out_ckv": [P, TT, LAT],
    "out_kr": [P, TT, ROPE],
    "out_y": [P, TT, D_MODEL],
}


SCRATCH = {
    "x1": [P, TT, D_MODEL],
    "gates": [HEADS, P, TT, HD],
    "queries": [HEADS, P, TT, BR],
}


def tokens(x):
    flat = np.moveaxis(x, 0, 1).reshape((TT * P,) + x.shape[2:])
    return flat[:SEQ], flat[SEQ:SEQ + NEW]


def kernel(**inputs):
    from concourse import bacc
    from concourse.bass_utils import run_bass_kernel_spmd

    nc = bacc.Bacc("TRN2", target_bir_lowering=False, num_devices=1, **BACC)
    arrays = lay_out(inputs)
    dram = {n: nc.dram_tensor(n, list(v.shape), F32, kind="ExternalInput").ap() for n, v in arrays.items()}
    dram.update({n: nc.dram_tensor(n, s, F32, kind="ExternalOutput").ap() for n, s in OUTS.items()})
    dram.update({n: nc.dram_tensor(n, s, F32, kind="Internal").ap() for n, s in SCRATCH.items()})
    program(nc, dram)
    r = run_bass_kernel_spmd(nc, [arrays], core_ids=[0]).results[0]
    heads = lambda x: [h[None, None] for h in tokens(np.asarray(x).transpose(1, 2, 0, 3))]
    (y_p, y_s), (lf_p, lf_s), (c_p, c_s), (kr_p, kr_s) = (tokens(np.asarray(r[n])) for n in
                                                         ("out_y", "out_logf", "out_ckv", "out_kr"))
    (k_p, k_s), (v_p, v_s) = heads(r["out_fk"]), heads(r["out_fv"])
    return (y_p[None], y_s[None], k_p, v_p, lf_p[None, None], c_p[None], kr_p[None],
            k_s, v_s, lf_s[None, None], c_s[None], kr_s[None])
```

```python
from contextlib import ExitStack

import numpy as np

import concourse.bass as bass
from concourse import mybir

F32 = mybir.dt.float32
F32R = mybir.dt.float32r
BF16 = mybir.dt.bfloat16
ALU = mybir.AluOpType
ACT = mybir.ActivationFunctionType
AX = mybir.AxisListType

P = 128
D_MODEL, SEQ, NEW, PAST = 2048, 512, 64, 512
HEADS, HD = 16, 128
LAT, ROPE = 512, 64
CHUNK = 64
EPS = 1e-6
FOX_SCALE = float(HD) ** -0.5
MLA_SCALE = float(HD + ROPE) ** -0.5
THETA = 10000.0
MASKED = -1e30

NT = SEQ // P
TT = NT + 1
SM = NT
KT = D_MODEL // P
LT = LAT // P
UK = 2
RAW_FOX = 2
TIME = SEQ + PAST + NEW
SAMP = PAST + NEW
BR = HD + ROPE


class Sig:

    def __init__(self, sem, per=1, unit=1, credit=0):
        self.sem, self.per, self.unit, self.credit = sem, per, unit, credit

    def grant(self, eng):
        eng.sem_inc(self.sem, self.credit * self.unit)

    def wait(self, eng, step, k):
        v = (step * self.per + k + self.credit) * self.unit
        if not isinstance(v, int) or v > 0:
            eng.wait_ge(self.sem, v)


def rows(t):
    return P if t < SM else NEW


def turn(eng, out, x, ident, first):
    if first:
        return eng.matmul(out, x, ident, start=True, stop=True)
    return eng.transpose(out, x, ident)


def steps(eng, n, body):
    body(0, n == 1)
    if n > 2:
        with eng.Fori(1, n - 1) as i:
            body(i, False)
    if n > 1:
        body(n - 1, True)


class Core:

    def __init__(self, nc, ctx, dram):
        self.nc, self.ctx, self.dram = nc, ctx, dram
        self.base = (nc.sbuf_base + 63) // 64 * 64
        self.limit = nc.sbuf_usable_end
        self.X = self.base
        self.Y = self.X + 73728
        self.W = self.Y + 40960
        self.bank = [ctx.enter_context(nc.psum_tensor(f"bank{b}", [P, 512], F32)) for b in range(8)]
        self.used = []

    def at(self, name, shape, dt, offset):
        size = int(np.prod(shape[1:])) * (2 if dt == BF16 else 4)
        assert offset + size <= self.limit, (name, offset + size, self.limit)
        return self.nc.alloc_sbuf_tensor_at(name, list(shape), dt, offset=offset)

    def packer(self, offset):
        cur = [offset]

        def place(name, shape, dt=F32):
            t = self.at(name, shape, dt, cur[0])
            cur[0] += (int(np.prod(shape[1:])) * (2 if dt == BF16 else 4) + 63) // 64 * 64
            return t
        place.cur = cur
        return place

    def sem(self, name, per=1, unit=1, credit=0):
        handle = self.nc.alloc_semaphore(name)
        self.used.append(handle)
        return Sig(handle, per, unit, credit)

    def clear_old(self, eng, keep):
        nums = sorted(h.num for h in self.old if h is not keep.sem)
        starts = [n for n in nums if n - 1 not in nums]
        ends = [n + 1 for n in nums if n + 1 not in nums]
        for a, b in zip(starts, ends):
            eng.sem_clear(range(a, b))

    def release_old(self, keep):
        for h in self.old:
            if h is not keep.sem:
                self.nc.release_semaphore(h)


class Gemm:

    def __init__(self, c, tag, src, steps_, units, kk, n, raw, act, gain, place, slots=2):
        self.slots = slots
        self.c, self.src, self.steps, self.units, self.kk, self.n, self.raws = c, src, steps_, units, kk, n, raw
        self.hi, self.lo, self.smp = act
        self.gain = gain
        assert units % raw == 0 or raw >= units * steps_
        self.raw = [place(f"{tag}_raw{i}", [P, kk, n]) for i in range(raw)]
        self.whi = [place(f"{tag}_whi{i}", [P, kk, n], F32R) for i in range(slots)]
        self.wlo = [place(f"{tag}_wlo{i}", [P, kk, n], F32R) for i in range(slots)]
        self.arrived = [c.sem(f"{tag}_arrived{i}", units // raw, 16) for i in range(raw)]
        self.w_hi = c.sem(f"{tag}_w_hi", units)
        self.w_lo = c.sem(f"{tag}_w_lo", units)
        self.used = c.sem(f"{tag}_used", units)
        self.done = c.sem(f"{tag}_done", NT)

    def load(self, eng, h, u):
        self.w_lo.wait(eng, h, u - self.raws + 1)
        eng.dma_start(self.raw[u % self.raws][:], self.src[h, u]).then_inc(self.arrived[u % self.raws].sem, 16)

    def make_hi(self, eng, h, u):
        self.arrived[u % self.raws].wait(eng, h, u // self.raws + 1)
        self.used.wait(eng, h, u - self.slots + 1)
        raw, hi = self.raw[u % self.raws], self.whi[u % self.slots]
        if self.gain is None:
            op = eng.activation(hi[:], raw[:], ACT.Copy)
        else:
            for k in range(self.kk):
                K = u * self.kk + k
                op = eng.activation(hi[:, k, :], raw[:, k, :], ACT.Copy, scale=self.gain[:, K:K + 1])
        op.then_inc(self.w_hi.sem, 1)

    def make_lo(self, eng, h, u):
        self.w_hi.wait(eng, h, u + 1)
        raw, hi, lo = self.raw[u % self.raws], self.whi[u % self.slots], self.wlo[u % self.slots]
        hi32 = hi[:].bitcast(F32)
        if self.gain is None:
            op = eng.tensor_tensor(lo[:], raw[:], hi32, ALU.subtract)
        else:
            for k in range(self.kk):
                K = u * self.kk + k
                op = eng.scalar_tensor_tensor(lo[:, k, :], raw[:, k, :], self.gain[:, K:K + 1], hi32[:, k, :],
                                              ALU.mult, ALU.subtract)
        op.then_inc(self.w_lo.sem, 1)

    def multiply(self, eng, h, u, t):
        out = self.c.bank[t][:, 0:self.n]
        whi, wlo = self.whi[u % self.slots], self.wlo[u % self.slots]
        first, last = u == 0, u == self.units - 1
        for k in range(self.kk):
            K = u * self.kk + k
            if t < SM:
                a_hi, a_lo = self.hi[:, K, t * P:(t + 1) * P], self.lo[:, K, t * P:(t + 1) * P]
                pairs = [(a_hi, whi), (a_hi, wlo), (a_lo, whi)]
            else:
                pairs = [(self.smp[:, K, :], whi), (self.smp[:, K, :], wlo)]
            for i, (a, w) in enumerate(pairs):
                op = eng.matmul(out, a, w[:, k, :], start=(first and k == 0 and i == 0),
                                stop=(last and k == self.kk - 1 and i == len(pairs) - 1))
        if t == SM:
            op.then_inc(self.used.sem, 1)
        elif last:
            op.then_inc(self.done.sem, 1)


def three(hi_a, lo_a, hi_b, lo_b):
    return [(hi_a, hi_b), (hi_a, lo_b), (lo_a, hi_b)]


class Transposer:

    def __init__(self, c, tag, src, act, ident, kt, banks=(0, 1, 2, 3), smp_banks=(4, 5)):
        self.banks, self.smp_banks = banks, smp_banks
        self.c, self.src, self.ident, self.kt = c, src, ident, kt
        self.hi, self.lo, self.smp = act
        self.turned = c.sem(f"{tag}_turned")
        self.hi_out = c.sem(f"{tag}_hi_out")
        self.lo_out = c.sem(f"{tag}_lo_out")

    def jobs(self):
        out, last = [], {}
        for k in range(self.kt):
            out.append((self.banks[k % len(self.banks)], [k], False))
            if k % 4 == 3:
                out.append((self.smp_banks[(k // 4) % len(self.smp_banks)], list(range(k - 3, k + 1)), True))
        full = []
        for i, (b, ks, s) in enumerate(out):
            full.append((i, b, ks, s, last.get(b)))
            last[b] = i
        return full

    def views(self, b, ks, s):
        if not s:
            k = ks[0]
            return self.c.bank[b][:, :], self.hi[:, k, :], self.lo[:, k, :]
        src = self.c.bank[b][:, 0:4 * NEW].rearrange("p (k t) -> p k t", k=4)
        return src, self.smp[:, ks[0]:ks[0] + 4, 0:NEW], self.smp[:, ks[0]:ks[0] + 4, NEW:2 * NEW]

    def pe(self, eng):
        for i, b, ks, s, prev in self.jobs():
            if prev is not None:
                eng.wait_ge(self.lo_out.sem, prev + 1)
            for j, k in enumerate(ks):
                if s:
                    op = eng.transpose(self.c.bank[b][:, j * NEW:(j + 1) * NEW],
                                       self.src[0:NEW, SM, k * P:(k + 1) * P], self.ident[0:NEW, 0:NEW])
                else:
                    for t in range(NT):
                        op = eng.transpose(self.c.bank[b][:, t * P:(t + 1) * P],
                                           self.src[:, t, k * P:(k + 1) * P], self.ident[:, :])
            op.then_inc(self.turned.sem, 1)

    def act(self, eng):
        for i, b, ks, s, _ in self.jobs():
            src, hi, lo = self.views(b, ks, s)
            eng.wait_ge(self.turned.sem, i + 1)
            eng.activation(hi, src, ACT.Copy).then_inc(self.hi_out.sem, 1)

    def dve(self, eng):
        for i, b, ks, s, _ in self.jobs():
            src, hi, lo = self.views(b, ks, s)
            eng.wait_ge(self.hi_out.sem, i + 1)
            eng.tensor_tensor(lo, src, hi.bitcast(F32), ALU.subtract).then_inc(self.lo_out.sem, 1)


def block_a(c, K):
    nc, d = c.nc, c.dram
    place = c.packer(c.W)
    x = c.at("a_x", [P, TT, D_MODEL], F32, c.Y)
    act = K.act
    junk = place("a_junk", [P, D_MODEL])
    ss, rstd, half = place("a_ss", [P, TT]), place("a_rstd", [P, TT]), place("a_half", [P, TT])
    wf = place("a_wf", [P, KT, HEADS])
    wfs = place("a_wfs", [P, KT, 48], F32R)
    fb = place("a_fb", [HEADS, SEQ])
    fbs = place("a_fbs", [HEADS, 3, NEW])
    z = place("a_z", [HEADS, SEQ + NEW])
    e = place("a_e", [HEADS, SEQ + NEW])
    lf = place("a_lf", [HEADS, TIME])
    lft = place("a_lft", [P, TT, HEADS])
    one = place("a_one", [HEADS, TIME])
    F = place("a_F", [HEADS, TIME])
    T = Transposer(c, "a", x, act, K.ident, KT)
    consts = c.sem("a_consts", unit=16)
    x_in = [c.sem(f"a_x_in{t}", unit=16) for t in range(TT)]
    sq, r0, r1, zero, xh = c.sem("a_sq"), c.sem("a_r0"), c.sem("a_r1"), c.sem("a_zero"), c.sem("a_xh")
    wf_hi, wf_lo, f_mm, f_mv, f_sum = c.sem("a_wf_hi"), c.sem("a_wf_lo"), c.sem("a_f_mm"), c.sem("a_f_mv"), c.sem("a_f_sum")
    soft, logs, scan, f_hi, f_lo, f_t, f_tc, out = (c.sem(f"a_{n}") for n in
        ("soft", "logs", "scan", "f_hi", "f_lo", "f_t", "f_tc", "out"))
    with nc.Block() as block:
        @block.sync
        def _(sp):
            sp.dma_start(K.ident[:], d["ident"]).then_inc(consts.sem, 16)
            for t in range(TT):
                sp.dma_start(x[0:rows(t), t, :], d["x"][0:rows(t), t, :]).then_inc(x_in[t].sem, 16)
            for dst, name in K.loads:
                sp.dma_start(dst[:], d[name]).then_inc(consts.sem, 16)
            sp.dma_start(wf[:], d["w_f"]).then_inc(consts.sem, 16)
            sp.dma_start(lf[:, SEQ:SEQ + PAST], d["cache_logf"]).then_inc(consts.sem, 16)
            sp.wait_ge(f_tc.sem, 1)
            sp.dma_start(d["out_logf"][:, 0:NT, :], lft[:, 0:NT, :]).then_inc(out.sem, 16)
            sp.dma_start(d["out_logf"][0:NEW, SM, :], lft[0:NEW, SM, :]).then_inc(out.sem, 16)
            sp.wait_ge(out.sem, 32)

        n_const = 1 + len(K.loads) + 2

        @block.gpsimd
        def _(pool):
            pool.memset(ss[:], 1.0).then_inc(zero.sem, 1)
            pool.memset(half[:], -0.5).then_inc(zero.sem, 1)
            pool.memset(wfs[:].bitcast(F32), 0.0).then_inc(zero.sem, 1)
            pool.memset(one[:], 1.0).then_inc(zero.sem, 1)
            pool.memset(K.A[:].bitcast(F32), 0.0).then_inc(zero.sem, 1)
            pool.memset(K.B[:].bitcast(F32), 0.0).then_inc(zero.sem, 1)
            pool.wait_ge(sq.sem, TT)
            pool.wait_ge(zero.sem, 2)
            pool.tensor_scalar(ss[:], ss[:], 1.0 / D_MODEL, EPS, ALU.mult, ALU.add).then_inc(r0.sem, 1)
            pool.wait_ge(r0.sem, 1)
            pool.tensor_tensor(rstd[:], ss[:], half[:], ALU.pow).then_inc(r1.sem, 1)

        @block.scalar
        def _(act_):
            act_.wait_ge(zero.sem, 1)
            for t in range(TT):
                act_.wait_ge(x_in[t].sem, 16)
                if t:
                    act_.wait_ge(sq.sem, t)
                act_.activation(junk[0:rows(t), :], x[0:rows(t), t, :], ACT.Square,
                                accum_out=ss[0:rows(t), t:t + 1]).then_inc(sq.sem, 1)
            act_.wait_ge(consts.sem, 16 * n_const)
            act_.wait_ge(zero.sem, 3)
            act_.activation(K.ident_b[:], K.ident[:], ACT.Copy).then_inc(soft.sem, 1)
            act_.activation(K.mask_fox_b[:], K.mask_fox[:], ACT.Copy).then_inc(soft.sem, 1)
            act_.activation(K.mask_mla_b[:], K.mask_mla[:], ACT.Copy).then_inc(soft.sem, 1)
            for k in range(KT):
                op = act_.activation(wfs[:, k, 0:HEADS], wf[:, k, :], ACT.Copy, scale=K.g_fox[:, k:k + 1])
            op.then_inc(wf_hi.sem, 1)
            T.act(act_)
            act_.wait_ge(f_mm.sem, 1)
            act_.activation(fb[:], c.bank[6][32:32 + HEADS, :], ACT.Copy).then_inc(f_mv.sem, 1)
            act_.wait_ge(f_mm.sem, 2)
            act_.activation(fbs[:, 0, :], c.bank[7][0:HEADS, NEW:2 * NEW], ACT.Copy).then_inc(f_mv.sem, 1)
            act_.activation(fbs[:, 1, :], c.bank[7][32:32 + HEADS, 0:NEW], ACT.Copy).then_inc(f_mv.sem, 1)
            act_.activation(fbs[:, 2, :], c.bank[7][32:32 + HEADS, NEW:2 * NEW], ACT.Copy).then_inc(f_mv.sem, 1)
            act_.wait_ge(f_sum.sem, 6)
            act_.activation(e[:], e[:], ACT.Exp).then_inc(soft.sem, 1)
            act_.wait_ge(soft.sem, 4)
            act_.activation(e[:], e[:], ACT.Ln, bias=K.one_col[0:HEADS, :]).then_inc(soft.sem, 1)
            act_.wait_ge(scan.sem, 2)
            act_.wait_ge(zero.sem, 6)
            act_.activation(K.B[0:HEADS, :], F[:], ACT.Copy).then_inc(f_hi.sem, 1)
            act_.activation(K.A[64:64 + HEADS, 0:SEQ], F[:, 0:SEQ], ACT.Copy).then_inc(f_hi.sem, 1)
            act_.activation(K.A[64:64 + HEADS, SEQ:SEQ + NEW], F[:, SEQ + PAST:TIME], ACT.Copy).then_inc(f_hi.sem, 1)

        @block.vector
        def _(dve):
            dve.memset(K.one_col[:], 1.0).then_inc(wf_lo.sem, 1)
            dve.wait_ge(r1.sem, 1)
            for t in range(TT):
                dve.tensor_scalar(x[0:rows(t), t, :], x[0:rows(t), t, :], rstd[0:rows(t), t:t + 1], None,
                                  ALU.mult).then_inc(xh.sem, 1)
            dve.wait_ge(wf_hi.sem, 1)
            for k in range(KT):
                op = dve.scalar_tensor_tensor(wfs[:, k, 32:48], wf[:, k, :], K.g_fox[:, k:k + 1],
                                              wfs[:, k, 0:HEADS].bitcast(F32), ALU.mult, ALU.subtract)
            op.then_inc(wf_lo.sem, 1)
            T.dve(dve)
            dve.wait_ge(f_mv.sem, 4)
            dve.tensor_tensor(z[:, 0:SEQ], c.bank[6][0:HEADS, :], fb[:], ALU.add).then_inc(f_sum.sem, 1)
            dve.tensor_tensor(z[:, SEQ:], c.bank[7][0:HEADS, 0:NEW], fbs[:, 0, :], ALU.add).then_inc(f_sum.sem, 1)
            dve.wait_ge(f_sum.sem, 2)
            dve.tensor_tensor(z[:, SEQ:], z[:, SEQ:], fbs[:, 1, :], ALU.add).then_inc(f_sum.sem, 1)
            dve.wait_ge(f_sum.sem, 3)
            dve.tensor_tensor(z[:, SEQ:], z[:, SEQ:], fbs[:, 2, :], ALU.add).then_inc(f_sum.sem, 1)
            dve.wait_ge(f_sum.sem, 4)
            dve.tensor_scalar(z[:], z[:], K.b_f[:, 0:1], None, ALU.add).then_inc(f_sum.sem, 1)
            dve.wait_ge(f_sum.sem, 5)
            dve.scalar_tensor_tensor(e[:], z[:], -1.0, z[:], ALU.mult, ALU.min).then_inc(f_sum.sem, 1)
            dve.wait_ge(soft.sem, 5)
            dve.scalar_tensor_tensor(lf[:, 0:SEQ], z[:, 0:SEQ], 0.0, e[:, 0:SEQ], ALU.min, ALU.subtract).then_inc(logs.sem, 1)
            dve.scalar_tensor_tensor(lf[:, SEQ + PAST:], z[:, SEQ:], 0.0, e[:, SEQ:], ALU.min, ALU.subtract).then_inc(logs.sem, 1)
            dve.wait_ge(logs.sem, 2)
            dve.wait_ge(zero.sem, 4)
            dve.tensor_tensor_scan(F[:, 0:SEQ], one[:, 0:SEQ], lf[:, 0:SEQ], 0.0, ALU.mult, ALU.add).then_inc(scan.sem, 1)
            dve.tensor_tensor_scan(F[:, SEQ:], one[:, SEQ:], lf[:, SEQ:], 0.0, ALU.mult, ALU.add).then_inc(scan.sem, 1)
            dve.wait_ge(f_t.sem, 1)
            dve.tensor_copy(lft[:, 0:NT, :], c.bank[0][:, 0:NT * HEADS].rearrange("p (t h) -> p t h", t=NT))
            dve.tensor_copy(lft[0:NEW, SM, :], c.bank[0][0:NEW, NT * HEADS:TT * HEADS]).then_inc(f_tc.sem, 1)
            dve.wait_ge(f_hi.sem, 3)
            dve.tensor_tensor(K.B[32:32 + HEADS, :], F[:], K.B[0:HEADS, :].bitcast(F32), ALU.subtract).then_inc(f_lo.sem, 1)
            dve.tensor_tensor(K.A[96:96 + HEADS, 0:SEQ], F[:, 0:SEQ], K.B[0:HEADS, 0:SEQ].bitcast(F32),
                              ALU.subtract).then_inc(f_lo.sem, 1)
            dve.tensor_tensor(K.A[96:96 + HEADS, SEQ:SEQ + NEW], F[:, SEQ + PAST:],
                              K.B[0:HEADS, SEQ + PAST:].bitcast(F32), ALU.subtract).then_inc(f_lo.sem, 1)

        @block.tensor
        def _(pe):
            pe.wait_ge(consts.sem, 16 * n_const)
            pe.wait_ge(xh.sem, TT)
            T.pe(pe)
            pe.wait_ge(T.lo_out.sem, len(T.jobs()))
            pe.wait_ge(wf_lo.sem, 2)
            for k in range(KT):
                for i, a in enumerate((act[0], act[1])):
                    op = pe.matmul(c.bank[6][0:48, :], wfs[:, k, :], a[:, k, :], start=(k == 0 and i == 0),
                                   stop=(k == KT - 1 and i == 1))
            op.then_inc(f_mm.sem, 1)
            for k in range(KT):
                op = pe.matmul(c.bank[7][0:48, 0:2 * NEW], wfs[:, k, :], act[2][:, k, :], start=(k == 0), stop=(k == KT - 1))
            op.then_inc(f_mm.sem, 1)
            pe.wait_ge(logs.sem, 2)
            for t in range(TT):
                n, a = rows(t), (t * P if t < SM else SEQ + PAST)
                op = pe.transpose(c.bank[0][0:n, t * HEADS:(t + 1) * HEADS], lf[:, a:a + n], K.ident[0:HEADS, 0:HEADS])
            op.then_inc(f_t.sem, 1)


class Consts:

    def __init__(self, c):
        self.base = (c.limit - 12544) // 64 * 64
        place = c.packer(self.base)
        self.c = c
        self.ident = place("ident", [P, P])
        self.mask_fox, self.mask_mla = place("mask_fox", [P, P]), place("mask_mla", [P, P])
        self.ident_b, self.mask_fox_b, self.mask_mla_b = (place(n, [P, P], BF16) for n in ("ident_b", "mask_fox_b", "mask_mla_b"))
        self.g_fox, self.g_kv, self.g_mla = (place(n, [P, KT]) for n in ("g_fox", "g_kv", "g_mla"))
        self.g_qa = place("g_qa", [P, LT])
        self.b_f = place("b_f", [HEADS, 1])
        self.one_col = place("one_col", [P, 1])
        self.nsel, self.psel = place("nsel", [P, HEADS]), place("psel", [P, HEADS])
        self.gq, self.gk = place("gq", [P, P]), place("gk", [P, P])
        self.rstd1, self.half_rstd1 = place("rstd1", [P, TT]), place("half_rstd1", [P, TT])
        self.A = place("decay_q", [P, SEQ + NEW], F32R)
        self.B = place("decay_k", [P, TIME], F32R)
        self.end = place.cur[0]
        assert self.end <= c.limit, (self.end, c.limit)
        self.loads = [(self.mask_fox, "mask_fox"), (self.mask_mla, "mask_mla"), (self.g_fox, "g_fox"),
                      (self.g_kv, "g_kv"), (self.g_mla, "g_mla"), (self.g_qa, "g_qa"), (self.b_f, "b_f"),
                      (self.nsel, "nsel"), (self.psel, "psel"), (self.gq, "g_q"), (self.gk, "g_k")]
        self.o_fox = c.at("o_fox", [HD, HEADS, SEQ + NEW], F32, c.Y)
        self.act = (c.at("x_hi", [P, KT, SEQ], F32R, c.X), c.at("x_lo", [P, KT, SEQ], F32R, c.X + 32768),
                    c.at("x_smp", [P, KT, 2 * NEW], F32R, c.X + 65536))


class FoxHead:

    NAMES = ["new_qk", "q", "k", "s3", "s2", "s1", "s0", "sa", "sb", "p0", "p1", "p2", "p3", "pn", "g", "gn", "o",
             "on"]
    SLOTS = [7, 8, 9, 12, 14, 16, 18, 20, 21, 25, 26, 27, 28, 29, 30, 31, 33, 35]
    SPLITS = ["cache_k", "new_qk", "q", "k", "p0", "p1", "p2", "p3", "pn"]

    def __init__(self, c, K, place):
        self.c, self.K = c, K
        self.jobs = {n: (s, i) for i, (n, s) in enumerate(zip(self.NAMES, self.SLOTS))}
        self.raw = place("b_raw", [P, TT, 4, HD])
        self.qk2 = place("b_qk2", [P, TT, 2, HD])
        self.ss, self.rstd, self.half = place("b_ss", [P, 2 * TT]), place("b_rstd", [P, 2 * TT]), place("b_half", [P, 2 * TT])
        self.vhi, self.vlo = place("b_vhi", [P, TT, HD], F32R), place("b_vlo", [P, TT, HD], F32R)
        self.ck = place("b_ck", [HD, PAST])
        self.cv = place("b_cv", [P, NT, HD])
        self.cvhi, self.cvlo = place("b_cvhi", [P, NT, HD], F32R), place("b_cvlo", [P, NT, HD], F32R)
        self.qhi, self.qlo = place("b_qhi", [HD, SEQ], F32R), place("b_qlo", [HD, SEQ], F32R)
        self.khi, self.klo = place("b_khi", [HD, SEQ], F32R), place("b_klo", [HD, SEQ], F32R)
        self.nqhi, self.nqlo = place("b_nqhi", [HD, NEW], F32R), place("b_nqlo", [HD, NEW], F32R)
        self.nkhi, self.nklo = place("b_nkhi", [HD, SAMP], F32R), place("b_nklo", [HD, SAMP], F32R)
        self.p = [place(f"b_p{i}", [P, (i + 1) * P]) for i in range(NT)]
        self.pn = place("b_pn", [NEW, SAMP])
        self.first = [0, P, 2 * P, 2 * P]
        self.pt = [(place(f"b_pt{j}hi", [P, SEQ - f], F32R), place(f"b_pt{j}lo", [P, SEQ - f], F32R))
                   for j, f in enumerate(self.first)]
        self.ptn = (place("b_ptnhi", [P, 512], F32R), place("b_ptnlo", [P, 512], F32R))
        self.gate = place("b_gate", [P, TT, HD])
        self.gt = place("b_gt", [HD, SEQ + NEW])
        self.nm, self.rs, self.ri = place("b_nm", [P, TT]), place("b_rs", [P, TT]), place("b_ri", [P, TT])
        self.m2, self.r2 = place("b_m2", [NEW, 2]), place("b_r2", [NEW, 2])
        s = c.sem
        self.ready = [s(f"b_ready{b}", 6) for b in range(3)]
        self.free = [s(f"b_free{b}", 6, credit=1) for b in range(3)]
        self.took = s("b_took", NT)
        self.took_lo = s("b_took_lo")
        self.took_smp = s("b_took_smp")
        self.sq = s("b_sq")
        self.sums = s("b_sums")
        self.var, self.rst = s("b_var"), s("b_rst")
        self.sel = s("b_sel", 2)
        self.normed = s("b_normed")
        self.v_hi, self.v_lo = s("b_v_hi"), s("b_v_lo")
        self.tanh, self.gated, self.scaled = s("b_tanh"), s("b_gated"), s("b_scaled")
        self.hi_done = s("b_hi_done", len(self.SPLITS))
        self.ck_lo = s("b_ck_lo")
        self.new_max = s("b_new_max", 2)
        self.negmax = s("b_negmax", TT)
        self.inv = s("b_inv", 2)
        self.o_done = s("b_o_done", 2)
        self.ck_in, self.cv_in = s("b_ck_in", 1, 16), s("b_cv_in", 1, 16)
        self.out = s("b_out", 4, 16)
        self.zero = s("b_zero")
        self.warm = place("b_warm", [P, 1])

    def bank(self, name):
        return self.c.bank[5 + self.jobs[name][1] % 3]

    def _nth(self, name):
        i = self.jobs[name][1]
        return i % 3, i // 3 + 1

    def wait_ready(self, eng, g, name):
        b, k = self._nth(name)
        self.ready[b].wait(eng, g, k)

    def wait_free(self, eng, g, name):
        b, k = self._nth(name)
        self.free[b].wait(eng, g, k - 1)

    def wait_out_of(self, eng, g, name):
        b, k = self._nth(name)
        self.free[b].wait(eng, g, k)

    def end(self, op, name):
        op.then_inc(self.ready[self._nth(name)[0]].sem, 1)

    def release(self, op, name):
        op.then_inc(self.free[self._nth(name)[0]].sem, 1)

    def split_views(self, name):
        b = self.bank(name)
        if name == "new_qk":
            return [(b[:, 0:NEW], self.nqhi[:], self.nqlo[:]),
                    (b[:, NEW:2 * NEW], self.nkhi[:, PAST:], self.nklo[:, PAST:])]
        if name == "q":
            return [(b[:, :], self.qhi[:], self.qlo[:])]
        if name == "k":
            return [(b[:, :], self.khi[:], self.klo[:])]
        if name == "pn":
            hi, lo = self.ptn
            n = NT * NEW
            return [(b[:, 0:n], hi[:, 0:n], lo[:, 0:n]),
                    (b[0:NEW, n:n + NEW], hi[0:NEW, n:n + NEW], lo[0:NEW, n:n + NEW])]
        if name[0] == "p":
            j = int(name[1])
            hi, lo = self.pt[j]
            a = j * P - self.first[j]
            return [(b[:, j * P:], hi[:, a:], lo[:, a:])]
        raise KeyError(name)

    def act_split(self, eng, g, name):
        if name == "cache_k":
            self.ck_in.wait(eng, g, 1)
            eng.activation(self.nkhi[:, 0:PAST], self.ck[:], ACT.Copy).then_inc(self.hi_done.sem, 1)
            return
        self.wait_ready(eng, g, name)
        for src, hi, lo in self.split_views(name):
            op = eng.activation(hi, src, ACT.Copy)
        op.then_inc(self.hi_done.sem, 1)

    def dve_split(self, eng, g, name):
        self.hi_done.wait(eng, g, self.SPLITS.index(name) + 1)
        if name == "cache_k":
            eng.tensor_tensor(self.nklo[:, 0:PAST], self.ck[:], self.nkhi[:, 0:PAST].bitcast(F32),
                              ALU.subtract).then_inc(self.ck_lo.sem, 1)
            return
        for src, hi, lo in self.split_views(name):
            op = eng.tensor_tensor(lo, src, hi.bitcast(F32), ALU.subtract)
        self.release(op, name)

    def act_take(self, eng, h, t, gemm):
        if t < SM:
            gemm.done.wait(eng, h, t + 1)
            eng.activation(self.raw[:, t, :, :], self.c.bank[t][:, :].rearrange("p (s d) -> p s d", s=4),
                           ACT.Copy).then_inc(self.took.sem, 1)
        else:
            gemm.used.wait(eng, h, gemm.units)
            eng.activation(self.raw[0:NEW, SM, :, :],
                           self.c.bank[SM][NEW:2 * NEW, :].rearrange("p (s d) -> p s d", s=4),
                           ACT.Copy).then_inc(self.took_lo.sem, 1)

    def dve_take(self, eng, h):
        self.took_lo.wait(eng, h, 1)
        raw = self.raw[0:NEW, SM, :, :].rearrange("p s d -> p (s d)")
        eng.tensor_tensor(raw, self.c.bank[SM][0:NEW, :], raw, ALU.add).then_inc(self.took_smp.sem, 1)

    def act_squares(self, eng, g):
        self.took_smp.wait(eng, g, 1)
        self.took.wait(eng, g, NT)
        for n, t in ((P, slice(0, NT)), (NEW, slice(SM, TT))):
            op = eng.activation(self.qk2[0:n, t, :, :], self.raw[0:n, t, 0:2, :], ACT.Square)
        op.then_inc(self.sq.sem, 1)

    def act_values(self, eng, g):
        for n, t in ((P, slice(0, NT)), (NEW, slice(SM, TT))):
            op = eng.activation(self.vhi[0:n, t, :], self.raw[0:n, t, 2, :], ACT.Copy)
        self.cv_in.wait(eng, g, 1)
        op = eng.activation(self.cvhi[:], self.cv[:], ACT.Copy)
        op.then_inc(self.v_hi.sem, 1)

    def act_tanh(self, eng, g):
        for n, t in ((P, slice(0, NT)), (NEW, slice(SM, TT))):
            op = eng.activation(self.gate[0:n, t, :], self.raw[0:n, t, 3, :], ACT.Tanh, scale=0.5)
        op.then_inc(self.tanh.sem, 1)

    def act_exp(self, eng, g, name):
        b = self.bank(name)
        if name in ("sa", "sb"):
            i = ("sa", "sb").index(name)
            self.negmax.wait(eng, g, TT)
            op = eng.activation(self.pn[:, i * 288:(i + 1) * 288], b[0:NEW, 0:288], ACT.Exp, bias=self.nm[0:NEW, SM:TT],
                                accum_out=self.r2[:, i:i + 1])
        else:
            i = int(name[1])
            self.negmax.wait(eng, g, NT - i)
            op = eng.activation(self.p[i][:], b[:, 0:(i + 1) * P], ACT.Exp, bias=self.nm[:, i:i + 1],
                                accum_out=self.rs[:, i:i + 1])
        self.release(op, name)

    def act_gate(self, eng, g, name):
        self.wait_ready(eng, g, name)
        a, n = (0, SEQ) if name == "g" else (SEQ, NEW)
        op = eng.activation(self.gt[:, a:a + n], self.bank(name)[:, 0:n], ACT.Copy)
        self.release(op, name)

    def dve_sums(self, eng, g):
        self.sq.wait(eng, g, 1)
        for n, t in ((P, slice(0, NT)), (NEW, slice(SM, TT))):
            op = eng.tensor_reduce(self.ss[0:n, 2 * t.start:2 * t.stop], self.qk2[0:n, t, :, :].rearrange("p t s d -> p (t s) d"),
                                   AX.X, ALU.add)
        op.then_inc(self.sums.sem, 1)
        self.sums.wait(eng, g, 1)
        eng.tensor_scalar(self.ss[:], self.ss[:], 1.0 / HD, EPS, ALU.mult, ALU.add).then_inc(self.var.sem, 1)

    def dve_norm(self, eng, g):
        self.rst.wait(eng, g, 1)
        for t in range(TT):
            for s, gain in ((0, self.K.gq), (1, self.K.gk)):
                x = self.raw[0:rows(t), t, s, :]
                op = eng.scalar_tensor_tensor(x, x, self.rstd[0:rows(t), 2 * t + s:2 * t + s + 1], gain[0:rows(t), :],
                                              ALU.mult, ALU.mult)
        op.then_inc(self.normed.sem, 1)

    def dve_values(self, eng, g):
        self.v_hi.wait(eng, g, 1)
        for n, t in ((P, slice(0, NT)), (NEW, slice(SM, TT))):
            op = eng.tensor_tensor(self.vlo[0:n, t, :], self.raw[0:n, t, 2, :], self.vhi[0:n, t, :].bitcast(F32), ALU.subtract)
        op = eng.tensor_tensor(self.cvlo[:], self.cv[:], self.cvhi[:].bitcast(F32), ALU.subtract)
        op.then_inc(self.v_lo.sem, 1)

    def dve_gate(self, eng, g):
        self.tanh.wait(eng, g, 1)
        for n, t in ((P, slice(0, NT)), (NEW, slice(SM, TT))):
            y = self.gate[0:n, t, :]
            op = eng.scalar_tensor_tensor(y, y, 1.0, self.raw[0:n, t, 3, :], ALU.add, ALU.mult)
        op.then_inc(self.gated.sem, 1)

    def dve_max(self, eng, g, name):
        self.wait_ready(eng, g, name)
        b = self.bank(name)
        if name in ("sa", "sb"):
            i = ("sa", "sb").index(name)
            eng.tensor_reduce(self.m2[:, i:i + 1], b[0:NEW, 0:288], AX.X, ALU.max).then_inc(self.new_max.sem, 1)
            if i:
                self.new_max.wait(eng, g, 2)
                eng.tensor_reduce(self.nm[0:NEW, SM:TT], self.m2[:], AX.X, ALU.max, negate=True).then_inc(self.negmax.sem, 1)
        else:
            i = int(name[1])
            eng.tensor_reduce(self.nm[:, i:i + 1], b[:, 0:(i + 1) * P], AX.X, ALU.max, negate=True).then_inc(self.negmax.sem, 1)

    def dve_scale_gate(self, eng, g):
        self.wait_out_of(eng, g, "sb")
        eng.tensor_tensor(self.rs[0:NEW, SM:TT], self.r2[:, 0:1], self.r2[:, 1:2], ALU.add).then_inc(self.inv.sem, 1)
        self.inv.wait(eng, g, 1)
        eng.reciprocal(self.ri[:], self.rs[:]).then_inc(self.inv.sem, 1)
        self.inv.wait(eng, g, 2)
        self.gated.wait(eng, g, 1)
        for t in range(TT):
            y = self.gate[0:rows(t), t, :]
            op = eng.tensor_scalar(y, y, self.ri[0:rows(t), t:t + 1], 0.5, ALU.mult, ALU.mult)
        op.then_inc(self.scaled.sem, 1)

    def dve_o(self, eng, g, name, dst):
        self.wait_ready(eng, g, name)
        self.wait_out_of(eng, g, "g" if name == "o" else "gn")
        a, n = (0, SEQ) if name == "o" else (SEQ, NEW)
        op = eng.tensor_tensor(dst[:, g, a:a + n], self.bank(name)[:, 0:n], self.gt[:, a:a + n], ALU.mult)
        self.release(op, name)

    def pe_job(self, eng, g, name):
        K, b = self.K, self.bank(name)
        self.wait_free(eng, g, name)
        if name == "new_qk":
            self.normed.wait(eng, g, 1)
            for s in range(2):
                op = turn(eng, b[:, s * NEW:(s + 1) * NEW], self.raw[0:NEW, SM, s, :], K.ident[0:NEW, 0:NEW], s == 0)
        elif name in ("q", "k"):
            for t in range(NT):
                op = eng.transpose(b[:, t * P:(t + 1) * P], self.raw[:, t, "qk".index(name), :], K.ident[:, :])
        elif name in ("s0", "s1", "s2", "s3"):
            i = int(name[1])
            n = max(i + 1, 2) * P
            self.wait_out_of(eng, g, "q")
            self.wait_out_of(eng, g, "k")
            self.sel.wait(eng, g, 2)
            q = slice(i * P, (i + 1) * P)
            for m, (x, y) in enumerate(three(self.qhi, self.qlo, self.khi, self.klo)):
                eng.matmul(b[:, 0:n], x[:, q], y[:, 0:n], start=(m == 0), stop=False)
            eng.matmul(b[:, q], K.ident_b[:, :], K.mask_fox_b[:, :], start=False, stop=False, skip_group_check=True)
            op = eng.matmul(b[:, 0:n], K.A[:, q], K.B[:, 0:n], start=False, stop=True)
        elif name in ("sa", "sb"):
            i = ("sa", "sb").index(name)
            k = slice(i * 288, (i + 1) * 288)
            self.ck_lo.wait(eng, g, 1)
            self.wait_out_of(eng, g, "new_qk")
            for m, (x, y) in enumerate(three(self.nqhi, self.nqlo, self.nkhi, self.nklo)):
                eng.matmul(b[0:NEW, 0:288], x[:, :], y[:, k], start=(m == 0), stop=False)
            if i:
                eng.matmul(b[0:NEW, 224:288], K.ident_b[0:NEW, 0:NEW], K.mask_fox_b[0:NEW, 0:NEW], start=False,
                           stop=False, skip_group_check=True)
            op = eng.matmul(b[0:NEW, 0:288], K.A[:, SEQ:SEQ + NEW], K.B[:, SEQ + i * 288:SEQ + (i + 1) * 288],
                            start=False, stop=True)
        elif name == "pn":
            self.wait_out_of(eng, g, "sb")
            for t in range(TT):
                n = rows(t)
                op = turn(eng, b[0:n, t * NEW:(t + 1) * NEW], self.pn[:, t * P:t * P + n], K.ident[0:NEW, 0:NEW], t == 0)
        elif name[0] == "p":
            j = int(name[1])
            self.wait_out_of(eng, g, "s0")
            for i in range(j, NT):
                op = eng.transpose(b[:, i * P:(i + 1) * P], self.p[i][:, j * P:(j + 1) * P], K.ident[:, :])
        elif name == "o":
            for j in range(NT):
                self.wait_out_of(eng, g, f"p{j}")
            self.v_lo.wait(eng, g, 1)
            for j in range(NT):
                f = self.first[j]
                for m, (x, y) in enumerate(three(self.vhi, self.vlo, *self.pt[j])):
                    op = eng.matmul(b[:, f:], x[:, j, :], y[:, :], start=(j == 0 and m == 0), stop=(j == NT - 1 and m == 2))
        elif name == "on":
            self.wait_out_of(eng, g, "pn")
            for t in range(TT):
                v = (self.cvhi, self.cvlo) if t < SM else (self.vhi, self.vlo)
                n = rows(t)
                for m, (x, y) in enumerate(three(*v, *self.ptn)):
                    op = eng.matmul(b[:, 0:256], x[0:n, t, :], y[0:n, t * NEW:t * NEW + 256],
                                    start=(t == 0 and m == 0), stop=(t == SM and m == 2))
        elif name == "g":
            self.scaled.wait(eng, g, 1)
            for t in range(NT):
                op = eng.transpose(b[:, t * P:(t + 1) * P], self.gate[:, t, :], K.ident[:, :])
        elif name == "gn":
            op = turn(eng, b[:, 0:NEW], self.gate[0:NEW, SM, :], K.ident[0:NEW, 0:NEW], True)
        self.end(op, name)


def block_b(c, K, proj):
    nc, d = c.nc, c.dram
    place = c.packer(c.W)
    act = K.act
    G = Gemm(c, "b", d["w_fox"], HEADS, KT // UK, UK, 512, RAW_FOX, act, K.g_fox, place)
    H = FoxHead(c, K, place)
    o_all = K.o_fox
    assert place.cur[0] <= K.base
    U, R = G.units, G.raws
    cached = "cache_k"
    zero = H.zero

    with nc.Block() as block:
        @block.sync
        def _(sp):
            def body(h, last, g):
                for u in range(U):
                    if h is not None and not (last and u + R >= U):
                        n = u + R
                        G.load(sp, h + n // U if n >= U else h, n % U)
                    if g is not None and u == 0:
                        H.took.wait(sp, g, NT)
                        H.took_smp.wait(sp, g, 1)
                        sp.dma_start(d["out_fv"][g][:, 0:NT, :], H.raw[:, 0:NT, 2, :]).then_inc(H.out.sem, 16)
                        sp.dma_start(d["out_fv"][g][0:NEW, SM, :], H.raw[0:NEW, SM, 2, :]).then_inc(H.out.sem, 16)
                        H.normed.wait(sp, g, 1)
                        sp.dma_start(d["out_fk"][g][:, 0:NT, :], H.raw[:, 0:NT, 1, :]).then_inc(H.out.sem, 16)
                        sp.dma_start(d["out_fk"][g][0:NEW, SM, :], H.raw[0:NEW, SM, 1, :]).then_inc(H.out.sem, 16)
                    if h is None and u < proj.lead:
                        proj.load_next(sp, 0, u)
                if h is not None:
                    if g is not None:
                        H.ck_lo.wait(sp, g, 1)
                        H.v_lo.wait(sp, g, 1)
                    sp.dma_start(H.ck[:], d["cache_k"][h]).then_inc(H.ck_in.sem, 16)
                    sp.dma_start(H.cv[:], d["cache_v"][h]).then_inc(H.cv_in.sem, 16)
            for u in range(R):
                G.load(sp, 0, u)
            body(0, False, None)
            with sp.Fori(1, HEADS - 1) as h:
                body(h, False, h - 1)
            body(HEADS - 1, True, HEADS - 2)
            G.w_lo.wait(sp, HEADS - 1, U)
            for u in range(proj.G.raws):
                proj.G.load(sp, 0, u)
            body(None, True, HEADS - 1)
            sp.wait_ge(H.out.sem, HEADS * 4 * 16)

        @block.gpsimd
        def _(pool):
            pool.tensor_scalar(K.gq[:], K.gq[:], FOX_SCALE, None, ALU.mult).then_inc(zero.sem, 1)
            pool.memset(H.ss[:], 1.0).then_inc(zero.sem, 1)
            pool.memset(H.rs[:], 1.0).then_inc(zero.sem, 1)
            pool.memset(H.half[:], -0.5).then_inc(zero.sem, 1)
            for x in (*H.ptn, *H.pt[NT - 1]):
                pool.memset(x[:].bitcast(F32), 0.0).then_inc(zero.sem, 1)

            def head(g):
                if not isinstance(g, int) or g > 0:
                    H.wait_ready(pool, g - 1, "sb")
                H.rst.wait(pool, g, 0)
                pool.tensor_copy(K.A[0:64, :], K.nsel[0:64, bass.ds(g, 1)].broadcast_to([64, SEQ + NEW])).then_inc(H.sel.sem, 1)
                H.sel.wait(pool, g, 1)
                pool.tensor_copy(K.B[64:P, :], K.psel[64:P, bass.ds(g, 1)].broadcast_to([64, TIME])).then_inc(H.sel.sem, 1)
                H.sel.wait(pool, g, 2)
                H.var.wait(pool, g, 1)
                pool.tensor_tensor(H.rstd[:], H.ss[:], H.half[:], ALU.pow).then_inc(H.rst.sem, 1)
            pool.wait_ge(zero.sem, 8)
            steps(pool, HEADS, lambda g, last: head(g))

        @block.scalar
        def _(act_):
            act_.activation(H.warm[:], K.one_col[:], ACT.Tanh)

            def body(h, last, g):
                for s in range(5 * U):
                    if h is not None and (s == 0 or (s > 5 and s % 5 == 1)) and not (last and s // 5 == U - 1):
                        n = s // 5 + 1
                        G.make_hi(act_, h + n // U if n >= U else h, n % U)
                    if h is None and s == 0:
                        proj.split_hi(act_, 0)
                    if h is None and s % 5 == 1 and s // 5 + 1 < proj.lead:
                        proj.split_hi(act_, s // 5 + 1)
                    if g is not None:
                        if s == 0:
                            H.act_squares(act_, g)
                            H.act_split(act_, g, cached)
                        if s == 3:
                            H.act_values(act_, g)
                        if s == 4:
                            H.act_tanh(act_, g)
                        for name, (slot, _) in H.jobs.items():
                            if slot + 1 == s:
                                if name in H.SPLITS:
                                    H.act_split(act_, g, name)
                                elif name == "sb":
                                    H.act_exp(act_, g, "sa")
                                    H.act_exp(act_, g, "sb")
                                elif name[0] == "s" and name != "sa":
                                    H.act_exp(act_, g, name)
                                elif name in ("g", "gn"):
                                    H.act_gate(act_, g, name)
                    if h is not None and s >= 5 * (U - 1) + 1:
                        t = s - 5 * (U - 1) - 1
                        if t == 0 and g is not None:
                            H.v_lo.wait(act_, g, 1)
                            H.gated.wait(act_, g, 1)
                            H.out.wait(act_, g, 4)
                        H.act_take(act_, h, t, G)
                if h is not None:
                    H.act_take(act_, h, SM, G)
            G.make_hi(act_, 0, 0)
            body(0, False, None)
            act_.wait_ge(zero.sem, 8)
            with act_.Fori(1, HEADS - 1) as h:
                body(h, False, h - 1)
            body(HEADS - 1, True, HEADS - 2)
            H.wait_out_of(act_, HEADS - 2, "on")
            body(None, True, HEADS - 1)

        @block.vector
        def _(dve):
            for bank_free in H.free:
                bank_free.grant(dve)

            def body(h, last, g):
                for s in range(5 * U):
                    if h is not None and (s == 0 or (s > 5 and s % 5 == 1)) and not (last and s // 5 == U - 1):
                        n = s // 5 + 1
                        G.make_lo(dve, h + n // U if n >= U else h, n % U)
                    if h is None and s == 0:
                        proj.split_lo(dve, 0)
                    if h is None and s % 5 == 1 and s // 5 + 1 < proj.lead:
                        proj.split_lo(dve, s // 5 + 1)
                    if g is not None:
                        if s == 0:
                            H.dve_sums(dve, g)
                            H.dve_split(dve, g, cached)
                        if s == 2:
                            H.dve_norm(dve, g)
                        if s == 4:
                            H.dve_values(dve, g)
                        if s == 5:
                            H.dve_gate(dve, g)
                        for name, (slot, _) in H.jobs.items():
                            if slot + 1 == s:
                                if name in H.SPLITS:
                                    H.dve_split(dve, g, name)
                                elif name[0] == "s":
                                    H.dve_max(dve, g, name)
                                elif name in ("o", "on"):
                                    H.dve_o(dve, g, name, o_all)
                        if s == H.jobs["sb"][0] + 3:
                            H.dve_scale_gate(dve, g)
                if h is not None:
                    H.dve_take(dve, h)
            G.make_lo(dve, 0, 0)
            body(0, False, None)
            dve.wait_ge(zero.sem, 8)
            with dve.Fori(1, HEADS - 1) as h:
                body(h, False, h - 1)
            body(HEADS - 1, True, HEADS - 2)
            body(None, True, HEADS - 1)

        @block.tensor
        def _(pe):
            def body(h, last, g):
                for s in range(5 * U):
                    u, t = s // 5, s % 5
                    if h is not None:
                        if t == 0:
                            G.w_lo.wait(pe, h, u + 1)
                        if u == 0 and g is not None:
                            if t < SM:
                                H.took.wait(pe, g, t + 1)
                            else:
                                H.took_smp.wait(pe, g, 1)
                        G.multiply(pe, h, u, t)
                    elif u < proj.lead:
                        if u == 0:
                            if t < SM:
                                H.took.wait(pe, g, t + 1)
                            else:
                                H.took_smp.wait(pe, g, 1)
                        proj.multiply(pe, u, t)
                    if g is not None:
                        for name, (slot, _) in H.jobs.items():
                            if slot == s:
                                H.pe_job(pe, g, name)
            body(0, False, None)
            pe.wait_ge(zero.sem, 8)
            with pe.Fori(1, HEADS - 1) as h:
                body(h, False, h - 1)
            body(HEADS - 1, True, HEADS - 2)
            body(None, True, HEADS - 1)


class OutProj:

    def __init__(self, c, K, tag, w, o, act, resid, base, finish, raw, lead):
        self.c, self.o, self.act, self.resid, self.lead = c, o, act, resid, lead
        place = c.packer(base)
        self.G = Gemm(c, tag, w, D_MODEL // 512, KT // UK, UK, 512, raw, act, None, place)
        self.res = [place(f"{tag}_res{i}", [P, TT, 512]) for i in range(2)]
        self.tmp = place(f"{tag}_tmp", [NEW, 512])
        self.hi_o, self.lo_o = c.sem(f"{tag}_hi_o"), c.sem(f"{tag}_lo_o")
        self.res_in = [c.sem(f"{tag}_res_in{i}", 2, 16) for i in range(2)]
        self.moved, self.summed, self.rows_out = c.sem(f"{tag}_moved"), c.sem(f"{tag}_summed"), c.sem(f"{tag}_rows_out", TT)
        self.finish = finish(c, K, tag, place, self.rows_out)

    def load_next(self, sp, n, u):
        m = n * self.G.units + u + self.G.raws
        if m < self.G.steps * self.G.units:
            self.G.load(sp, m // self.G.units, m % self.G.units)

    def split_hi(self, act_, u):
        hi, _, smp = self.act
        k = slice(u * UK, (u + 1) * UK)
        act_.activation(hi[:, k, :], self.o[:, k, 0:SEQ], ACT.Copy)
        act_.activation(smp[:, k, 0:NEW], self.o[:, k, SEQ:SEQ + NEW], ACT.Copy).then_inc(self.hi_o.sem, 1)
        self.G.make_hi(act_, 0, u)

    def split_lo(self, dve, u):
        hi, lo, smp = self.act
        k = slice(u * UK, (u + 1) * UK)
        dve.wait_ge(self.hi_o.sem, u + 1)
        dve.tensor_tensor(lo[:, k, :], self.o[:, k, 0:SEQ], hi[:, k, :].bitcast(F32), ALU.subtract)
        dve.tensor_tensor(smp[:, k, NEW:2 * NEW], self.o[:, k, SEQ:SEQ + NEW], smp[:, k, 0:NEW].bitcast(F32),
                          ALU.subtract).then_inc(self.lo_o.sem, 1)
        self.G.make_lo(dve, 0, u)

    def multiply(self, pe, u, t):
        if t == 0:
            self.G.w_lo.wait(pe, 0, u + 1)
            pe.wait_ge(self.lo_o.sem, u + 1)
        self.G.multiply(pe, 0, u, t)

    def block(self):
        c, G, F, res, tmp = self.c, self.G, self.finish, self.res, self.tmp
        moved, summed, rows_out, res_in = self.moved, self.summed, self.rows_out, self.res_in
        U, N = G.units, G.steps
        left = [range(self.lead if n == 0 else 0, U) for n in range(N)]

        with c.nc.Block() as block:
            @block.sync
            def _(sp):
                def load_res(n):
                    if n >= 2:
                        rows_out.wait(sp, n - 2, TT)
                    for q, t in ((P, slice(0, NT)), (NEW, slice(SM, TT))):
                        sp.dma_start(res[n % 2][0:q, t, :], self.resid[0:q, t, n * 512:(n + 1) * 512]).then_inc(res_in[n % 2].sem, 16)
                if not self.lead:
                    for u in range(G.raws):
                        G.load(sp, 0, u)
                load_res(0)
                load_res(1)
                for n in range(N):
                    for u in left[n]:
                        self.load_next(sp, n, u)
                        if u == 1 and n >= 1:
                            F.sp_step(sp, n - 1)
                            if n + 1 < N:
                                load_res(n + 1)
                F.sp_step(sp, N - 1)
                F.sp_tail(sp)

            @block.gpsimd
            def _(pool):
                F.pool(pool)

            @block.scalar
            def _(act_):
                for n in range(N):
                    for u in left[n]:
                        if n == 0:
                            self.split_hi(act_, u)
                        elif u:
                            G.make_hi(act_, n, u)
                        if u == 2 and n:
                            F.act_step(act_, n - 1)
                    if n + 1 < N:
                        G.make_hi(act_, n + 1, 0)
                    G.used.wait(act_, n, U)
                    if n:
                        rows_out.wait(act_, n - 1, TT)
                    act_.activation(tmp[:], c.bank[SM][NEW:2 * NEW, :], ACT.Copy).then_inc(moved.sem, 1)
                F.act_step(act_, N - 1)
                F.act_tail(act_)

            @block.vector
            def _(dve):
                for n in range(N):
                    for u in left[n]:
                        if n == 0:
                            self.split_lo(dve, u)
                        elif u:
                            G.make_lo(dve, n, u)
                    if n + 1 < N:
                        G.make_lo(dve, n + 1, 0)
                    res_in[n % 2].wait(dve, n // 2, 2)
                    F.dve_ready(dve, n)
                    for t in range(NT):
                        G.done.wait(dve, n, t + 1)
                        dve.tensor_tensor(F.dst(n, t), c.bank[t][:, :], res[n % 2][:, t, :], ALU.add).then_inc(rows_out.sem, 1)
                    moved.wait(dve, n, 1)
                    dve.tensor_tensor(tmp[:], tmp[:], res[n % 2][0:NEW, SM, :], ALU.add).then_inc(summed.sem, 1)
                    summed.wait(dve, n, 1)
                    dve.tensor_tensor(F.dst(n, SM), c.bank[SM][0:NEW, :], tmp[:], ALU.add).then_inc(rows_out.sem, 1)
                F.dve_tail(dve)

            @block.tensor
            def _(pe):
                for n in range(N):
                    for u in left[n]:
                        for t in range(TT):
                            if n == 0:
                                self.multiply(pe, u, t)
                                continue
                            if t == 0:
                                G.w_lo.wait(pe, n, u + 1)
                            if u == 0:
                                rows_out.wait(pe, n - 1, t + 1)
                            G.multiply(pe, n, u, t)
                F.pe_tail(pe)


class FinishC:

    def __init__(self, c, K, tag, place, rows_out):
        self.c, self.K, self.rows_out = c, K, rows_out
        self.x1 = c.at("x1", [P, TT, D_MODEL], F32, c.Y)
        self.sq = place("c_squares", [P, TT, 512])
        self.ss4, self.ss2, self.ss = place("c_ss4", [P, TT, 4]), place("c_ss2", [P, TT, 2]), place("c_ss", [P, TT])
        self.half = place("c_half", [P, TT])
        self.T = Transposer(c, "c", self.x1, K.act, K.ident, KT)
        self.squared = c.sem("c_squared", TT)
        self.stored = c.sem("c_stored", 2, 16)
        self.init, self.total = c.sem("c_init"), c.sem("c_total")

    def dst(self, n, t):
        return self.x1[0:rows(t), t, n * 512:(n + 1) * 512]

    def sp_step(self, sp, n):
        self.rows_out.wait(sp, n, TT)
        for q, t in ((P, slice(0, NT)), (NEW, slice(SM, TT))):
            sp.dma_start(self.c.dram["x1"][0:q, t, n * 512:(n + 1) * 512],
                         self.x1[0:q, t, n * 512:(n + 1) * 512]).then_inc(self.stored.sem, 16)

    def sp_tail(self, sp):
        sp.wait_ge(self.stored.sem, 8 * 16)

    def pool(self, pool):
        K = self.K
        pool.memset(self.ss4[:], 1.0).then_inc(self.init.sem, 1)
        pool.memset(self.half[:], -0.5).then_inc(self.init.sem, 1)
        pool.wait_ge(self.init.sem, 2)
        pool.wait_ge(self.squared.sem, 4 * TT)
        pool.tensor_tensor(self.ss2[:], self.ss4[:, :, 0:2], self.ss4[:, :, 2:4], ALU.add).then_inc(self.total.sem, 1)
        pool.wait_ge(self.total.sem, 1)
        pool.tensor_tensor(self.ss[:], self.ss2[:, :, 0], self.ss2[:, :, 1], ALU.add).then_inc(self.total.sem, 1)
        pool.wait_ge(self.total.sem, 2)
        pool.tensor_scalar(self.ss[:], self.ss[:], 1.0 / D_MODEL, EPS, ALU.mult, ALU.add).then_inc(self.total.sem, 1)
        pool.wait_ge(self.total.sem, 3)
        pool.tensor_tensor(K.rstd1[:], self.ss[:], self.half[:], ALU.pow).then_inc(self.total.sem, 1)
        pool.wait_ge(self.total.sem, 4)
        pool.tensor_scalar(K.half_rstd1[:], K.rstd1[:], 0.5, None, ALU.mult)

    def act_step(self, act_, n):
        if n == 0:
            act_.wait_ge(self.init.sem, 2)
        for t in range(TT):
            self.rows_out.wait(act_, n, t + 1)
            if n:
                self.squared.wait(act_, n - 1, t + 1)
            act_.activation(self.sq[0:rows(t), t, :], self.x1[0:rows(t), t, n * 512:(n + 1) * 512], ACT.Square,
                            accum_out=self.ss4[0:rows(t), t, n:n + 1]).then_inc(self.squared.sem, 1)

    def act_tail(self, act_):
        self.T.act(act_)

    def dve_ready(self, dve, n):
        pass

    def dve_tail(self, dve):
        self.T.dve(dve)

    def pe_tail(self, pe):
        pe.wait_ge(self.rows_out.sem, 4 * TT)
        self.T.pe(pe)


class FinishG:

    def __init__(self, c, K, tag, place, rows_out):
        self.c, self.rows_out = c, rows_out
        self.y = [place(f"y{i}", [P, TT, 512]) for i in range(2)]
        self.stored = c.sem("g_stored", 2, 16)

    def dst(self, n, t):
        return self.y[n % 2][0:rows(t), t, :]

    def sp_step(self, sp, n):
        self.rows_out.wait(sp, n, TT)
        for q, t in ((P, slice(0, NT)), (NEW, slice(SM, TT))):
            sp.dma_start(self.c.dram["out_y"][0:q, t, n * 512:(n + 1) * 512], self.y[n % 2][0:q, t, :]).then_inc(self.stored.sem, 16)

    def sp_tail(self, sp):
        sp.wait_ge(self.stored.sem, 8 * 16)

    def dve_ready(self, dve, n):
        if n >= 2:
            self.stored.wait(dve, n - 2, 2)

    def pool(self, pool):
        pass

    act_step = lambda self, eng, n: None
    act_tail = dve_tail = pe_tail = lambda self, eng: None


class Shared:

    def __init__(self, c):
        y = c.packer(c.Y)
        self.c = (y("c_hi", [P, LT, SEQ], F32R), y("c_lo", [P, LT, SEQ], F32R), y("c_smp", [P, LT, 2 * NEW], F32R))
        self.pc = (y("pc_hi", [P, LT, PAST], F32R), y("pc_lo", [P, LT, PAST], F32R))
        self.g_ckv = y("g_ckv", [P, LAT])
        self.cos, self.sin = y("cos", [P, 2, TT, ROPE // 2]), y("sin", [P, 2, TT, ROPE // 2])
        w = c.packer(max(c.W, y.cur[0]))
        self.gkr = w("g_kr", [P, ROPE])
        self.gqr, self.gkn, self.gqn = w("g_qr", [P, ROPE]), w("g_kn", [P, HD]), w("g_qn", [P, HD])
        self.kr = (w("kr_hi", [ROPE, TIME], F32R), w("kr_lo", [ROPE, TIME], F32R))
        self.f_base = w.cur[0]
        self.ql = (w("ql_hi", [P, LT, SEQ], F32R), w("ql_lo", [P, LT, SEQ], F32R), w("ql_smp", [P, LT, 2 * NEW], F32R))
        self.base = w.cur[0]


def rotate(eng, dst, x, cos, sin, tmp, wait_tmp, sig):
    H = ROPE // 2
    x1, x2 = x[..., 0:H], x[..., H:ROPE]
    for i, (a, b) in enumerate(((x1, cos), (x2, sin), (x2, cos), (x1, sin))):
        op = eng.tensor_tensor(tmp[i], a, b, ALU.mult)
    op.then_inc(sig.sem, 1)
    wait_tmp(eng)
    eng.tensor_tensor(dst[..., 0:H], tmp[0], tmp[1], ALU.subtract)
    return eng.tensor_tensor(dst[..., H:ROPE], tmp[2], tmp[3], ALU.add)


def block_d(c, K, S):
    nc, d = c.nc, c.dram
    place = c.packer(S.base)
    Gd = Gemm(c, "d", d["w_dkv"], 2, KT // UK, UK, 288, 2, K.act, K.g_kv, place)
    Gm = Gemm(c, "m", d["w_mla"], 5, KT // UK, UK, 512, 2, K.act, K.g_mla, place)
    U = KT // UK
    raw = place("d_raw", [P, TT, LAT + ROPE])
    sq = c.at("d_sq", [P, TT, LAT + ROPE], F32, S.base)
    ss, rstd, half = place("d_ss", [P, 2 * TT]), place("d_rstd", [P, 2 * TT]), place("d_half", [P, 2 * TT])
    kr = place("d_kr", [P, TT, ROPE])
    rt = place("d_rt", [P, 4, TT, ROPE // 2])
    lat_lo = place("d_lo", [NEW, 512])
    pkr = place("d_pkr", [ROPE, PAST])
    gate_at = place.cur[0]
    gate = place("d_gate", [P, TT, 512])
    assert place.cur[0] <= K.base, (place.cur[0], K.base)
    pc = c.at("d_pc", [P, LT, PAST], F32, gate_at)
    Tc = Transposer(c, "tc", raw, S.c, K.ident, LT, banks=(5, 6), smp_banks=(7,))
    Tq = Transposer(c, "tq", raw, S.ql, K.ident, LT, banks=(5, 6), smp_banks=(7,))
    s = c.sem
    init, loads = s("d_init"), s("d_loads", unit=16)
    took, took_lo, took_smp = s("d_took", NT), s("d_took_lo"), s("d_took_smp")
    added = s("d_added")
    sqd, sums, var, rst = s("d_sqd"), s("d_sums"), s("d_var", 2), s("d_rst")
    normed, scaled_kr, prods, kr_done = s("d_normed"), s("d_scaled_kr"), s("d_prods"), s("d_kr_done")
    out = s("d_out", unit=16)
    past_hi, past_lo = s("d_past_hi"), s("d_past_lo")
    kr_t, kr_hi, kr_lo = s("d_kr_t"), s("d_kr_hi"), s("d_kr_lo")
    th, gated = s("d_tanh", TT), s("d_gated", TT)
    g_lo, g_sum = s("d_g_lo"), s("d_g_sum")
    g_out = s("d_g_out", 2, 16)
    order = [(Gd, 0), (Gd, 1)] + [(Gm, n) for n in range(5)]
    flat = [(i, G, n, u) for i, (G, n) in enumerate(order) for u in range(U)]
    n_loads = 9

    def store_gate(sp, g):
        gated.wait(sp, g, TT)
        for q, t in ((P, slice(0, NT)), (NEW, slice(SM, TT))):
            sp.dma_start(d["gates"][0:q, t, g * 512:(g + 1) * 512], gate[0:q, t, :]).then_inc(g_out.sem, 16)

    with nc.Block() as block:
        @block.sync
        def _(sp):
            for u in range(2):
                Gd.load(sp, 0, u)
            for dst, name in ((S.g_ckv, "g_ckv"), (S.gkr, "g_kr"), (S.gqr, "g_qr"), (S.gkn, "g_kn"), (S.gqn, "g_qn"),
                              (S.cos, "cos"), (S.sin, "sin"), (pc, "cache_ckv"), (pkr, "cache_kr")):
                sp.dma_start(dst[:], d[name]).then_inc(loads.sem, 16)
            for u in range(2):
                Gm.load(sp, 0, u)
            for i, G, n, u in flat:
                m = n * U + u + 2
                if m < G.steps * U:
                    G.load(sp, m // U, m % U)
                if i == 2 and u == 4:
                    sp.wait_ge(normed.sem, 1)
                    sp.dma_start(d["out_ckv"][:, 0:NT, :], raw[:, 0:NT, 0:LAT]).then_inc(out.sem, 16)
                    sp.dma_start(d["out_ckv"][0:NEW, SM, :], raw[0:NEW, SM, 0:LAT]).then_inc(out.sem, 16)
                    sp.wait_ge(kr_done.sem, 1)
                    sp.dma_start(d["out_kr"][:, 0:NT, :], kr[:, 0:NT, :]).then_inc(out.sem, 16)
                    sp.dma_start(d["out_kr"][0:NEW, SM, :], kr[0:NEW, SM, :]).then_inc(out.sem, 16)
                if i >= 4 and u == 2:
                    store_gate(sp, i - 4)
            store_gate(sp, 3)
            sp.wait_ge(out.sem, 64)

        @block.gpsimd
        def _(pool):
            pool.memset(raw[:, SM, :], 0.0).then_inc(init.sem, 1)
            pool.memset(half[:], -0.5).then_inc(init.sem, 1)
            pool.wait_ge(init.sem, 2)
            for g in range(2):
                sums.wait(pool, g, 1)
                if g:
                    rst.wait(pool, 0, 1)
                pool.tensor_scalar(ss[:, 0:TT], ss[:, 0:TT], 1.0 / LAT, EPS, ALU.mult, ALU.add).then_inc(var.sem, 1)
                pool.tensor_scalar(ss[:, TT:], ss[:, TT:], 1.0 / ROPE, EPS, ALU.mult, ALU.add).then_inc(var.sem, 1)
                var.wait(pool, g, 2)
                pool.tensor_tensor(rstd[:], ss[:], half[:], ALU.pow).then_inc(rst.sem, 1)

        @block.scalar
        def _(act_):
            act_.wait_ge(init.sem, 2)
            Gd.make_hi(act_, 0, 0)
            for i, G, n, u in flat:
                if (i, u) != (0, 0) and u:
                    G.make_hi(act_, n, u)
                if i in (2, 3) and u == 1:
                    g = i - 2
                    took.wait(act_, i - 1, NT)
                    took_smp.wait(act_, i - 1, 1)
                    w = LAT + ROPE if g == 0 else LAT
                    act_.activation(sq[:, :, 0:w], raw[:, :, 0:w], ACT.Square).then_inc(sqd.sem, 1)
                if i == 2 and u == 3:
                    act_.wait_ge(loads.sem, 16 * n_loads)
                    act_.activation(S.pc[0][:], pc[:], ACT.Copy)
                    act_.activation(S.kr[0][:, SEQ:SEQ + PAST], pkr[:], ACT.Copy).then_inc(past_hi.sem, 1)
                if i == 2 and u == 6:
                    Tc.act(act_)
                    act_.wait_ge(kr_t.sem, 2)
                    act_.activation(S.kr[0][:, 0:SEQ], c.bank[5][0:ROPE, 0:SEQ], ACT.Copy)
                    act_.activation(S.kr[0][:, SEQ + PAST:], c.bank[6][0:ROPE, 0:NEW], ACT.Copy).then_inc(kr_hi.sem, 1)
                if i == 3 and u == 6:
                    Tq.act(act_)
                if u == U - 1:
                    if i + 1 < len(order):
                        order[i + 1][0].make_hi(act_, order[i + 1][1], 0)
                    if i <= 2:
                        a, w = (i * 288, 288) if i < 2 else (0, LAT)
                        if i == 2:
                            act_.wait_ge(out.sem, 64)
                            act_.wait_ge(kr_lo.sem, 1)
                        for t in range(NT):
                            G.done.wait(act_, n, t + 1)
                            act_.activation(raw[:, t, a:a + w], c.bank[t][:, 0:w], ACT.Copy,
                                            scale=K.rstd1[:, t:t + 1]).then_inc(took.sem, 1)
                        G.used.wait(act_, n, U)
                        act_.activation(raw[0:NEW, SM, a:a + w], c.bank[SM][NEW:2 * NEW, 0:w], ACT.Copy).then_inc(took_lo.sem, 1)
                    else:
                        g = i - 3
                        if g:
                            g_out.wait(act_, g - 1, 2)
                        else:
                            act_.wait_ge(past_lo.sem, 1)
                        for t in range(NT):
                            G.done.wait(act_, n, t + 1)
                            act_.activation(gate[:, t, :], c.bank[t][:, :], ACT.Tanh,
                                            scale=K.half_rstd1[:, t:t + 1]).then_inc(th.sem, 1)
                        G.used.wait(act_, n, U)
                        if g:
                            gated.wait(act_, g - 1, TT)
                        act_.activation(lat_lo[:], c.bank[SM][NEW:2 * NEW, :], ACT.Copy).then_inc(g_lo.sem, 1)
                        g_sum.wait(act_, g, 1)
                        act_.activation(gate[0:NEW, SM, :], lat_lo[:], ACT.Tanh,
                                        scale=K.half_rstd1[0:NEW, SM:TT]).then_inc(th.sem, 1)

        @block.vector
        def _(dve):
            dve.wait_ge(init.sem, 2)
            Gd.make_lo(dve, 0, 0)
            for i, G, n, u in flat:
                if (i, u) != (0, 0) and u:
                    G.make_lo(dve, n, u)
                if i in (2, 3) and u == 2:
                    g = i - 2
                    sqd.wait(dve, g, 1)
                    if g == 0:
                        dve.tensor_reduce(ss[:, TT:], sq[:, :, LAT:], AX.X, ALU.add)
                    dve.tensor_reduce(ss[:, 0:TT], sq[:, :, 0:LAT], AX.X, ALU.add).then_inc(sums.sem, 1)
                    rst.wait(dve, g, 1)
                    dve.wait_ge(loads.sem, 16 * n_loads)
                    for t in range(TT):
                        x = raw[:, t, 0:LAT]
                        if g == 0:
                            op = dve.scalar_tensor_tensor(x, x, rstd[:, t:t + 1], S.g_ckv[:], ALU.mult, ALU.mult)
                        else:
                            op = dve.tensor_scalar(x, x, rstd[:, t:t + 1], None, ALU.mult)
                    op.then_inc(normed.sem, 1)
                if i == 2 and u == 3:
                    for t in range(TT):
                        x = raw[:, t, LAT:]
                        op = dve.scalar_tensor_tensor(x, x, rstd[:, TT + t:TT + t + 1], S.gkr[:], ALU.mult, ALU.mult)
                    op.then_inc(scaled_kr.sem, 1)
                    dve.wait_ge(scaled_kr.sem, 1)
                    rotate(dve, kr[:, :, :], raw[:, :, LAT:], S.cos[:, 0, :, :], S.sin[:, 0, :, :],
                           [rt[:, q, :, :] for q in range(4)], lambda e: e.wait_ge(prods.sem, 1), prods).then_inc(kr_done.sem, 1)
                if i == 2 and u == 4:
                    dve.wait_ge(past_hi.sem, 1)
                    dve.tensor_tensor(S.pc[1][:], pc[:], S.pc[0][:].bitcast(F32), ALU.subtract)
                    dve.tensor_tensor(S.kr[1][:, SEQ:SEQ + PAST], pkr[:], S.kr[0][:, SEQ:SEQ + PAST].bitcast(F32),
                                      ALU.subtract).then_inc(past_lo.sem, 1)
                if i == 2 and u == 6:
                    Tc.dve(dve)
                    dve.wait_ge(kr_hi.sem, 1)
                    dve.tensor_tensor(S.kr[1][:, 0:SEQ], c.bank[5][0:ROPE, 0:SEQ], S.kr[0][:, 0:SEQ].bitcast(F32), ALU.subtract)
                    dve.tensor_tensor(S.kr[1][:, SEQ + PAST:], c.bank[6][0:ROPE, 0:NEW], S.kr[0][:, SEQ + PAST:].bitcast(F32),
                                      ALU.subtract).then_inc(kr_lo.sem, 1)
                if i == 3 and u == 6:
                    Tq.dve(dve)
                if u == U - 1:
                    if i + 1 < len(order):
                        order[i + 1][0].make_lo(dve, order[i + 1][1], 0)
                    if i <= 2:
                        a, w = (i * 288, 288) if i < 2 else (0, LAT)
                        took_lo.wait(dve, i, 1)
                        x = raw[0:NEW, SM, a:a + w]
                        dve.tensor_tensor(x, c.bank[SM][0:NEW, 0:w], x, ALU.add).then_inc(added.sem, 1)
                        added.wait(dve, i, 1)
                        dve.tensor_scalar(x, x, K.rstd1[0:NEW, SM:TT], None, ALU.mult).then_inc(took_smp.sem, 1)
                    else:
                        g = i - 3
                        for t in range(NT):
                            th.wait(dve, g, t + 1)
                            y = gate[:, t, :]
                            dve.scalar_tensor_tensor(y, y, 1.0, c.bank[t][:, :], ALU.add,
                                                     ALU.mult).then_inc(gated.sem, 1)
                        g_lo.wait(dve, g, 1)
                        dve.tensor_tensor(lat_lo[:], c.bank[SM][0:NEW, :], lat_lo[:], ALU.add).then_inc(g_sum.sem, 1)
                        th.wait(dve, g, TT)
                        y = gate[0:NEW, SM, :]
                        dve.scalar_tensor_tensor(y, y, 1.0, lat_lo[:], ALU.add,
                                                 ALU.mult).then_inc(gated.sem, 1)

        @block.tensor
        def _(pe):
            for i, G, n, u in flat:
                G.w_lo.wait(pe, n, u + 1)
                for t in range(TT):
                    if u == 0 and i:
                        if i <= 3:
                            took.wait(pe, i - 1, t + 1) if t < SM else took_smp.wait(pe, i - 1, 1)
                        else:
                            gated.wait(pe, i - 4, t + 1)
                    G.multiply(pe, n, u, t)
                if i == 2 and u == 5:
                    pe.wait_ge(normed.sem, 1)
                    Tc.pe(pe)
                    pe.wait_ge(Tc.lo_out.sem, len(Tc.jobs()))
                    pe.wait_ge(kr_done.sem, 1)
                    for t in range(NT):
                        op = pe.transpose(c.bank[5][0:ROPE, t * P:(t + 1) * P], kr[:, t, :], K.ident[:, :])
                    op.then_inc(kr_t.sem, 1)
                    pe.transpose(c.bank[6][0:ROPE, 0:NEW], kr[0:NEW, SM, :], K.ident[0:NEW, 0:NEW]).then_inc(kr_t.sem, 1)
                if i == 3 and u == 5:
                    pe.wait_ge(normed.sem, 2)
                    pe.wait_ge(kr_lo.sem, 1)
                    Tq.pe(pe)
    return g_out


class Tail:
    pass


def block_e(c, K, S, gates_stored):
    nc, d = c.nc, c.dram
    place = c.packer(c.X)
    W2 = 2 * BR
    N = HEADS // 2
    odd = place("e_raw1", [P, 2, TT, BR])
    sq, q = (place(f"e_{n}", [P, 2, TT, BR]) for n in ("sq", "q"))
    rt = place("e_rt", [P, 4, 2, TT, ROPE // 2])
    tab = place("e_tab", [P, 4, 2, TT, ROPE // 2])
    M = 2 * TT
    ss, rstd, half = place("e_ss", [P, 2 * M]), place("e_rstd", [P, 2 * M]), place("e_half", [P, 2 * M])
    assert place.cur[0] <= c.X + 36864
    raws = [place("e_raw0", [P, 2, TT, BR]), odd]
    G = Gemm(c, "e", d["w_uq"], N, 2, 2, W2, 2, S.ql, K.g_qa, place)
    assert place.cur[0] <= c.Y
    s = c.sem
    init, took, took_lo, took_smp = s("e_init"), s("e_took", NT), s("e_took_lo"), s("e_took_smp")
    sqd, sums, var, rst = s("e_sqd"), s("e_sums"), s("e_var", 2), s("e_rst")
    sc, prods, done = s("e_scaled", 2), s("e_prods"), s("e_turned", credit=1)
    out = s("e_out", 2, 16, credit=1)
    U = 2
    H2 = ROPE // 2
    wide = lambda x, n: x.rearrange("p (m o) -> p m o", o=1).broadcast_to([P, M, n])
    flat = lambda y: y.rearrange("p h t d -> p (h t) d")
    N_INIT = 10

    def run(eng, body):
        body(0, 0, True, False)
        body(1, 1, False, False)
        with eng.Fori(1, N // 2 - 1) as i:
            body(2 * i, 0, False, False)
            body(2 * i + 1, 1, False, False)
        body(N - 2, 0, False, False)
        body(N - 1, 1, False, True)

    tail = Tail()

    with nc.Block() as block:
        @block.sync
        def _(sp):
            def store(sp, g):
                sc.wait(sp, g, 2)
                done.wait(sp, g, 1)
                for j in range(2):
                    sp.dma_start(d["queries"][2 * g + j], q[:, j, :, :]).then_inc(out.sem, 16)

            def body(h, par, first, last):
                for u in range(U):
                    if not last:
                        G.load(sp, h + 1, u)
                if not isinstance(h, int) or h >= 2:
                    store(sp, h - 2)

            def finish(sp, g):
                store(sp, g)
                out.wait(sp, g, 2)
            tail.sp = finish
            for u in range(U):
                G.load(sp, 0, u)
            run(sp, body)
            gates_stored.wait(sp, 3, 2)

        @block.gpsimd
        def _(pool):
            done.grant(pool)
            c.clear_old(pool, keep=gates_stored)
            for raw in raws:
                pool.memset(raw[:, :, SM, :], 0.0).then_inc(init.sem, 1)
            pool.memset(half[:], -0.5).then_inc(init.sem, 1)
            pool.tensor_scalar(S.gqr[:], S.gqr[:], MLA_SCALE, None, ALU.mult).then_inc(init.sem, 1)
            pool.tensor_scalar(S.gkn[:], S.gkn[:], MLA_SCALE, None, ALU.mult).then_inc(init.sem, 1)
            pool.wait_ge(init.sem, 5)
            pool.tensor_tensor(S.gkn[:], S.gkn[:], S.gqn[:], ALU.mult).then_inc(init.sem, 1)
            for i, (t, a) in enumerate(((S.cos, 0), (S.sin, H2), (S.cos, H2), (S.sin, 0))):
                gain = S.gqr[:, a:a + H2].rearrange("p (o d) -> p o d", o=1).broadcast_to([P, M, H2])
                pool.tensor_tensor(flat(tab[:, i, :, :, :]), flat(t[:]), gain, ALU.mult).then_inc(init.sem, 1)
            pool.wait_ge(init.sem, N_INIT)

            def root(g):
                var.wait(pool, g, 2)
                pool.tensor_tensor(rstd[:], ss[:], half[:], ALU.pow).then_inc(rst.sem, 1)

            def rotate(g, par):
                sc.wait(pool, g, 2)
                out.wait(pool, g - 1, 2)
                x = flat(raws[par][:])[:, :, HD:]
                for i, a in enumerate((0, H2, H2, 0)):
                    op = pool.tensor_tensor(flat(rt[:, i, :, :, :]), x[:, :, a:a + H2], flat(tab[:, i, :, :, :]), ALU.mult)
                op.then_inc(prods.sem, 1)
                prods.wait(pool, g, 1)
                o, r4 = flat(q[:])[:, :, HD:], [flat(rt[:, i, :, :, :]) for i in range(4)]
                pool.tensor_tensor(o[:, :, 0:H2], r4[0], r4[1], ALU.subtract)
                pool.tensor_tensor(o[:, :, H2:], r4[2], r4[3], ALU.add).then_inc(done.sem, 1)

            def body(g, par, first, last):
                if not last:
                    root(g)
                    if not (isinstance(g, int) and g == N - 2):
                        rotate(g, par)

            def finish(pool):
                rotate(N - 2, 0)
                root(N - 1)
                rotate(N - 1, 1)
            run(pool, body)
            tail.pool = finish

        @block.scalar
        def _(act_):
            def squares(g, par):
                took_smp.wait(act_, g, 1)
                took.wait(act_, g, NT)
                act_.activation(sq[:], raws[par][:], ACT.Square).then_inc(sqd.sem, 1)

            def body(h, par, first, last):
                raw = raws[par]
                G.make_hi(act_, h, 1)
                if not first:
                    squares(h - 1, 1 - par)
                if not last:
                    G.make_hi(act_, h + 1, 0)
                if first:
                    act_.wait_ge(init.sem, N_INIT)
                else:
                    done.wait(act_, h - 2, 1)
                for t in range(NT):
                    G.done.wait(act_, h, t + 1)
                    act_.activation(raw[:, :, t, :], c.bank[t][:, 0:W2].rearrange("p (h d) -> p h d", h=2),
                                    ACT.Copy).then_inc(took.sem, 1)
                G.used.wait(act_, h, U)
                act_.activation(raw[0:NEW, :, SM, :], c.bank[SM][NEW:2 * NEW, 0:W2].rearrange("p (h d) -> p h d", h=2),
                                ACT.Copy).then_inc(took_lo.sem, 1)
            G.make_hi(act_, 0, 0)
            run(act_, body)

            tail.act = lambda act_: squares(N - 1, 1)

        @block.vector
        def _(dve):
            out.grant(dve)

            def sum_up(g):
                sqd.wait(dve, g, 1)
                v = flat(sq[:])
                dve.tensor_reduce(ss[:, 0:M], v[:, :, 0:HD], AX.X, ALU.add)
                dve.tensor_reduce(ss[:, M:], v[:, :, HD:], AX.X, ALU.add).then_inc(sums.sem, 1)
                sums.wait(dve, g, 1)
                dve.tensor_scalar(ss[:, 0:M], ss[:, 0:M], 1.0 / HD, EPS, ALU.mult, ALU.add).then_inc(var.sem, 1)
                dve.tensor_scalar(ss[:, M:], ss[:, M:], 1.0 / ROPE, EPS, ALU.mult, ALU.add).then_inc(var.sem, 1)

            def scale(g, par):
                rst.wait(dve, g, 1)
                v = flat(raws[par][:])
                x = v[:, :, HD:]
                dve.tensor_tensor(x, x, wide(rstd[:, M:], ROPE), ALU.mult).then_inc(sc.sem, 1)

            def scale_q(g, par):
                v = flat(raws[par][:])
                out.wait(dve, g - 1, 2)
                dve.tensor_tensor(flat(q[:])[:, :, 0:HD], v[:, :, 0:HD], wide(rstd[:, 0:M], HD), ALU.mult).then_inc(sc.sem, 1)

            def take(h, par):
                took_lo.wait(dve, h, 1)
                x = raws[par][0:NEW, :, SM, :]
                dve.tensor_tensor(x, c.bank[SM][0:NEW, 0:W2].rearrange("p (h d) -> p h d", h=2), x, ALU.add).then_inc(took_smp.sem, 1)

            def body(h, par, first, last):
                G.make_lo(dve, h, 1)
                if first:
                    dve.wait_ge(init.sem, N_INIT)
                else:
                    sum_up(h - 1)
                if not last:
                    G.make_lo(dve, h + 1, 0)
                if not first:
                    scale(h - 1, 1 - par)
                take(h, par)
                if not first:
                    scale_q(h - 1, 1 - par)
            G.make_lo(dve, 0, 0)
            run(dve, body)

            def finish(dve):
                sum_up(N - 1)
                scale(N - 1, 1)
                scale_q(N - 1, 1)
            tail.dve = finish

        @block.tensor
        def _(pe):
            def body(h, par, first, last):
                for u in range(U):
                    G.w_lo.wait(pe, h, u + 1)
                    for t in range(TT):
                        if u == 0 and not first:
                            took.wait(pe, h - 1, t + 1) if t < SM else took_smp.wait(pe, h - 1, 1)
                        G.multiply(pe, h, u, t)
            run(pe, body)
    return tail


class MlaHead:

    ORDER = ["qn", "kp", "qr", "T0", "T1", "s3", "ka", "T2", "s2", "new", "T3", "s1", "s0", "T8", "sa", "sb", "T4",
             "p3", "T5", "p2", "p1", "p0", "T6", "pn", "g", "gn", "T7", "on", "o"]
    JOBS = [n for n in ORDER if n[0] != "T"]
    SPLITS = ["qn", "kp", "qr", "ka", "new", "p3", "p2", "p1", "p0", "pn"]
    HALF = [slice(0, NT), slice(NT, 2 * NT + 1)]
    KV = 2 * NT + 1

    def __init__(self, c, K, S, wplace, xplace):
        self.c, self.K, self.S = c, K, S
        place = wplace
        self.G = Gemm(c, "f", c.dram["w_ukv"], HEADS, 1, LT, 2 * HD, 1, (None, None, None), None, place, slots=1)
        self.G.used = self.G.done
        self.vhi, self.vlo = place("f_vhi", [P, self.KV, HD], F32R), place("f_vlo", [P, self.KV, HD], F32R)
        self.k = place("f_k", [P, self.KV, HD])
        self.sq = place("f_sq", [P, self.KV, HD])
        self.kv_new = place("f_kv_new", [NEW, 2 * HD])
        self.ss, self.rstd, self.half = (place(f"f_{n}", [P, self.KV]) for n in ("ss", "rstd", "half"))
        self.q = place("f_q", [P, TT, BR])
        self.gate = place("f_gate", [P, TT, HD])
        self.qn = (place("f_qnhi", [HD, SEQ], F32R), place("f_qnlo", [HD, SEQ], F32R))
        self.qr = (place("f_qrhi", [ROPE, SEQ], F32R), place("f_qrlo", [ROPE, SEQ], F32R))
        self.nqn = (place("f_nqnhi", [HD, NEW], F32R), place("f_nqnlo", [HD, NEW], F32R))
        self.nqr = (place("f_nqrhi", [ROPE, NEW], F32R), place("f_nqrlo", [ROPE, NEW], F32R))
        place = xplace
        self.kp = (place("f_kphi", [HD, SEQ], F32R), place("f_kplo", [HD, SEQ], F32R))
        self.kn = (place("f_knhi", [HD, SAMP], F32R), place("f_knlo", [HD, SAMP], F32R))
        self.p = [place(f"f_p{i}", [P, (i + 1) * P]) for i in range(NT)]
        self.pn = place("f_pn", [NEW, SAMP])
        self.first = [0, P, 2 * P, 2 * P]
        self.pt = [(place(f"f_pt{j}hi", [P, SEQ - f], F32R), place(f"f_pt{j}lo", [P, SEQ - f], F32R))
                   for j, f in enumerate(self.first)]
        self.ptn = (place("f_ptnhi", [P, 512], F32R), place("f_ptnlo", [P, 512], F32R))
        self.gt = place("f_gt", [HD, SEQ + NEW])
        self.nm, self.rs, self.ri = place("f_nm", [P, TT]), place("f_rs", [P, TT]), place("f_ri", [P, TT])
        self.m2, self.r2 = place("f_m2", [NEW, 2]), place("f_r2", [NEW, 2])
        s = c.sem
        self.use = [sum(1 for i in range(len(self.JOBS)) if i % 3 == b) for b in range(3)]
        self.ready = [s(f"f_ready{b}", n) for b, n in enumerate(self.use)]
        self.free = [s(f"f_free{b}", n, credit=1) for b, n in enumerate(self.use)]
        self.kv_done = self.G.done
        self.new_done = s("f_new_done")
        self.squared = s("f_squared", 2)
        self.new_lo, self.new_sum = s("f_new_lo"), s("f_new_sum")
        self.sums, self.var, self.rst = s("f_sums", 2), s("f_var", 2), s("f_rst", 2)
        self.keys = s("f_keys", 2)
        self.v_hi = s("f_v_hi", TT)
        self.v_lo = s("f_v_lo", TT)
        self.hi_done = s("f_hi_done", len(self.SPLITS))
        self.new_max, self.negmax = s("f_new_max", 2), s("f_negmax", TT)
        self.inv, self.scaled = s("f_inv", 3), s("f_scaled")
        self.q_in, self.g_in = s("f_q_in", 1, 16), s("f_g_in", 2, 16)
        self.zero = s("f_zero")

    def job(self, name):
        i = self.JOBS.index(name)
        return i % 3, i // 3 + 1

    def bank(self, name):
        return self.c.bank[5 + self.job(name)[0]]

    def wait_ready(self, eng, g, name):
        b, k = self.job(name)
        self.ready[b].wait(eng, g, k)

    FROM = {**{f"s{i}": ("qn", "qr", "kp") for i in range(4)}, "sa": ("new", "ka"), "sb": ("new", "ka"),
            **{f"p{j}": (f"s{j}",) for j in range(4)}, "pn": ("sb",), "o": ("p0", "p1", "p2", "p3"), "on": ("pn",)}

    def wait_operands(self, eng, g, name):
        own, k = self.job(name)
        count = {own: k - 1}
        for b, k in map(self.job, self.FROM.get(name, ())):
            count[b] = max(count.get(b, k), k)
        for b, k in count.items():
            self.free[b].wait(eng, g, k)

    def wait_out_of(self, eng, g, name):
        b, k = self.job(name)
        self.free[b].wait(eng, g, k)

    def end(self, op, name):
        op.then_inc(self.ready[self.job(name)[0]].sem, 1)

    def release(self, op, name):
        op.then_inc(self.free[self.job(name)[0]].sem, 1)

    def split_views(self, name):
        b = self.bank(name)
        full = {"qn": (self.qn, HD), "qr": (self.qr, ROPE), "kp": (self.kp, HD)}
        if name in full:
            (hi, lo), n = full[name]
            return [(b[0:n, :], hi[:], lo[:])]
        if name == "ka":
            return [(b[:, :], self.kn[0][:, 0:PAST], self.kn[1][:, 0:PAST])]
        if name == "new":
            return [(b[:, 0:NEW], self.nqn[0][:], self.nqn[1][:]),
                    (b[:, NEW:2 * NEW], self.kn[0][:, PAST:], self.kn[1][:, PAST:]),
                    (b[0:ROPE, 2 * NEW:3 * NEW], self.nqr[0][:], self.nqr[1][:])]
        if name == "pn":
            hi, lo = self.ptn
            n = NT * NEW
            return [(b[:, 0:n], hi[:, 0:n], lo[:, 0:n]),
                    (b[0:NEW, n:n + NEW], hi[0:NEW, n:n + NEW], lo[0:NEW, n:n + NEW])]
        j = int(name[1])
        hi, lo = self.pt[j]
        a = j * P - self.first[j]
        return [(b[:, j * P:], hi[:, a:], lo[:, a:])]

    def pe_tile(self, eng, h, tau):
        S, G = self.S, self.G
        whi, wlo = G.whi[0], G.wlo[0]
        bank = self.c.bank[tau // 2]
        if tau == 0:
            G.w_lo.wait(eng, h, 1)
        if tau % 2 == 0:
            self.v_lo.wait(eng, h, tau // 2 + 1 - TT)
        out = bank[:, (tau % 2) * 256:(tau % 2) * 256 + 256]
        for k in range(LT):
            if tau < 2 * NT:
                hi, lo = (S.c[0], S.c[1]) if tau < NT else S.pc
                a = slice((tau % NT) * P, (tau % NT + 1) * P)
                pairs = three(hi[:, k, a], lo[:, k, a], whi[:, k, :], wlo[:, k, :])
            else:
                pairs = [(S.c[2][:, k, :], whi[:, k, :]), (S.c[2][:, k, :], wlo[:, k, :])]
            for i, (x, w) in enumerate(pairs):
                op = eng.matmul(out, x, w, start=(k == 0 and i == 0), stop=(k == LT - 1 and i == len(pairs) - 1))
        if tau == 2 * NT:
            op.then_inc(self.new_done.sem, 1)
        elif tau % 2:
            op.then_inc(self.kv_done.sem, 1)

    def pe_job(self, eng, g, name):
        K, S, b = self.K, self.S, self.bank(name)
        self.wait_operands(eng, g, name)
        if name == "kp":
            self.keys.wait(eng, g, 1)
        elif name == "ka":
            self.keys.wait(eng, g, 2)
        I = K.ident
        if name in ("qn", "qr"):
            if name == "qn":
                self.q_in.wait(eng, g, 1)
            n, a = (HD, 0) if name == "qn" else (ROPE, HD)
            for t in range(NT):
                op = turn(eng, b[0:n, t * P:(t + 1) * P], self.q[:, t, a:a + n], I[:, :], name == "qr" and t == 0)
        elif name == "new":
            turn(eng, b[:, 0:NEW], self.q[0:NEW, SM, 0:HD], I[0:NEW, 0:NEW], True)
            eng.transpose(b[:, NEW:2 * NEW], self.k[0:NEW, 2 * NT, :], I[0:NEW, 0:NEW])
            op = eng.transpose(b[0:ROPE, 2 * NEW:3 * NEW], self.q[0:NEW, SM, HD:BR], I[0:NEW, 0:NEW])
        elif name in ("kp", "ka"):
            t0 = 0 if name == "kp" else NT
            for t in range(NT):
                op = eng.transpose(b[:, t * P:(t + 1) * P], self.k[:, t0 + t, :], I[:, :])
        elif name in ("s0", "s1", "s2", "s3"):
            i = int(name[1])
            n = max(i + 1, 2) * P
            q = slice(i * P, (i + 1) * P)
            for m, (x, y) in enumerate(three(*self.qn, *self.kp)):
                eng.matmul(b[:, 0:n], x[:, q], y[:, 0:n], start=(m == 0), stop=False)
            eng.matmul(b[:, q], K.ident_b[:, :], K.mask_mla_b[:, :], start=False, stop=False, skip_group_check=True)
            for m, (x, y) in enumerate(three(*self.qr, *S.kr)):
                op = eng.matmul(b[:, 0:n], x[:, q], y[:, 0:n], start=False, stop=(m == 2))
        elif name in ("sa", "sb"):
            i = ("sa", "sb").index(name)
            for m, (x, y) in enumerate(three(*self.nqn, *self.kn)):
                eng.matmul(b[0:NEW, 0:288], x[:, :], y[:, i * 288:(i + 1) * 288], start=(m == 0), stop=False)
            for m, (x, y) in enumerate(three(*self.nqr, *S.kr)):
                op = eng.matmul(b[0:NEW, 0:288], x[:, :], y[:, SEQ + i * 288:SEQ + (i + 1) * 288], start=False, stop=(m == 2))
        elif name == "pn":
            for t in range(TT):
                n = rows(t)
                op = turn(eng, b[0:n, t * NEW:(t + 1) * NEW], self.pn[:, t * P:t * P + n], I[0:NEW, 0:NEW], t == 0)
        elif name[0] == "p":
            j = int(name[1])
            for i in range(j, NT):
                op = eng.transpose(b[:, i * P:(i + 1) * P], self.p[i][:, j * P:(j + 1) * P], I[:, :])
        elif name == "o":
            self.v_lo.wait(eng, g, TT)
            for j in range(NT):
                f = self.first[j]
                for m, (x, y) in enumerate(three(self.vhi, self.vlo, *self.pt[j])):
                    op = eng.matmul(b[:, f:], x[:, j, :], y[:, :], start=(j == 0 and m == 0), stop=(j == NT - 1 and m == 2))
        elif name == "on":
            for t in range(TT):
                n = rows(t)
                for m, (x, y) in enumerate(three(self.vhi, self.vlo, *self.ptn)):
                    op = eng.matmul(b[:, 0:256], x[0:n, NT + t, :], y[0:n, t * NEW:t * NEW + 256],
                                    start=(t == 0 and m == 0), stop=(t == SM and m == 2))
        elif name == "g":
            self.scaled.wait(eng, g, 1)
            for t in range(NT):
                op = eng.transpose(b[:, t * P:(t + 1) * P], self.gate[:, t, :], I[:, :])
        elif name == "gn":
            op = turn(eng, b[:, 0:NEW], self.gate[0:NEW, SM, :], I[0:NEW, 0:NEW], True)
        self.end(op, name)

    def act_job(self, eng, g, name):
        if name == "sa":
            return
        if name == "sb":
            self.act_exp(eng, g, "sa")
            self.act_exp(eng, g, "sb")
        elif name in self.SPLITS:
            self.wait_ready(eng, g, name)
            for src, hi, lo in self.split_views(name):
                op = eng.activation(hi, src, ACT.Copy)
            op.then_inc(self.hi_done.sem, 1)
        elif name[0] == "s":
            self.act_exp(eng, g, name)
        elif name in ("g", "gn"):
            self.wait_ready(eng, g, name)
            a, n = (0, SEQ) if name == "g" else (SEQ, NEW)
            self.release(eng.activation(self.gt[:, a:a + n], self.bank(name)[:, 0:n], ACT.Copy), name)

    def act_exp(self, eng, g, name):
        b = self.bank(name)
        if name in ("sa", "sb"):
            i = ("sa", "sb").index(name)
            self.negmax.wait(eng, g, TT)
            op = eng.activation(self.pn[:, i * 288:(i + 1) * 288], b[0:NEW, 0:288], ACT.Exp, bias=self.nm[0:NEW, SM:TT],
                                accum_out=self.r2[:, i:i + 1])
        else:
            i = int(name[1])
            self.negmax.wait(eng, g, NT - i)
            op = eng.activation(self.p[i][:], b[:, 0:(i + 1) * P], ACT.Exp, bias=self.nm[:, i:i + 1],
                                accum_out=self.rs[:, i:i + 1])
        self.release(op, name)

    def act_keys(self, eng, h, b):
        self.kv_done.wait(eng, h, b + 1)
        src = self.c.bank[b][:, :].rearrange("p (t n) -> p t n", t=2)[:, :, 0:HD]
        op = eng.activation(self.sq[:, 2 * b:2 * b + 2, :], src, ACT.Square)
        if b % 2:
            op.then_inc(self.squared.sem, 1)

    def act_new_lo(self, eng, h):
        self.new_done.wait(eng, h, 1)
        eng.activation(self.kv_new[:], self.c.bank[SM][NEW:2 * NEW, 0:256], ACT.Copy).then_inc(self.new_lo.sem, 1)

    def act_new_keys(self, eng, h):
        self.new_sum.wait(eng, h, 1)
        eng.activation(self.sq[0:NEW, 2 * NT, :], self.kv_new[:, 0:HD], ACT.Square)

    def act_values(self, eng, h, b):
        if b < NT:
            src = self.c.bank[b][:, :].rearrange("p (t n) -> p t n", t=2)[:, :, HD:]
            op = eng.activation(self.vhi[:, 2 * b:2 * b + 2, :], src, ACT.Copy)
        else:
            op = eng.activation(self.vhi[0:NEW, 2 * NT, :], self.kv_new[:, HD:], ACT.Copy)
        op.then_inc(self.v_hi.sem, 1)

    def dve_job(self, eng, g, name, dst):
        b = self.bank(name)
        if name in self.SPLITS:
            self.hi_done.wait(eng, g, self.SPLITS.index(name) + 1)
            for src, hi, lo in self.split_views(name):
                op = eng.tensor_tensor(lo, src, hi.bitcast(F32), ALU.subtract)
            self.release(op, name)
        elif name in ("sa", "sb"):
            self.wait_ready(eng, g, name)
            i = ("sa", "sb").index(name)
            eng.tensor_reduce(self.m2[:, i:i + 1], b[0:NEW, 0:288], AX.X, ALU.max).then_inc(self.new_max.sem, 1)
            if i:
                self.new_max.wait(eng, g, 2)
                eng.tensor_reduce(self.nm[0:NEW, SM:TT], self.m2[:], AX.X, ALU.max, negate=True).then_inc(self.negmax.sem, 1)
        elif name[0] == "s":
            self.wait_ready(eng, g, name)
            i = int(name[1])
            eng.tensor_reduce(self.nm[:, i:i + 1], b[:, 0:(i + 1) * P], AX.X, ALU.max, negate=True).then_inc(self.negmax.sem, 1)
        elif name in ("o", "on"):
            self.wait_ready(eng, g, name)
            self.wait_out_of(eng, g, "g" if name == "o" else "gn")
            a, n = (0, SEQ) if name == "o" else (SEQ, NEW)
            op = eng.tensor_tensor(dst[:, g, a:a + n], b[:, 0:n], self.gt[:, a:a + n], ALU.mult)
            self.release(op, name)

    def dve_scale_gate(self, eng, g):
        self.wait_out_of(eng, g, "sb")
        eng.tensor_tensor(self.rs[0:NEW, SM:TT], self.r2[:, 0:1], self.r2[:, 1:2], ALU.add).then_inc(self.inv.sem, 1)
        self.inv.wait(eng, g, 1)
        eng.reciprocal(self.ri[:], self.rs[:]).then_inc(self.inv.sem, 1)
        self.inv.wait(eng, g, 2)
        eng.tensor_tensor(self.ri[:], self.ri[:], self.K.half_rstd1[:], ALU.mult).then_inc(self.inv.sem, 1)
        self.inv.wait(eng, g, 3)
        self.g_in.wait(eng, g, 2)
        for t in range(TT):
            y = self.gate[0:rows(t), t, :]
            op = eng.tensor_scalar(y, y, self.ri[0:rows(t), t:t + 1], None, ALU.mult)
        op.then_inc(self.scaled.sem, 1)

    def dve_new(self, eng, h):
        self.new_lo.wait(eng, h, 1)
        eng.tensor_tensor(self.kv_new[:], self.c.bank[SM][0:NEW, 0:256], self.kv_new[:], ALU.add).then_inc(self.new_sum.sem, 1)

    def dve_sums(self, eng, h, half):
        a, z = self.HALF[half].start, self.HALF[half].stop
        self.squared.wait(eng, h, half + 1)
        if half:
            eng.tensor_reduce(self.ss[:, a:2 * NT], self.sq[:, a:2 * NT, :], AX.X, ALU.add)
            eng.tensor_reduce(self.ss[0:NEW, 2 * NT:], self.sq[0:NEW, 2 * NT:, :], AX.X, ALU.add).then_inc(self.sums.sem, 1)
        else:
            eng.tensor_reduce(self.ss[:, a:z], self.sq[:, a:z, :], AX.X, ALU.add).then_inc(self.sums.sem, 1)
        self.sums.wait(eng, h, half + 1)
        eng.tensor_scalar(self.ss[:, a:z], self.ss[:, a:z], 1.0 / HD, EPS, ALU.mult, ALU.add).then_inc(self.var.sem, 1)

    def dve_keys(self, eng, h, half):
        self.rst.wait(eng, h, half + 1)
        for t in range(self.HALF[half].start, self.HALF[half].stop):
            n = P if t < 2 * NT else NEW
            src = self.c.bank[t // 2][:, (t % 2) * 256:(t % 2) * 256 + HD] if t < 2 * NT else self.kv_new[:, 0:HD]
            op = eng.scalar_tensor_tensor(self.k[0:n, t, :], src, self.rstd[0:n, t:t + 1], self.S.gkn[0:n, :], ALU.mult, ALU.mult)
        op.then_inc(self.keys.sem, 1)

    def dve_values(self, eng, h, b):
        self.v_hi.wait(eng, h, b + 1)
        if b < NT:
            src = self.c.bank[b][:, :].rearrange("p (t n) -> p t n", t=2)[:, :, HD:]
            hi, lo = self.vhi[:, 2 * b:2 * b + 2, :], self.vlo[:, 2 * b:2 * b + 2, :]
        else:
            src, hi, lo = self.kv_new[:, HD:], self.vhi[0:NEW, 2 * NT, :], self.vlo[0:NEW, 2 * NT, :]
        eng.tensor_tensor(lo, src, hi.bitcast(F32), ALU.subtract).then_inc(self.v_lo.sem, 1)


def block_f(c, K, S, tail):
    nc, d = c.nc, c.dram
    o_all = c.at("o_mla", [HD, HEADS, SEQ + NEW], F32, c.X)
    wplace, xplace = c.packer(S.f_base), c.packer(c.X + 36864)
    H = MlaHead(c, K, S, wplace, xplace)
    assert wplace.cur[0] <= K.base and xplace.cur[0] <= c.Y, (wplace.cur[0], K.base, xplace.cur[0], c.Y)
    G = H.G
    started = lambda g: not isinstance(g, int) or g > 0

    with nc.Block() as block:
        @block.sync
        def _(sp):
            def load_q(g):
                if started(g):
                    H.wait_ready(sp, g - 1, "new")
                sp.dma_start(H.q[:], d["queries"][g]).then_inc(H.q_in.sem, 16)

            def load_gate(g):
                if started(g):
                    H.wait_ready(sp, g - 1, "gn")
                cols = bass.ds(g * HD, HD) if not isinstance(g, int) else slice(g * HD, (g + 1) * HD)
                for q, t in ((P, slice(0, NT)), (NEW, slice(SM, TT))):
                    sp.dma_start(H.gate[0:q, t, :], d["gates"][0:q, t, cols]).then_inc(H.g_in.sem, 16)

            G.load(sp, 0, 0)
            G.load(sp, 1, 0)
            tail.sp(sp, HEADS // 2 - 2)
            load_q(0)
            tail.sp(sp, HEADS // 2 - 1)
            load_gate(0)
            with sp.Fori(1, HEADS - 1) as h:
                G.load(sp, h + 1, 0)
                load_q(h)
                load_gate(h)
            load_q(HEADS - 1)
            load_gate(HEADS - 1)

        @block.gpsimd
        def _(pool):
            pool.memset(H.ss[:], 1.0).then_inc(H.zero.sem, 1)
            pool.memset(H.rs[:], 1.0).then_inc(H.zero.sem, 1)
            pool.memset(H.half[:], -0.5).then_inc(H.zero.sem, 1)
            for x in (*H.ptn, *H.pt[NT - 1]):
                pool.memset(x[:].bitcast(F32), 0.0).then_inc(H.zero.sem, 1)
            pool.wait_ge(H.zero.sem, 7)
            tail.pool(pool)

            def body(h, last):
                for half, t in enumerate(H.HALF):
                    H.var.wait(pool, h, half + 1)
                    pool.tensor_tensor(H.rstd[:, t], H.ss[:, t], H.half[:, t], ALU.pow).then_inc(H.rst.sem, 1)
            steps(pool, HEADS, body)

        @block.scalar
        def _(act_):
            def body(h, last, g):
                for name in H.ORDER:
                    if name[0] != "T":
                        if g is not None:
                            H.act_job(act_, g, name)
                    elif h is not None:
                        if name in ("T1", "T3", "T5", "T7"):
                            H.act_keys(act_, h, int(name[1]) // 2)
                        elif name == "T8":
                            H.act_new_lo(act_, h)
                        elif name == "T4":
                            H.act_new_keys(act_, h)
                    if h is not None:
                        if name == "T7" and not last:
                            G.make_hi(act_, h + 1, 0)
                        if name == "o":
                            H.keys.wait(act_, h, 1)
                            if g is not None:
                                H.wait_ready(act_, g, name)
                            for b in (0, 1):
                                H.act_values(act_, h, b)
                    if g is not None and name == "qr":
                        H.keys.wait(act_, g, 2)
                        for b in (2, 3, 4):
                            H.act_values(act_, g, b)
            G.make_hi(act_, 0, 0)
            tail.act(act_)
            body(0, False, None)
            act_.wait_ge(H.zero.sem, 7)
            with act_.Fori(1, HEADS - 1) as h:
                body(h, False, h - 1)
            body(HEADS - 1, True, HEADS - 2)
            body(None, True, HEADS - 1)

        @block.vector
        def _(dve):
            for bank_free in H.free:
                bank_free.grant(dve)

            def body(h, last, g):
                for name in H.ORDER:
                    if name[0] != "T":
                        if g is not None:
                            H.dve_job(dve, g, name, o_all)
                            if name == "p3":
                                H.dve_scale_gate(dve, g)
                    elif name == "T8" and h is not None:
                        H.dve_new(dve, h)
                    if h is not None:
                        if name == "s0":
                            H.dve_sums(dve, h, 0)
                        if name == "sb":
                            H.dve_keys(dve, h, 0)
                        if name == "T7":
                            H.dve_sums(dve, h, 1)
                            if not last:
                                G.make_lo(dve, h + 1, 0)
                        if name == "o":
                            for b in (0, 1):
                                H.dve_values(dve, h, b)
                    if g is not None and name == "qr":
                        H.dve_keys(dve, g, 1)
                        for b in (2, 3, 4):
                            H.dve_values(dve, g, b)
            G.make_lo(dve, 0, 0)
            tail.dve(dve)
            dve.wait_ge(H.zero.sem, 7)
            body(0, False, None)
            with dve.Fori(1, HEADS - 1) as h:
                body(h, False, h - 1)
            body(HEADS - 1, True, HEADS - 2)
            body(None, True, HEADS - 1)

        @block.tensor
        def _(pe):
            def body(h, last, g):
                for name in H.ORDER:
                    if name[0] != "T":
                        if g is not None:
                            H.pe_job(pe, g, name)
                    elif h is not None:
                        H.pe_tile(pe, h, int(name[1]))
            body(0, False, None)
            pe.wait_ge(H.zero.sem, 7)
            with pe.Fori(1, HEADS - 1) as h:
                body(h, False, h - 1)
            body(HEADS - 1, True, HEADS - 2)
            body(None, True, HEADS - 1)
    return o_all


def block_g(c, K, o):
    place = c.packer(c.X + 36864)
    act = (place("g_ohi", [P, KT, SEQ], F32R), place("g_olo", [P, KT, SEQ], F32R), place("g_osmp", [P, KT, 2 * NEW], F32R))
    OutProj(c, K, "g", c.dram["w_out2"], o, act, c.dram["x1"], place.cur[0], FinishG, raw=4, lead=0).block()


def program(nc, dram):
    with ExitStack() as ctx:
        c = Core(nc, ctx, dram)
        K = Consts(c)
        block_a(c, K)
        proj = OutProj(c, K, "c", dram["w_out1"], K.o_fox, K.act, dram["x"], c.W, FinishC, raw=RAW_FOX, lead=KT // UK - 1)
        block_b(c, K, proj)
        proj.block()
        S = Shared(c)
        gates_stored = block_d(c, K, S)
        c.old, c.used = c.used, []
        tail = block_e(c, K, S, gates_stored)
        c.release_old(keep=gates_stored)
        block_g(c, K, block_f(c, K, S, tail))


BACC = {"dynamic_dma_scratch_size": 1024}


def unit_layout(w, cols, units, kk):
    k, n = w.shape
    return w.reshape(units, kk, P, n // cols, cols).transpose(3, 0, 2, 1, 4)


def lay_out(a):
    g = {n: np.asarray(v) for n, v in a.items()}
    out = {}
    rows_ = np.zeros((TT * P, D_MODEL), np.float32)
    rows_[:SEQ], rows_[SEQ:SEQ + NEW] = g["x_prompt"][0], g["x_sample"][0]
    out["x"] = rows_.reshape(TT, P, D_MODEL).transpose(1, 0, 2)
    w = g["fox_w_in"][0]
    blocks = w[:, :4 * D_MODEL].reshape(D_MODEL, 4, HEADS, HD).transpose(0, 2, 1, 3).reshape(D_MODEL, HEADS * 4 * HD)
    out["w_fox"] = unit_layout(blocks, 512, KT // UK, UK)
    out["w_f"] = w[:, 4 * D_MODEL:].reshape(KT, P, HEADS).transpose(1, 0, 2)
    out["g_fox"] = g["fox_norm_g"][0].reshape(KT, P).T
    out["g_kv"] = g["kv_norm_g"].reshape(KT, P).T
    out["g_mla"] = g["mla_norm_g"][0].reshape(KT, P).T
    out["g_qa"] = g["mla_qa_norm_g"][0].reshape(LT, P).T
    out["b_f"] = g["fox_b_f"][0].reshape(HEADS, 1)
    out["g_q"] = np.broadcast_to(g["fox_q_norm_g"][0], (P, HD))
    out["g_k"] = np.broadcast_to(g["fox_k_norm_g"][0], (P, HD))
    out["cache_logf"] = g["cache_fox_logf"][0, 0].T
    out["cache_k"] = g["cache_fox_k"][0, 0].transpose(1, 2, 0)
    out["cache_v"] = g["cache_fox_v"][0, 0].reshape(NT, P, HEADS, HD).transpose(2, 1, 0, 3)
    out["w_out1"] = unit_layout(g["fox_w_out"][0], 512, KT // UK, UK)
    out["w_dkv"] = unit_layout(g["mla_w_dkv"], 288, KT // UK, UK)
    out["w_mla"] = unit_layout(g["mla_w_in"][0], 512, KT // UK, UK)
    out["w_uq"] = unit_layout(g["mla_w_uq"][0].reshape(LAT, HEADS * BR), 2 * BR, LT // UK, UK)
    for n, k in (("g_ckv", "mla_ckv_norm_g"), ("g_kr", "mla_krope_norm_g"), ("g_kn", "mla_knope_norm_g")):
        out[n] = np.broadcast_to(g[k], (P, g[k].shape[-1]))
    for n, k in (("g_qr", "mla_qrope_norm_g"), ("g_qn", "mla_qnope_norm_g")):
        out[n] = np.broadcast_to(g[k][0], (P, g[k].shape[-1]))
    out["w_ukv"] = unit_layout(g["mla_w_ukv"].reshape(LAT, HEADS * 2 * HD), 2 * HD, 1, LT)
    out["w_out2"] = unit_layout(g["mla_w_out"][0], 512, KT // UK, UK)
    out["cache_ckv"] = g["cache_mla_ckv"][0].T.reshape(LT, P, PAST).transpose(1, 0, 2)
    out["cache_kr"] = g["cache_mla_krope"][0].T
    pos = np.arange(TT * P, dtype=np.float32)
    pos[SEQ:] += PAST - SEQ
    inv = np.float32(THETA) ** (-np.arange(ROPE // 2, dtype=np.float32) / np.float32(ROPE // 2))
    ang = (pos[:, None] * inv[None, :]).astype(np.float32).reshape(TT, P, ROPE // 2).transpose(1, 0, 2)
    out["cos"], out["sin"] = (np.broadcast_to(f(ang)[:, None], (P, 2, TT, ROPE // 2)) for f in (np.cos, np.sin))
    r = np.arange(P)
    out["ident"] = np.eye(P, dtype=np.float32)
    out["mask_fox"] = np.where(r[None, :] > r[:, None], MASKED, 0.0).astype(np.float32)
    out["mask_mla"] = np.where(r[None, :] // CHUNK > r[:, None] // CHUNK, MASKED, 0.0).astype(np.float32)
    heads = np.arange(HEADS)
    neg, pos = np.zeros((P, HEADS), np.float32), np.zeros((P, HEADS), np.float32)
    neg[heads, heads] = neg[32 + heads, heads] = -1.0
    pos = np.zeros((P, HEADS), np.float32)
    pos[64 + heads, heads] = pos[96 + heads, heads] = 1.0
    out["nsel"], out["psel"] = neg, pos
    return {n: np.ascontiguousarray(v) for n, v in out.items()}


OUTS = {
    "out_logf": [P, TT, HEADS],
    "out_fk": [HEADS, P, TT, HD],
    "out_fv": [HEADS, P, TT, HD],
    "out_ckv": [P, TT, LAT],
    "out_kr": [P, TT, ROPE],
    "out_y": [P, TT, D_MODEL],
}


SCRATCH = {
    "x1": [P, TT, D_MODEL],
    "gates": [P, TT, D_MODEL],
    "queries": [HEADS, P, TT, BR],
}


def tokens(x):
    flat = np.moveaxis(x, 0, 1).reshape((TT * P,) + x.shape[2:])
    return flat[:SEQ], flat[SEQ:SEQ + NEW]


def kernel(**inputs):
    from concourse import bacc
    from concourse.bass_utils import run_bass_kernel_spmd

    nc = bacc.Bacc("TRN2", target_bir_lowering=False, num_devices=1, **BACC)
    arrays = lay_out(inputs)
    dram = {n: nc.dram_tensor(n, list(v.shape), F32, kind="ExternalInput").ap() for n, v in arrays.items()}
    dram.update({n: nc.dram_tensor(n, s, F32, kind="ExternalOutput").ap() for n, s in OUTS.items()})
    dram.update({n: nc.dram_tensor(n, s, F32, kind="Internal").ap() for n, s in SCRATCH.items()})
    program(nc, dram)
    r = run_bass_kernel_spmd(nc, [arrays], core_ids=[0]).results[0]
    heads = lambda x: [h[None, None] for h in tokens(np.asarray(x).transpose(1, 2, 0, 3))]
    (y_p, y_s), (lf_p, lf_s), (c_p, c_s), (kr_p, kr_s) = (tokens(np.asarray(r[n])) for n in
                                                         ("out_y", "out_logf", "out_ckv", "out_kr"))
    (k_p, k_s), (v_p, v_s) = heads(r["out_fk"]), heads(r["out_fv"])
    return (y_p[None], y_s[None], k_p, v_p, lf_p[None, None], c_p[None], kr_p[None],
            k_s, v_s, lf_s[None, None], c_s[None], kr_s[None])
```
